# Optimizing a Trainium2 kernel written in Bass

```python
import math
import jax, jax.numpy as jnp
from jax import lax
import numpy as np

D_MODEL = 1024
BATCH = 1
SEQ = 512
DEPTH = 2

N_MIXERS = 2
N_NSA_LAYERS = (DEPTH + N_MIXERS - 1) // N_MIXERS
N_DIFF_LAYERS = DEPTH // N_MIXERS

REL_BUCKETS = 32
REL_MAX_DIST = 128
N_BIAS_MAPS = 16

NSA_HEADS = 16
NSA_GROUPS = 4
NSA_HPG = NSA_HEADS // NSA_GROUPS
NSA_HEAD_DIM = D_MODEL // NSA_HEADS
NSA_WIDTH = NSA_HEADS * NSA_HEAD_DIM
NSA_KV = NSA_GROUPS * NSA_HEAD_DIM
CMP_BLOCK = 32
CMP_STRIDE = 16
CMP_HIDDEN = 2 * NSA_HEAD_DIM
SEL_BLOCK = 64
SEL_TOPK = 8
WINDOW = 512
NSA_QBLOCK = 64
NSA_SPLIT_SIZES = [NSA_WIDTH] + [NSA_KV] * 6 + [3 * NSA_HEADS, NSA_WIDTH]
NSA_IN = sum(NSA_SPLIT_SIZES)

DIFF_HEADS = 8
DIFF_HALF = D_MODEL // (2 * DIFF_HEADS)
DIFF_VDIM = 2 * DIFF_HALF
DIFF_WIDTH = DIFF_HEADS * DIFF_VDIM
DIFF_IN = 4 * DIFF_WIDTH
DIFF_QBLOCK = 128

NEG = -1e30
BIG = 1e9
EPS = 1e-6


def rmsnorm(x, g):
    xf = x.astype(jnp.float32)
    y = xf * lax.rsqrt(jnp.mean(xf * xf, axis=-1, keepdims=True) + EPS)
    return (y * g.astype(jnp.float32)).astype(x.dtype)

def rel_bucket(dist):
    n = jnp.maximum(dist, 0)
    max_exact = REL_BUCKETS // 2
    nf = jnp.maximum(n, 1).astype(jnp.float32)
    large = max_exact + (jnp.log(nf / max_exact) / math.log(REL_MAX_DIST / max_exact)
                         * (REL_BUCKETS - max_exact)).astype(jnp.int32)
    large = jnp.minimum(large, REL_BUCKETS - 1)
    return jnp.where(n < max_exact, n, large)

def compress(kv, pe, w1, w2):
    b, s, g, dh = kv.shape
    nc = (s - CMP_BLOCK) // CMP_STRIDE + 1
    idx = jnp.arange(nc)[:, None] * CMP_STRIDE + jnp.arange(CMP_BLOCK)[None, :]
    blocks = kv[:, idx] + pe[None, None, :, None, :]
    flat = jnp.moveaxis(blocks, 3, 2).reshape(b, nc, g, CMP_BLOCK * dh)
    return jax.nn.silu(flat @ w1) @ w2

def nsa_mixer(u, table, w_in, pe_k, w1_k, w2_k, pe_v, w1_v, w2_v, w_out):
    b, s, _ = u.shape
    G, J, dh = NSA_GROUPS, NSA_HPG, NSA_HEAD_DIM
    points = np.cumsum(NSA_SPLIT_SIZES)[:-1].tolist()
    q, kc, vc, ks, vs, kw, vw, gate, z = jnp.split(u @ w_in, points, axis=-1)
    q = q.reshape(b, s, G, J, dh) * (dh ** -0.5)
    kc, vc, ks, vs, kw, vw = [t.reshape(b, s, G, dh) for t in (kc, vc, ks, vs, kw, vw)]
    gate = jax.nn.sigmoid(gate.astype(jnp.float32)).reshape(b, s, G, J, 3)

    k_cmp = compress(kc, pe_k, w1_k, w2_k)
    v_cmp = compress(vc, pe_v, w1_v, w2_v)
    nc = k_cmp.shape[1]
    cmp_lo = jnp.arange(nc) * CMP_STRIDE
    cmp_end = cmp_lo + CMP_BLOCK - 1
    n_sel = s // SEL_BLOCK
    topk = min(SEL_TOPK, n_sel)
    sel_lo = jnp.arange(n_sel) * SEL_BLOCK
    overlap = jnp.clip(jnp.minimum(cmp_lo[:, None] + CMP_BLOCK, sel_lo[None, :] + SEL_BLOCK)
                       - jnp.maximum(cmp_lo[:, None], sel_lo[None, :]), 0).astype(jnp.float32) / CMP_BLOCK

    table_g = table.reshape(REL_BUCKETS, G, J)
    table_gt = jnp.transpose(table_g, (1, 0, 2))
    ks_t = jnp.transpose(ks, (0, 2, 1, 3))
    vs_t = jnp.transpose(vs, (0, 2, 1, 3))
    kw_pad = jnp.pad(kw, ((0, 0), (WINDOW, 0), (0, 0), (0, 0)))
    vw_pad = jnp.pad(vw, ((0, 0), (WINDOW, 0), (0, 0), (0, 0)))
    bi = jnp.arange(b)[:, None, None, None]
    gi = jnp.arange(G)[None, :, None, None]
    blk_n = jnp.arange(n_sel)

    def block(qb):
        start = qb * NSA_QBLOCK
        t = start + jnp.arange(NSA_QBLOCK)
        qblk = lax.dynamic_slice_in_dim(q, start, NSA_QBLOCK, axis=1)

        dist_c = t[:, None] - cmp_end[None, :]
        m_c = dist_c >= 0
        bias_c = jnp.transpose(table_g[rel_bucket(dist_c)], (2, 3, 0, 1))
        s_c = jnp.einsum('bqgjd,bcgd->bgjqc', qblk, k_cmp).astype(jnp.float32) + bias_c
        p_c = jax.nn.softmax(jnp.where(m_c, s_c, NEG), axis=-1) * jnp.any(m_c, axis=-1)[:, None]
        o_c = jnp.einsum('bgjqc,bcgd->bqgjd', p_c.astype(v_cmp.dtype), v_cmp)

        imp = jnp.einsum('bgjqc,cn->bgqn', p_c, overlap)
        cur = t // SEL_BLOCK
        forced = (blk_n[None, :] == 0) | (blk_n[None, :] == cur[:, None]) | (blk_n[None, :] == cur[:, None] - 1)
        future = blk_n[None, :] > cur[:, None]
        imp = jnp.where(forced, BIG, jnp.where(future, -BIG, imp))
        _, sel = lax.top_k(imp, topk)
        pos = (sel[..., None] * SEL_BLOCK + jnp.arange(SEL_BLOCK)).reshape(b, G, NSA_QBLOCK, topk * SEL_BLOCK)
        k_g = ks_t[bi, gi, pos]
        v_g = vs_t[bi, gi, pos]
        dist_s = t[None, None, :, None] - pos
        bias_s = jnp.moveaxis(table_gt[gi, rel_bucket(dist_s)], -1, 2)
        s_s = jnp.einsum('bqgjd,bgqkd->bgjqk', qblk, k_g).astype(jnp.float32) + bias_s
        p_s = jax.nn.softmax(jnp.where((dist_s >= 0)[:, :, None], s_s, NEG), axis=-1)
        o_s = jnp.einsum('bgjqk,bgqkd->bqgjd', p_s.astype(v_g.dtype), v_g)

        k_win = lax.dynamic_slice_in_dim(kw_pad, start, NSA_QBLOCK + WINDOW, axis=1)
        v_win = lax.dynamic_slice_in_dim(vw_pad, start, NSA_QBLOCK + WINDOW, axis=1)
        pos_w = start - WINDOW + jnp.arange(NSA_QBLOCK + WINDOW)
        dist_w = t[:, None] - pos_w[None, :]
        m_w = (dist_w >= 0) & (dist_w < WINDOW) & (pos_w[None, :] >= 0)
        bias_w = jnp.transpose(table_g[rel_bucket(dist_w)], (2, 3, 0, 1))
        s_w = jnp.einsum('bqgjd,bkgd->bgjqk', qblk, k_win).astype(jnp.float32) + bias_w
        p_w = jax.nn.softmax(jnp.where(m_w, s_w, NEG), axis=-1)
        o_w = jnp.einsum('bgjqk,bkgd->bqgjd', p_w.astype(v_win.dtype), v_win)
        return o_c, o_s, o_w

    o_c, o_s, o_w = lax.map(block, jnp.arange(s // NSA_QBLOCK))
    o_c, o_s, o_w = [jnp.moveaxis(o, 0, 1).reshape(b, s, G, J, dh) for o in (o_c, o_s, o_w)]
    o = gate[..., 0:1] * o_c + gate[..., 1:2] * o_s + gate[..., 2:3] * o_w
    o = o.astype(u.dtype).reshape(b, s, NSA_WIDTH) * jax.nn.silu(z)
    return o @ w_out

def diff_mixer(u, table, w_in, lq1, lk1, lq2, lk2, subln, w_out, lambda_init):
    b, s, _ = u.shape
    H, d, dv = DIFF_HEADS, DIFF_HALF, DIFF_VDIM
    q, k, v, z = jnp.split(u @ w_in, 4, axis=-1)
    q = q.reshape(b, s, H, 2, d) * (d ** -0.5)
    k = k.reshape(b, s, H, 2, d)
    v = v.reshape(b, s, H, dv)
    lam = (jnp.exp(jnp.sum(lq1.astype(jnp.float32) * lk1.astype(jnp.float32)))
           - jnp.exp(jnp.sum(lq2.astype(jnp.float32) * lk2.astype(jnp.float32))) + lambda_init)
    table_h = table.reshape(REL_BUCKETS, H, 2)
    kpos = jnp.arange(s)

    def block(qb):
        start = qb * DIFF_QBLOCK
        t = start + jnp.arange(DIFF_QBLOCK)
        qblk = lax.dynamic_slice_in_dim(q, start, DIFF_QBLOCK, axis=1)
        dist = t[:, None] - kpos[None, :]
        bias = jnp.transpose(table_h[rel_bucket(dist)], (2, 3, 0, 1))
        sc = jnp.einsum('bqhmd,bkhmd->bhmqk', qblk, k).astype(jnp.float32) + bias
        p = jax.nn.softmax(jnp.where(dist >= 0, sc, NEG), axis=-1)
        a = p[:, :, 0] - lam * p[:, :, 1]
        return jnp.einsum('bhqk,bkhe->bqhe', a.astype(v.dtype), v)

    o = lax.map(block, jnp.arange(s // DIFF_QBLOCK))
    o = jnp.moveaxis(o, 0, 1).reshape(b, s, H, dv)
    o = rmsnorm(o, subln.reshape(H, dv)) * (1.0 - lambda_init)
    o = o.reshape(b, s, DIFF_WIDTH) * jax.nn.silu(z)
    return o @ w_out

def first_inputs(seed: int = 0) -> dict:
    key = jax.random.key(seed)
    ks = jax.random.split(key, 20)
    nrm = jax.random.normal
    f32 = jnp.float32
    A, Bn = N_NSA_LAYERS, N_DIFF_LAYERS
    ld = CMP_BLOCK * NSA_HEAD_DIM
    return {
        "x": nrm(ks[0], (BATCH, SEQ, D_MODEL), f32),
        "rel_bias_table": 0.3 * nrm(ks[1], (REL_BUCKETS, N_BIAS_MAPS), f32),
        "norm_pre": 1.0 + 0.05 * nrm(ks[2], (DEPTH, D_MODEL), f32),
        "norm_post": 1.0 + 0.05 * nrm(ks[3], (DEPTH, D_MODEL), f32),
        "nsa_w_in": nrm(ks[4], (A, D_MODEL, NSA_IN), f32) * D_MODEL ** -0.5,
        "nsa_cmp_pe_k": 0.5 * nrm(ks[5], (A, CMP_BLOCK, NSA_HEAD_DIM), f32),
        "nsa_cmp_w1_k": nrm(ks[6], (A, ld, CMP_HIDDEN), f32) * ld ** -0.5,
        "nsa_cmp_w2_k": nrm(ks[7], (A, CMP_HIDDEN, NSA_HEAD_DIM), f32) * CMP_HIDDEN ** -0.5,
        "nsa_cmp_pe_v": 0.5 * nrm(ks[8], (A, CMP_BLOCK, NSA_HEAD_DIM), f32),
        "nsa_cmp_w1_v": nrm(ks[9], (A, ld, CMP_HIDDEN), f32) * ld ** -0.5,
        "nsa_cmp_w2_v": nrm(ks[10], (A, CMP_HIDDEN, NSA_HEAD_DIM), f32) * CMP_HIDDEN ** -0.5,
        "nsa_w_out": nrm(ks[11], (A, NSA_WIDTH, D_MODEL), f32) * NSA_WIDTH ** -0.5,
        "diff_w_in": nrm(ks[12], (Bn, D_MODEL, DIFF_IN), f32) * D_MODEL ** -0.5,
        "diff_lambda_q1": 0.1 * nrm(ks[13], (Bn, DIFF_HALF), f32),
        "diff_lambda_k1": 0.1 * nrm(ks[14], (Bn, DIFF_HALF), f32),
        "diff_lambda_q2": 0.1 * nrm(ks[15], (Bn, DIFF_HALF), f32),
        "diff_lambda_k2": 0.1 * nrm(ks[16], (Bn, DIFF_HALF), f32),
        "diff_subln": 1.0 + 0.05 * nrm(ks[17], (Bn, DIFF_WIDTH), f32),
        "diff_w_out": nrm(ks[18], (Bn, DIFF_WIDTH, D_MODEL), f32) * DIFF_WIDTH ** -0.5,
    }

def first_block(x, rel_bias_table, norm_pre, norm_post, nsa_w_in, nsa_cmp_pe_k, nsa_cmp_w1_k,
              nsa_cmp_w2_k, nsa_cmp_pe_v, nsa_cmp_w1_v, nsa_cmp_w2_v, nsa_w_out, diff_w_in,
              diff_lambda_q1, diff_lambda_k1, diff_lambda_q2, diff_lambda_k2, diff_subln, diff_w_out):
    for i in range(DEPTH):
        u = rmsnorm(x, norm_pre[i])
        j = i // N_MIXERS
        if i % N_MIXERS == 0:
            y = nsa_mixer(u, rel_bias_table, nsa_w_in[j], nsa_cmp_pe_k[j], nsa_cmp_w1_k[j],
                          nsa_cmp_w2_k[j], nsa_cmp_pe_v[j], nsa_cmp_w1_v[j], nsa_cmp_w2_v[j],
                          nsa_w_out[j])
        else:
            lambda_init = 0.8 - 0.6 * math.exp(-0.3 * i)
            y = diff_mixer(u, rel_bias_table, diff_w_in[j], diff_lambda_q1[j], diff_lambda_k1[j],
                           diff_lambda_q2[j], diff_lambda_k2[j], diff_subln[j], diff_w_out[j],
                           lambda_init)
        x = x + rmsnorm(y, norm_post[i])
    return x


N_A_LAYERS = DEPTH // 2
N_B_LAYERS = DEPTH - N_A_LAYERS
HEAD_DIM = 64
RWKV_HEADS = D_MODEL // HEAD_DIM
DECAY_LORA = 64
AAA_LORA = 64
GATE_LORA = 160
ATTN_HEADS = D_MODEL // HEAD_DIM
KV_HEADS = 4
GROUP = ATTN_HEADS // KV_HEADS
WINDOW_2 = 128
BLOCK = 128
D_FF = 2816
CONV_WIDTH = 3
RMS_EPS = 1e-6
GN_EPS = 64e-5
NEG_INF = -1e30


def rms_norm(x, g):
    xf = x.astype(jnp.float32)
    y = xf * lax.rsqrt(jnp.mean(xf * xf, axis=-1, keepdims=True) + RMS_EPS)
    return (y * g.astype(jnp.float32)).astype(x.dtype)

def conv_ffn(x, w_up, conv_w, conv_b, w_down):
    h = x @ w_up
    c = h.shape[-1]
    h = lax.conv_general_dilated(
        h, conv_w[:, None, :].astype(h.dtype), window_strides=(1,),
        padding=[(CONV_WIDTH - 1, 0)], dimension_numbers=('NWC', 'WIO', 'NWC'),
        feature_group_count=c) + conv_b
    a, u = jnp.split(h, 2, axis=-1)
    return (jax.nn.gelu(a, approximate=True) * u) @ w_down

def rwkv7_time_mix(x, mu, w_rkv, w_decay0, w_decay1, w_decay2, a0, a1, a2, g1, g2,
                   k_k, k_a, r_k, gn_g, gn_b, w_o):
    B, T, D = x.shape
    H, N = RWKV_HEADS, HEAD_DIM
    f32 = jnp.float32
    xx = jnp.pad(x, ((0, 0), (1, 0), (0, 0)))[:, :-1] - x
    xr, xw, xk, xv, xa, xg = [x + xx * mu[i] for i in range(6)]
    r = xr @ w_rkv[0]
    k = xk @ w_rkv[1]
    v = xv @ w_rkv[2]
    w = -jax.nn.softplus(-(w_decay0 + jnp.tanh(xw @ w_decay1) @ w_decay2)) - 0.5
    a = jax.nn.sigmoid(a0 + (xa @ a1) @ a2)
    g = jax.nn.sigmoid(xg @ g1) @ g2
    heads = lambda z: z.reshape(B, T, H, N).astype(f32)
    kk = heads(k * k_k)
    kk = kk * lax.rsqrt(jnp.maximum(jnp.sum(kk * kk, axis=-1, keepdims=True), 1e-24))
    k = k * (1 + (a - 1) * k_a)
    r_h, k_h, v_h, a_h = heads(r), heads(k), heads(v), heads(a)
    decay = jnp.exp(-jnp.exp(heads(w)))
    vec_a, vec_b = -kk, kk * a_h

    def step(S, inp):
        r_t, d_t, k_t, v_t, a_t, b_t = inp
        sa = jnp.einsum('bhij,bhj->bhi', S, a_t)
        S = (S * d_t[:, :, None, :] + sa[..., None] * b_t[:, :, None, :]
             + v_t[..., None] * k_t[:, :, None, :])
        return S, jnp.einsum('bhij,bhj->bhi', S, r_t)

    seq_first = lambda z: jnp.moveaxis(z, 1, 0)
    state0 = jnp.zeros((B, H, N, N), f32)
    _, y = lax.scan(step, state0, tuple(seq_first(z) for z in (r_h, decay, k_h, v_h, vec_a, vec_b)))
    y = jnp.moveaxis(y, 0, 1)
    mean = jnp.mean(y, axis=-1, keepdims=True)
    var = jnp.mean(jnp.square(y - mean), axis=-1, keepdims=True)
    y = ((y - mean) * lax.rsqrt(var + GN_EPS)).reshape(B, T, D)
    y = y * gn_g.astype(f32) + gn_b.astype(f32)
    bonus = jnp.sum(r_h * k_h * r_k.astype(f32), axis=-1, keepdims=True) * v_h
    y = y + bonus.reshape(B, T, D)
    return (y * g.astype(f32)).astype(x.dtype) @ w_o

def shared_kv(h, kv_g, w_kv):
    B, T, _ = h.shape
    kv = rms_norm(h, kv_g) @ w_kv
    k, v = jnp.split(kv, 2, axis=-1)
    return k.reshape(B, T, KV_HEADS, HEAD_DIM), v.reshape(B, T, KV_HEADS, HEAD_DIM)

def swa_sink_attention(x, k, v, w_q, sinks, w_o):
    B, T, D = x.shape
    nb = T // BLOCK
    q = (x @ w_q).reshape(B, nb, BLOCK, KV_HEADS, GROUP, HEAD_DIM)

    def band(z):
        zp = jnp.pad(z, ((0, 0), (BLOCK, 0), (0, 0), (0, 0))).reshape(B, nb + 1, BLOCK, KV_HEADS, HEAD_DIM)
        return jnp.concatenate([zp[:, :-1], zp[:, 1:]], axis=2)

    kb, vb = band(k), band(v)
    s = jnp.einsum('bnqhgd,bnkhd->bnhgqk', q, kb).astype(jnp.float32) * (HEAD_DIM ** -0.5)
    q_pos = jnp.arange(BLOCK)[:, None]
    k_pos = jnp.arange(2 * BLOCK)[None, :] - BLOCK
    rel = q_pos - k_pos
    in_window = (rel >= 0) & (rel < WINDOW_2)
    blk = jnp.arange(nb)[:, None, None]
    mask = in_window[None] & ((blk > 0) | (k_pos[None] >= 0))
    s = jnp.where(mask[None, :, None, None], s, NEG_INF)
    sk = sinks.astype(jnp.float32).reshape(1, 1, KV_HEADS, GROUP, 1, 1)
    m = jnp.maximum(jnp.max(s, axis=-1, keepdims=True), sk)
    p = jnp.exp(s - m)
    denom = jnp.sum(p, axis=-1, keepdims=True) + jnp.exp(sk - m)
    o = jnp.einsum('bnhgqk,bnkhd->bnqhgd', (p / denom).astype(vb.dtype), vb)
    return o.reshape(B, T, ATTN_HEADS * HEAD_DIM) @ w_o

def second_inputs(seed: int = 0) -> dict:
    key = jax.random.key(seed)
    ks = jax.random.split(key, 27)
    nrm = lambda k, shape, scale: jax.random.normal(k, shape, jnp.float32) * scale
    D, NA, NB = D_MODEL, N_A_LAYERS, N_B_LAYERS
    return {
        'x': nrm(ks[0], (BATCH, SEQ, D), 1.0),
        'norm_g': 1.0 + nrm(ks[1], (DEPTH, 4, D), 0.05),
        'mu': jax.random.uniform(ks[2], (NA, 6, D), jnp.float32),
        'w_rkv': nrm(ks[3], (NA, 3, D, D), D ** -0.5),
        'w_decay0': jax.random.uniform(ks[4], (NA, D), jnp.float32, -6.5, -1.5),
        'w_decay1': nrm(ks[5], (NA, D, DECAY_LORA), D ** -0.5),
        'w_decay2': nrm(ks[6], (NA, DECAY_LORA, D), 0.1 * DECAY_LORA ** -0.5),
        'a0': nrm(ks[7], (NA, D), 0.1),
        'a1': nrm(ks[8], (NA, D, AAA_LORA), D ** -0.5),
        'a2': nrm(ks[9], (NA, AAA_LORA, D), 0.5 * AAA_LORA ** -0.5),
        'g1': nrm(ks[10], (NA, D, GATE_LORA), D ** -0.5),
        'g2': nrm(ks[11], (NA, GATE_LORA, D), GATE_LORA ** -0.5),
        'k_k': 0.85 + nrm(ks[12], (NA, D), 0.05),
        'k_a': 1.0 + nrm(ks[13], (NA, D), 0.05),
        'r_k': nrm(ks[14], (NA, RWKV_HEADS, HEAD_DIM), 0.1),
        'gn_g': 1.0 + nrm(ks[15], (NA, D), 0.05),
        'gn_b': nrm(ks[16], (NA, D), 0.01),
        'w_o_rwkv': nrm(ks[17], (NA, D, D), D ** -0.5),
        'kv_g': 1.0 + nrm(ks[18], (D,), 0.05),
        'w_kv': nrm(ks[19], (D, 2 * KV_HEADS * HEAD_DIM), D ** -0.5),
        'w_q': nrm(ks[20], (NB, D, ATTN_HEADS * HEAD_DIM), D ** -0.5),
        'sinks': nrm(ks[21], (NB, ATTN_HEADS), 0.5),
        'w_o_attn': nrm(ks[22], (NB, ATTN_HEADS * HEAD_DIM, D), (ATTN_HEADS * HEAD_DIM) ** -0.5),
        'w_up': nrm(ks[23], (DEPTH, D, 2 * D_FF), D ** -0.5),
        'conv_w': nrm(ks[24], (DEPTH, CONV_WIDTH, 2 * D_FF), CONV_WIDTH ** -0.5),
        'conv_b': nrm(ks[25], (DEPTH, 2 * D_FF), 0.01),
        'w_down': nrm(ks[26], (DEPTH, D_FF, D), D_FF ** -0.5),
    }

def second_block(x, norm_g, mu, w_rkv, w_decay0, w_decay1, w_decay2, a0, a1, a2, g1, g2,
              k_k, k_a, r_k, gn_g, gn_b, w_o_rwkv, kv_g, w_kv, w_q, sinks, w_o_attn,
              w_up, conv_w, conv_b, w_down):
    k_sh = v_sh = None
    for l in range(DEPTH):
        h = rms_norm(x, norm_g[l, 0])
        if l < N_A_LAYERS:
            i = l
            h = rwkv7_time_mix(h, mu[i], w_rkv[i], w_decay0[i], w_decay1[i], w_decay2[i],
                               a0[i], a1[i], a2[i], g1[i], g2[i], k_k[i], k_a[i], r_k[i],
                               gn_g[i], gn_b[i], w_o_rwkv[i])
        else:
            j = l - N_A_LAYERS
            h = swa_sink_attention(h, k_sh, v_sh, w_q[j], sinks[j], w_o_attn[j])
        x = x + rms_norm(h, norm_g[l, 1])
        h = conv_ffn(rms_norm(x, norm_g[l, 2]), w_up[l], conv_w[l], conv_b[l], w_down[l])
        x = x + rms_norm(h, norm_g[l, 3])
        if l == N_A_LAYERS - 1:
            k_sh, v_sh = shared_kv(x, kv_g, w_kv)
    return x


def setup_inputs(seed=0):
    out = dict(first_inputs(seed))
    for name, value in second_inputs(seed + 1).items():
        if name != "x":
            out[name + "_2"] = value
    return out


def reference(
    x, rel_bias_table, norm_pre, norm_post, nsa_w_in, nsa_cmp_pe_k, nsa_cmp_w1_k, nsa_cmp_w2_k,
    nsa_cmp_pe_v, nsa_cmp_w1_v, nsa_cmp_w2_v, nsa_w_out, diff_w_in, diff_lambda_q1,
    diff_lambda_k1, diff_lambda_q2, diff_lambda_k2, diff_subln, diff_w_out, norm_g_2, mu_2,
    w_rkv_2, w_decay0_2, w_decay1_2, w_decay2_2, a0_2, a1_2, a2_2, g1_2, g2_2, k_k_2, k_a_2,
    r_k_2, gn_g_2, gn_b_2, w_o_rwkv_2, kv_g_2, w_kv_2, w_q_2, sinks_2, w_o_attn_2, w_up_2,
    conv_w_2, conv_b_2, w_down_2,
):
    x = first_block(
        x, rel_bias_table, norm_pre, norm_post, nsa_w_in, nsa_cmp_pe_k, nsa_cmp_w1_k,
        nsa_cmp_w2_k, nsa_cmp_pe_v, nsa_cmp_w1_v, nsa_cmp_w2_v, nsa_w_out, diff_w_in,
        diff_lambda_q1, diff_lambda_k1, diff_lambda_q2, diff_lambda_k2, diff_subln, diff_w_out,
    )
    return second_block(
        x, norm_g_2, mu_2, w_rkv_2, w_decay0_2, w_decay1_2, w_decay2_2, a0_2, a1_2, a2_2, g1_2,
        g2_2, k_k_2, k_a_2, r_k_2, gn_g_2, gn_b_2, w_o_rwkv_2, kv_g_2, w_kv_2, w_q_2, sinks_2,
        w_o_attn_2, w_up_2, conv_w_2, conv_b_2, w_down_2,
    )


_drawn_inputs = setup_inputs


def setup_inputs(seed=0):
    import zlib

    import numpy as np

    out = dict(_drawn_inputs(seed))
    spreads = {}
    factors = {'w_decay1_2': 8.0, 'w_decay2_2': 8.0, 'gn_b_2': 5.724, 'sinks_2': 8.0, 'conv_b_2': 5.84}
    for name, (base, spread) in spreads.items():
        noise = np.random.default_rng([zlib.crc32(name.encode()), seed]).standard_normal(out[name].shape)
        drawn = base * np.exp(spread * noise) if base else spread * noise
        out[name] = __import__('jax').numpy.asarray(drawn.astype(out[name].dtype))
    for name, factor in factors.items():
        out[name] = (out[name] * factor).astype(out[name].dtype)
    return out
```

```python
from contextlib import ExitStack

import numpy as np

import concourse.bass as bass
from concourse import mybir

ALU = mybir.AluOpType
ACT = mybir.ActivationFunctionType
AX = mybir.AxisListType.X
F32 = mybir.dt.float32
BF16 = mybir.dt.bfloat16

P = 128
T = 512
NT = T // P
D = 1024
KD = D // P
NEG = -1e30
EPS = 1e-6

HEADS, GROUPS, HPG, DH = 16, 4, 4, 64
BUCKETS, MAX_DIST = 32, 128
CMP_BLOCK, CMP_STRIDE = 32, 16
NC = (T - CMP_BLOCK) // CMP_STRIDE + 1
NCP = 32
CMP_K = CMP_BLOCK * DH // P
DIFF_HEADS = 8
LAMBDA_INIT = 0.8 - 0.6 * float(np.exp(-0.3))
NSA_IN = D + 6 * 256 + 3 * HEADS + D
D_FF = 2816
FT = D_FF // P
RH = 16
GN_EPS = 64e-5
DECAY_SCALE = float(np.exp(-0.5))
LEVELS = 7

DIST0 = (NCP - 1) * CMP_STRIDE + CMP_BLOCK - 1 + 1
NDIST = DIST0 + T


def distance_one_hot():
    n = np.arange(NDIST) - DIST0
    exact = BUCKETS // 2
    nf = np.maximum(n, 1)
    large = exact + (np.log(nf / exact) / np.log(MAX_DIST / exact) * (BUCKETS - exact) + 1e-9).astype(np.int64)
    bucket = np.where(n < exact, np.maximum(n, 0), np.minimum(large, BUCKETS - 1))
    table = np.zeros((P, NDIST), np.float32)
    for part in range(3):
        table[32 * part + bucket, np.arange(NDIST)] = n >= 0
    table[96] = n < 0
    return table


C_IDENT = 0
C_HEADSUM = C_IDENT + P
C_HEADSEL = C_HEADSUM + P
C_BAND = C_HEADSEL + 2
C_STRICT_T = C_BAND + 2 * P
C_INCL_T = C_STRICT_T + P
C_PAIR = C_INCL_T + P
C_PAIR_T = C_PAIR + P
C_ONES = C_PAIR_T + P
C_LEVEL_T = C_ONES + P
N_CONST = C_LEVEL_T + (LEVELS - 1) * P


def shape_constants():
    c = np.zeros((P, N_CONST), np.float32)
    r = np.arange(P)
    c[:, C_IDENT:C_IDENT + P] = np.eye(P)
    c[:, C_HEADSUM:C_HEADSUM + P] = (r[:, None] // DH) == (r[None] // DH)
    c[:, C_HEADSEL:C_HEADSEL + 2] = (r[:, None] // DH) == np.arange(2)[None]
    c[:, C_BAND:C_BAND + P] = np.where(r[None] > r[:, None], 0.0, NEG)
    c[:, C_BAND + P:C_BAND + 2 * P] = np.where(r[None] <= r[:, None], 0.0, NEG)
    c[:, C_STRICT_T:C_STRICT_T + P] = r[:, None] < r[None]
    c[:, C_INCL_T:C_INCL_T + P] = r[:, None] <= r[None]
    pair = (r[None] == r[:, None] - 1) & (r[:, None] % 2 == 1)
    c[:, C_PAIR:C_PAIR + P] = pair
    c[:, C_PAIR_T:C_PAIR_T + P] = pair.T
    c[:, C_ONES:C_ONES + P] = 1.0
    for lv in range(1, LEVELS):
        b = 1 << lv
        low = (r[:, None] // (2 * b) == r[None] // (2 * b)) & (r[:, None] // b % 2 == 1) & (r[None] // b % 2 == 0)
        c[:, C_LEVEL_T + (lv - 1) * P:C_LEVEL_T + lv * P] = low.T
    return c


V_PRE = 0
V_G = 16
V_MU = 80
V_B = 128
V_CONV = 176
N_VEC = V_CONV + 2 * 176


class Env:

    RING = 2

    def __init__(self, nc, ctx, io):
        self.nc, self.ctx, self.io = nc, ctx, io
        words = 52500
        self.arena = ctx.enter_context(nc.sbuf_tensor("arena", [P, words], F32))
        self.words = words
        self.ps = ctx.enter_context(nc.psum_tensor("ps", [P, 8, 512], F32))
        self.at = 0
        self.x = self.take(NT, D)
        self.uT = self.take(KD, T)
        self.big = self.take(4096)
        self.ring = self.take(self.RING, 4096)
        self.const = self.take(N_CONST)
        self.vec = self.take(N_VEC)
        self.grow = self.take(D)
        self.stat_at = self.at
        self.stat = self.take(256)
        self.junk = self.take(512)
        self.junk2 = self.take(2, 512)
        self.area = self.at
        self.ident = self.const[:, C_IDENT:C_IDENT + P]
        self.proj_ready = self.sem("proj_ready")
        self.proj_taken = self.sem("proj_taken")
        self.groups = 0
        self.w_arrived = [self.sem(f"w_arrived{r}") for r in range(self.RING)]
        self.loads = []
        self.aux_arrived = self.sem("aux_arrived")
        self.stage_done = self.sem("stage_done")
        self.dve_step = self.sem("dve_step")
        self.act_step = self.sem("act_step")
        self.pool_step = self.sem("pool_step")
        self.ssq_ready = self.sem("ssq_ready")
        self.ms_ready = self.sem("ms_ready")
        self.rstd_ready = self.sem("rstd_ready")
        self.un_ready = self.sem("un_ready")
        self.tr_ready = self.sem("tr_ready")
        self.uT_ready = self.sem("uT_ready")
        self.norms = 0
        self.oT_ready = self.sem("oT_ready")
        self.yms_ready = self.sem("yms_ready")
        self.yrstd_ready = self.sem("yrstd_ready")
        self.g_arrived = self.sem("g_arrived")
        self.outs = 0
        self.trs = 0
        self.ots = 0
        self.slots_done = 0
        self.slot_done = self.sem("slot_done")
        self.stored = self.sem("stored")
        self.aux = 0
        self.x_added = self.sem("x_added")

    def sem(self, name):
        return self.ctx.enter_context(self.nc.semaphore(name))

    def take(self, *shape, at=None):
        n = int(np.prod(shape))
        if at is None:
            at = self.at
            self.at += n
        assert at + n <= self.words, (at + n, self.words)
        v = self.arena[:, at:at + n]
        if len(shape) == 2:
            v = v.rearrange("p (a b) -> p a b", a=shape[0])
        if len(shape) == 3:
            v = v.rearrange("p (a b c) -> p a b c", a=shape[0], b=shape[1])
        return v

    def group(self, n=1):
        g = self.groups
        self.groups += n
        return g

    def load(self, *parts):
        self.loads.append([parts, None, None])
        return len(self.loads) - 1

    def slot(self, load, k, n, first=0):
        return self.ring[:, load % self.RING, first:first + k * n].rearrange("p (k n) -> p k n", k=k)

    def release(self, load, sem, value):
        self.loads[load][1:] = [sem, value]

    def wait_load(self, pe, load):
        n = sum(len(parts) for parts, _, _ in self.loads[load % self.RING:load + 1:self.RING])
        pe.wait_ge(self.w_arrived[load % self.RING], 16 * n)

    def bank(self, g):
        return self.ps[:, g % 4, :]

    def wait_bank(self, pe, g):
        if g >= 4:
            pe.wait_ge(self.proj_taken, g - 3)


class Steps:

    def __init__(self, eng, sem):
        self.eng, self.sem, self.n = eng, sem, 0

    def __call__(self, ins):
        self.n += 1
        ins.then_inc(self.sem, 1)
        self.eng.wait_ge(self.sem, self.n)


def w_cols(w, c0, n):
    return w.rearrange("(k p) m -> p k m", p=P)[:, :, c0:c0 + n]


def project_features(env, pe, load, m0, rhs, g, kd=KD, cols=None):
    nc = env.nc
    w = env.slot(load, kd, cols or 4096 // kd)
    env.wait_bank(pe, g)
    for k in range(kd):
        mm = nc.tensor.matmul(env.bank(g), w[:, k, m0:m0 + P], rhs[:, k, :], start=(k == 0), stop=(k == kd - 1))
    mm.then_inc(env.proj_ready, 1)


def project_tokens(env, pe, load, c0, n, lhs, tile, g, kd=KD, cols=None):
    nc = env.nc
    w = env.slot(load, kd, cols or 4096 // kd)
    env.wait_bank(pe, g)
    for k in range(kd):
        mm = nc.tensor.matmul(env.bank(g)[:, 0:n], lhs[:, k, tile * P:(tile + 1) * P], w[:, k, c0:c0 + n],
                              start=(k == 0), stop=(k == kd - 1))
    mm.then_inc(env.proj_ready, 1)


class Stage:
    def __init__(self, env):
        self.env = env

    def tensor(self, pe):
        pass

    def scalar(self, act, step):
        pass

    def vector(self, dve, step):
        pass

    def gpsimd(self, pool, step):
        pass


class Setup(Stage):

    def __init__(self, env):
        super().__init__(env)
        self.bias = env.take(HEADS, T, at=env.words - HEADS * T)
        at = env.area
        self.rows = env.take(6, P, at=at)
        self.tab = env.take(HEADS, at=at + 1000)
        self.tab_rest = env.take(HEADS, at=at + 1016)
        self.hot = env.ctx.enter_context(env.nc.sbuf_tensor("one_hot", [P, NDIST], BF16))
        self.tab_hi = env.ctx.enter_context(env.nc.sbuf_tensor("table_parts", [P, 3, HEADS], BF16))
        self.table3 = env.ctx.enter_context(env.nc.sbuf_tensor("table3", [P, HEADS], BF16))
        self.x_arrived = env.sem("x_arrived")
        self.table_ready = env.sem("table_ready")
        self.rows_zeroed = env.sem("rows_zeroed")
        self.bias_ready = env.sem("bias_ready")
        self.bias_taken = env.sem("bias_taken")
        self.vec_ready = env.sem("vec_ready")
        self.vec_taken = env.sem("vec_taken")
        self.rows_arrived = env.sem("rows_arrived")
        self.tab_arrived = env.sem("tab_arrived")
        self.const_arrived = env.sem("const_arrived")

    def load(self, sp):
        env, io, nc = self.env, self.env.io, self.env.nc
        sp.dma_start(env.x, io["x"].rearrange("b (t p) d -> p (b t) d", p=P)).then_inc(self.x_arrived, 16)
        sp.dma_start(env.const, io["shape_constants"]).then_inc(self.const_arrived, 16)
        sp.wait_ge(self.rows_zeroed, 1)
        for part in range(3):
            sp.dma_start(self.tab[32 * part:32 * part + 32, :], io["rel_bias_table"]).then_inc(self.tab_arrived, 16)
        sp.dma_start(self.hot[:], io["distance_one_hot"]).then_inc(self.tab_arrived, 16)
        r = self.rows
        vec = lambda a: a.rearrange("(k p) -> k p", p=P)
        put = lambda row, at, n, src: sp.dma_start(r[at:at + n, row, :], src).then_inc(self.rows_arrived, 16)
        put(0, 0, 16, io["norm_pre"].rearrange("l (k p) -> (l k) p", p=P))
        put(0, 16, 64, io["norm_g_2"].rearrange("l w (k p) -> (l w k) p", p=P))
        put(0, 80, 48, io["mu_2"].rearrange("a i (k p) -> (a i k) p", p=P))
        for n, name in enumerate(["w_decay0_2", "a0_2", "k_k_2", "k_a_2"]):
            put(1, 8 * n, 8, io[name].rearrange("a (k p) -> (a k) p", p=P))
        put(1, 32, 8, io["r_k_2"].rearrange("a (k h) n -> (a k) (h n)", h=2))
        put(1, 40, 8, vec(io["kv_g_2"]))
        for l in range(2):
            w = io["conv_w_2"][l].rearrange("w (k p) -> (w k) p", p=P)
            put(2 + 2 * l, 0, 88, w[0:88])
            put(3 + 2 * l, 0, 44, w[88:132])
            put(3 + 2 * l, 44, 44, vec(io["conv_b_2"][l]))
    N_ROWS = 3 + 4 + 2 + 6

    def tensor(self, pe):
        env, nc = self.env, self.env.nc
        pe.wait_ge(self.rows_arrived, 16 * self.N_ROWS)
        pe.wait_ge(self.const_arrived, 16)
        for n in range(6):
            size = [128, 48, 88, 88, 88, 88][n]
            tr = nc.tensor.transpose(env.ps[:, n // 4, (n % 4) * P:(n % 4) * P + size], self.rows[0:size, n, :],
                                     env.ident[0:size, 0:size])
        tr.then_inc(self.vec_ready, 1)
        pe.wait_ge(self.table_ready, 1)
        pe.wait_ge(self.tab_arrived, 64)
        pe.wait_ge(self.vec_taken, 1)
        with pe.Fori(0, 8) as i:
            for c in range(32):
                mm = nc.tensor.matmul(env.ps[:, i, c * HEADS:(c + 1) * HEADS],
                                      self.hot[:, bass.ds((DIST0 + P - c) - i * 32, P)],
                                      self.table3[:], start=True, stop=True)
            mm.then_inc(self.bias_ready, 1)

    def vector(self, dve, step):
        env, nc = self.env, self.env.nc
        nc.vector.memset(self.tab[:], 0.0).then_inc(self.rows_zeroed, 1)
        dve.wait_ge(self.tab_arrived, 64)
        dve.wait_ge(self.rows_zeroed, 1)
        step(nc.vector.tensor_copy(self.tab_hi[:, 0, :], self.tab))
        step(nc.vector.tensor_tensor(self.tab_rest, self.tab, self.tab_hi[:, 0, :], ALU.subtract))
        step(nc.vector.tensor_copy(self.tab_hi[:, 1, :], self.tab_rest))
        step(nc.vector.tensor_tensor(self.tab_rest, self.tab_rest, self.tab_hi[:, 1, :], ALU.subtract))
        step(nc.vector.tensor_copy(self.tab_hi[:, 2, :], self.tab_rest))
        for part in range(3):
            q = slice(32 * part, 32 * part + 32)
            nc.vector.tensor_copy(self.table3[q, :], self.tab_hi[q, part, :])
        nc.vector.memset(self.table3[96:128, :], NEG).then_inc(self.table_ready, 1)
        dve.wait_ge(self.vec_ready, 1)
        o = 0
        for n in range(6):
            size = [128, 48, 88, 88, 88, 88][n]
            step(nc.vector.tensor_copy(env.vec[:, o:o + size], env.ps[:, n // 4, (n % 4) * P:(n % 4) * P + size]))
            o += size
        nc.vector.memset(self.tab_rest, 0.0).then_inc(self.vec_taken, 1)
        with dve.Fori(0, 8) as i:
            dve.wait_ge(self.bias_ready, i + 1)
            nc.vector.tensor_copy(
                self.bias.rearrange("p h c -> p c h")[:, bass.ds(i * 32 + 2 * P, 32), :],
                env.ps[:, i, :].rearrange("p (c h) -> p c h", h=HEADS)).then_inc(self.bias_taken, 1)
        dve.wait_ge(self.bias_taken, 8)
        step(nc.vector.tensor_copy(self.bias[:, :, 0:2 * P],
                                   self.bias[:, :, 2 * P:2 * P + 1].to_broadcast([P, HEADS, 2 * P])))


class Norm(Stage):

    def __init__(self, env, col, x_arrived=None, raw=False):
        super().__init__(env)
        self.col, self.n, self.x_arrived = col, env.norms, x_arrived
        self.tr0 = env.trs
        env.trs += KD
        env.norms += 1
        self.un = env.big.rearrange("p (t d) -> p t d", t=NT)
        self.ssq, self.ms, self.rstd = env.stat[:, 0:4], env.stat[:, 4:8], env.stat[:, 8:12]

    def scalar(self, act, step):
        env, nc, n = self.env, self.env.nc, self.n
        if self.x_arrived is not None:
            act.wait_ge(self.x_arrived, 16)
        for t in range(NT):
            nc.scalar.activation(self.un[:, t, :], env.x[:, t, :], ACT.Square,
                                 accum_out=self.ssq[:, t:t + 1]).then_inc(env.ssq_ready, 1)
        act.wait_ge(env.ms_ready, n + 1)
        nc.scalar.activation(self.rstd, self.ms, ACT.Sqrt).then_inc(env.rstd_ready, 1)
        for k in range(KD):
            act.wait_ge(env.tr_ready, self.tr0 + k + 1)
            nc.scalar.activation(env.uT[:, k, :], env.ps[:, 6 + k % 2, :], ACT.Copy,
                                 scale=env.vec[:, self.col + k:self.col + k + 1]).then_inc(env.uT_ready, 1)

    def vector(self, dve, step):
        env, nc, n = self.env, self.env.nc, self.n
        dve.wait_ge(env.ssq_ready, 4 * n + 4)
        step(nc.vector.tensor_scalar(self.ms, self.ssq, 1.0 / D, EPS, ALU.mult, ALU.add))
        nc.vector.reciprocal(self.ms, self.ms).then_inc(env.ms_ready, 1)
        dve.wait_ge(env.rstd_ready, n + 1)
        for t in range(NT):
            nc.vector.tensor_scalar(self.un[:, t, :], env.x[:, t, :], self.rstd[:, t:t + 1], None,
                                    ALU.mult).then_inc(env.un_ready, 1)

    def tensor(self, pe):
        env, nc, n = self.env, self.env.nc, self.n
        pe.wait_ge(env.un_ready, 4 * n + 4)
        for k in range(KD):
            if k >= 2:
                pe.wait_ge(env.uT_ready, 8 * n + k - 1)
            for t in range(NT):
                tr = nc.tensor.transpose(env.ps[:, 6 + k % 2, t * P:(t + 1) * P], self.un[:, t, k * P:(k + 1) * P],
                                         env.ident)
            tr.then_inc(env.tr_ready, 1)
        pe.wait_ge(env.uT_ready, 8 * n + 8)


class Output(Stage):

    def __init__(self, env, w_out, g_row, oT, o=None, z=None, kd=KD):
        super().__init__(env)
        self.o, self.oT, self.kd, self.g_row = o, oT, kd, g_row
        self.n = env.outs
        env.outs += 1
        self.ot0, self.tr0 = env.ots, env.trs
        if o is not None:
            env.ots += KD
            env.trs += KD
        self.zload = []
        if z is not None:
            w, c0 = z
            for half in range(2):
                ld = env.load((0, KD, 512, w_cols(w, c0 + 512 * half, 512)))
                g = env.group(4)
                env.release(ld, env.proj_ready, g + 4)
                self.zload.append((ld, g))
        src = w_out.rearrange("(k p) m -> p k m", p=P)
        self.wload = []
        for k0 in range(0, kd, 4):
            m = min(4, kd - k0)
            self.wload.append((env.load((0, m, D, src[:, k0:k0 + m, :])), k0, m))
            if k0 + m < kd:
                env.slots_done += 1
                env.release(self.wload[-1][0], env.slot_done, env.slots_done)
        self.g0 = env.group(8)
        env.release(self.wload[-1][0], env.proj_ready, self.g0 + 8)
        self.y = env.big.rearrange("p (t d) -> p t d", t=NT)
        self.ssq, self.ms, self.rstd = env.stat[:, 16:24], env.stat[:, 24:28], env.stat[:, 28:32]
        self.ztmp = env.junk2

    def turn(self, pe, k):
        env, nc = self.env, self.env.nc
        if k >= 2:
            pe.wait_ge(env.oT_ready, self.ot0 + k - 1)
        for t in range(NT):
            tr = nc.tensor.transpose(env.ps[:, 6 + k % 2, t * P:(t + 1) * P], self.o[:, t, k * P:(k + 1) * P],
                                     env.ident)
        tr.then_inc(env.tr_ready, 1)

    def tensor(self, pe):
        env, nc = self.env, self.env.nc
        for half, (ld, g0) in enumerate(self.zload):
            env.wait_load(pe, ld)
            for m in range(4):
                project_features(env, pe, ld, m * P, env.uT, g0 + m)
                self.turn(pe, 4 * half + m)
        if self.o is not None and not self.zload:
            for k in range(KD):
                self.turn(pe, k)
        if self.o is not None:
            pe.wait_ge(env.oT_ready, self.ot0 + KD)
        if self.g0:
            pe.wait_ge(env.proj_taken, self.g0)
        for ld, k0, m in self.wload:
            env.wait_load(pe, ld)
            w = env.slot(ld, m, D)
            for k in range(k0, k0 + m):
                for i in range(NT):
                    for half in range(2):
                        mm = nc.tensor.matmul(env.ps[:, 2 * i + half, :], self.oT[:, k, i * P:(i + 1) * P],
                                              w[:, k - k0, 512 * half:512 * half + 512],
                                              start=(k == 0), stop=(k == self.kd - 1))
                        if k == self.kd - 1:
                            mm.then_inc(env.proj_ready, 1)
            if k0 + m < self.kd:
                mm.then_inc(env.slot_done, 1)

    def scalar(self, act, step):
        env, nc = self.env, self.env.nc
        for half, (ld, g0) in enumerate(self.zload):
            for m in range(4):
                k = 4 * half + m
                if k >= 2:
                    act.wait_ge(env.oT_ready, self.ot0 + k - 1)
                act.wait_ge(env.proj_ready, g0 + m + 1)
                nc.scalar.activation(self.ztmp[:, k % 2, :], env.bank(g0 + m), ACT.Silu).then_inc(env.proj_taken, 1)
        for i in range(NT):
            for half in range(2):
                act.wait_ge(env.proj_ready, self.g0 + 2 * i + half + 1)
                nc.scalar.activation(self.y[:, i, 512 * half:512 * half + 512], env.ps[:, 2 * i + half, :], ACT.Copy)
                act.wait_ge(env.proj_taken, self.g0 + 2 * i + half)
                nc.scalar.activation(env.junk, env.ps[:, 2 * i + half, :], ACT.Square,
                                     accum_out=self.ssq[:, 2 * i + half:2 * i + half + 1]).then_inc(env.proj_taken, 1)
        act.wait_ge(env.yms_ready, self.n + 1)
        nc.scalar.activation(self.rstd, self.ms, ACT.Sqrt).then_inc(env.yrstd_ready, 1)

    def gpsimd(self, pool, step):
        env = self.env
        pool.dma_start(env.grow, self.g_row.partition_broadcast(P)).then_inc(env.g_arrived, 16)

    def vector(self, dve, step):
        env, nc = self.env, self.env.nc
        if self.o is not None:
            for k in range(KD):
                dve.wait_ge(env.tr_ready, self.tr0 + k + 1)
                tr = env.ps[:, 6 + k % 2, :]
                if self.zload:
                    dve.wait_ge(env.proj_taken, self.zload[k // 4][1] + k % 4 + 1)
                    nc.vector.tensor_tensor(self.oT[:, k, :], tr, self.ztmp[:, k % 2, :],
                                            ALU.mult).then_inc(env.oT_ready, 1)
                else:
                    nc.vector.tensor_copy(self.oT[:, k, :], tr).then_inc(env.oT_ready, 1)
        dve.wait_ge(env.proj_taken, self.g0 + 8)
        pair = self.ssq.rearrange("p (t h) -> p t h", h=2)
        step(nc.vector.tensor_tensor(self.ms, pair[:, :, 0], pair[:, :, 1], ALU.add))
        step(nc.vector.tensor_scalar(self.ms, self.ms, 1.0 / D, EPS, ALU.mult, ALU.add))
        nc.vector.reciprocal(self.ms, self.ms).then_inc(env.yms_ready, 1)
        dve.wait_ge(env.g_arrived, 16 * (self.n + 1))
        dve.wait_ge(env.yrstd_ready, self.n + 1)
        for i in range(NT):
            step(nc.vector.scalar_tensor_tensor(self.y[:, i, :], self.y[:, i, :], self.rstd[:, i:i + 1], env.grow,
                                                ALU.mult, ALU.mult))
            nc.vector.tensor_tensor(env.x[:, i, :], env.x[:, i, :], self.y[:, i, :], ALU.add).then_inc(env.x_added, 1)


class NsaProject(Stage):

    def __init__(self, env, m):
        super().__init__(env)
        self.m = m
        w = env.io["nsa_w_in"][0]
        self.lds, self.gs = [], []
        for n in range(5):
            self.lds.append(env.load((0, KD, 512, w_cols(w, 512 * n, 512))))
            self.gs.append(env.group(4 if n < 3 else 6))
            env.release(self.lds[-1], env.proj_ready, env.groups)
        ng = 3 * HEADS
        self.lds.append(env.load((0, KD, ng, w_cols(w, 2560, ng))))
        self.gs.append(env.group(NT))
        env.release(self.lds[-1], env.proj_ready, env.groups)
        self.zero_done = env.sem("nsa_zero_done")

    def tensor(self, pe):
        env = self.env
        for n in range(3):
            env.wait_load(pe, self.lds[n])
            for j in range(4):
                project_features(env, pe, self.lds[n], j * P, env.uT, self.gs[n] + j)
        for n in range(3, 5):
            env.wait_load(pe, self.lds[n])
            for j in range(2):
                project_features(env, pe, self.lds[n], j * P, env.uT, self.gs[n] + j)
            for i in range(NT):
                project_tokens(env, pe, self.lds[n], 256, 256, env.uT, i, self.gs[n] + 2 + i)
        env.wait_load(pe, self.lds[5])
        for i in range(NT):
            project_tokens(env, pe, self.lds[5], 0, 3 * HEADS, env.uT, i, self.gs[5] + i, cols=3 * HEADS)

    def scalar(self, act, step):
        env, nc, m = self.env, self.env.nc, self.m
        for n in range(2):
            for j in range(4):
                g = self.gs[n] + j
                act.wait_ge(env.proj_ready, g + 1)
                nc.scalar.activation(m.qT[:, 4 * n + j, :], env.bank(g), ACT.Copy,
                                     scale=DH ** -0.5).then_inc(env.proj_taken, 1)
        for j in range(4):
            g = self.gs[2] + j
            dst = (m.kcT, m.vcT)[j // 2]
            act.wait_ge(env.proj_ready, g + 1)
            for half in range(2):
                src = env.bank(g)[64 * half:64 * half + 64, :]
                grp = 2 * (j % 2) + half
                nc.scalar.activation(dst[0:64, grp, :], src, ACT.Copy)
                cp = nc.scalar.activation(dst[64:128, grp, 0:T - 1], src[:, 1:T], ACT.Copy)
            cp.then_inc(env.proj_taken, 1)
        for n, (kT, v) in ((3, (m.ksT, m.vs)), (4, (m.kwT, m.vw))):
            for j in range(2):
                g = self.gs[n] + j
                act.wait_ge(env.proj_ready, g + 1)
                for half in range(2):
                    for to in range(2):
                        cp = nc.scalar.activation(kT[64 * to:64 * to + 64, 2 * j + half, :],
                                                  env.bank(g)[64 * half:64 * half + 64, :], ACT.Copy)
                cp.then_inc(env.proj_taken, 1)
            for i in range(NT):
                g = self.gs[n] + 2 + i
                act.wait_ge(env.proj_ready, g + 1)
                nc.scalar.activation(v[:, i, :], env.bank(g)[:, 0:256], ACT.Copy).then_inc(env.proj_taken, 1)
        for i in range(NT):
            g = self.gs[5] + i
            act.wait_ge(env.proj_ready, g + 1)
            nc.scalar.activation(m.gate[:, i, :], env.bank(g)[:, 0:3 * HEADS], ACT.Sigmoid).then_inc(env.proj_taken, 1)


class NsaCompress(Stage):

    def __init__(self, env, m):
        super().__init__(env)
        self.m = m
        self.aux = env.sem("cmp_weights")
        self.pe_rows_ready = env.sem("pe_cols_ready")
        self.pe_cols = env.sem("pe_cols_taken")
        self.hid_bias = env.sem("hid_bias")
        self.hid_bias_taken = env.sem("hid_bias_taken")
        self.hid_ready = env.sem("hid_ready")
        self.hid_taken = env.sem("hid_taken")
        self.cmp_ready = env.sem("cmp_ready")
        self.vbd_zeroed = env.sem("vbd_zeroed")

    def gpsimd(self, pool, step):
        env, m, io = self.env, self.m, self.env.io
        pool.dma_start(m.w1[0], io["nsa_cmp_w1_k"][0].rearrange("(k p) n -> p k n", p=P)).then_inc(self.aux, 16)
        pool.dma_start(m.w1[1], io["nsa_cmp_w1_v"][0].rearrange("(k p) n -> p k n", p=P)).then_inc(self.aux, 16)
        for to in range(2):
            pool.dma_start(m.w2[:, 64 * to:64 * to + 64], io["nsa_cmp_w2_k"][0]).then_inc(self.aux, 16)
        pool.dma_start(m.w2[:, 128:192], io["nsa_cmp_w2_v"][0]).then_inc(self.aux, 16)
        for kv, name in enumerate(("nsa_cmp_pe_k", "nsa_cmp_pe_v")):
            pool.dma_start(m.pe_rows[0:CMP_K, kv, :],
                           io[name][0].rearrange("(k two) d -> k (two d)", two=2)).then_inc(self.aux, 16)

    def tensor(self, pe):
        env, nc, m = self.env, self.env.nc, self.m
        pe.wait_ge(self.aux, 16 * 7)
        for kv in range(2):
            tr = nc.tensor.transpose(env.ps[:, 4, kv * CMP_K:(kv + 1) * CMP_K], m.pe_rows[0:CMP_K, kv, :],
                                     env.ident[0:CMP_K, 0:CMP_K])
        tr.then_inc(self.pe_rows_ready, 1)
        pe.wait_ge(self.pe_cols, 1)
        for kv in range(2):
            for k in range(CMP_K):
                mm = nc.tensor.matmul(env.ps[:, 5, 2 * kv:2 * kv + 2], m.w1[kv][:, k, :],
                                      m.pe_cols[:, kv * CMP_K + k:kv * CMP_K + k + 1].to_broadcast([P, 2]),
                                      start=(k == 0), stop=(k == CMP_K - 1))
        mm.then_inc(self.hid_bias, 1)
        for kv, src in enumerate((m.kcT, m.vcT)):
            for k in range(CMP_K):
                rhs = src[:, :, 2 * k:2 * k + CMP_STRIDE * (NC - 1) + 1:CMP_STRIDE]
                mm = nc.tensor.matmul(env.ps[:, 6 + kv, 0:GROUPS * NC], m.w1[kv][:, k, :], rhs,
                                      start=(k == 0), stop=(k == CMP_K - 1))
            mm.then_inc(self.hid_ready, 1)
        pe.wait_ge(self.hid_taken, 2)
        nc.tensor.matmul(env.ps[:, 4, 0:GROUPS * NC], m.w2[:, 0:128], m.hid[:, 0, 0:GROUPS * NC], start=True, stop=True)
        for g in range(GROUPS):
            mm = nc.tensor.matmul(env.ps[0:NC, 5, g * DH:(g + 1) * DH], m.hid[:, 1, g * NC:(g + 1) * NC],
                                  m.w2[:, 128:192], start=True, stop=True)
        mm.then_inc(self.cmp_ready, 1)

    def scalar(self, act, step):
        env, nc, m = self.env, self.env.nc, self.m
        act.wait_ge(self.hid_bias_taken, 1)
        for kv in range(2):
            act.wait_ge(self.hid_ready, kv + 1)
            nc.scalar.activation(m.hid[:, kv, 0:GROUPS * NC], env.ps[:, 6 + kv, 0:GROUPS * NC], ACT.Silu,
                                 bias=m.hid_bias[:, 2 * kv:2 * kv + 1]).then_inc(self.hid_taken, 1)

    def vector(self, dve, step):
        env, nc, m = self.env, self.env.nc, self.m
        nc.vector.memset(m.vbd, 0.0)
        step(nc.vector.memset(m.kcmp, 0.0))
        dve.wait_ge(self.pe_rows_ready, 1)
        nc.vector.tensor_copy(m.pe_cols, env.ps[:, 4, 0:2 * CMP_K]).then_inc(self.pe_cols, 1)
        dve.wait_ge(self.hid_bias, 1)
        nc.vector.tensor_copy(m.hid_bias, env.ps[:, 5, 0:4]).then_inc(self.hid_bias_taken, 1)
        dve.wait_ge(self.cmp_ready, 1)
        step(nc.vector.tensor_copy(m.kcmp[:, :, 0:NC], env.ps[:, 4, 0:GROUPS * NC].rearrange("p (g c) -> p g c", c=NC)))
        for j in range(HPG):
            step(nc.vector.tensor_copy(m.vbd[32 * j:32 * j + NC, :, DH * j:DH * j + DH],
                                       env.ps[0:NC, 5, 0:GROUPS * DH].rearrange("p (g d) -> p g d", d=DH)))


class NsaCompressed(Stage):

    def __init__(self, env, m):
        super().__init__(env)
        self.m = m
        self.bias_ready, self.bias_taken = env.sem("cbias_ready"), env.sem("cbias_taken")
        self.s_ready, self.s_taken = env.sem("cs_ready"), env.sem("cs_taken")
        self.shifted, self.p_ready, self.p_scaled = env.sem("c_shifted"), env.sem("cp_ready"), env.sem("cp_scaled")
        self.pT_ready, self.pT_taken = env.sem("cpT_ready"), env.sem("cpT_taken")
        self.o_ready, self.o_taken = env.sem("co_ready"), env.sem("co_taken")

    def tensor(self, pe):
        env, nc, m = self.env, self.env.nc, self.m
        for i in range(NT):
            if i:
                pe.wait_ge(self.bias_taken, i)
            out = env.ps[:, 6, :].rearrange("p (h c) -> p h c", c=NCP)
            for c in range(NCP):
                at = DIST0 + P * i - CMP_STRIDE * c - (CMP_BLOCK - 1)
                mm = nc.tensor.matmul(out[:, :, c], m.hot[:, at:at + P], m.table3[:], start=True, stop=True)
            mm.then_inc(self.bias_ready, 1)
            if i:
                pe.wait_ge(self.s_taken, i)
            for h in range(HEADS):
                half = 64 * (h % 2)
                mm = nc.tensor.matmul(env.ps[:, 7 - 5 * (h % 2), h // 2 * NCP:(h // 2 + 1) * NCP],
                                      m.qT[half:half + 64, h // 2, i * P:(i + 1) * P],
                                      m.kcmp[half:half + 64, h // HPG, :], start=True, stop=True)
            mm.then_inc(self.s_ready, 1)
            pe.wait_ge(self.p_scaled, i + 1)
            if i:
                pe.wait_ge(self.pT_taken, i)
            for g in range(GROUPS):
                tr = nc.tensor.transpose(env.ps[:, 5, g * P:(g + 1) * P], m.pc[:, g * P:(g + 1) * P], env.ident)
            tr.then_inc(self.pT_ready, 1)
            pe.wait_ge(self.pT_taken, i + 1)
            if i:
                pe.wait_ge(self.o_taken, i)
            for g in range(GROUPS):
                mm = nc.tensor.matmul(env.ps[:, 3 + g // 2, (g % 2) * 256:(g % 2) * 256 + 256],
                                      m.pcT[:, g * P:(g + 1) * P], m.vbd[:, g, :], start=True, stop=True)
            mm.then_inc(self.o_ready, 1)

    def scalar(self, act, step):
        env, nc, m = self.env, self.env.nc, self.m
        for i in range(NT):
            act.wait_ge(self.shifted, i + 1)
            nc.scalar.activation(m.pc, m.sc, ACT.Exp).then_inc(self.p_ready, 1)
            act.wait_ge(self.o_ready, i + 1)
            nc.scalar.activation(m.o[:, i, :].rearrange("p (b n) -> p b n", b=2), env.ps[:, 3:5, :],
                                 ACT.Copy).then_inc(self.o_taken, 1)

    def vector(self, dve, step):
        env, nc, m = self.env, self.env.nc, self.m
        sc, pc = (v.rearrange("p (h c) -> p h c", c=NCP) for v in (m.sc, m.pc))
        col = m.cstat
        wide = lambda v: v.unsqueeze(2).to_broadcast([P, HEADS, NCP])
        for i in range(NT):
            dve.wait_ge(self.bias_ready, i + 1)
            nc.vector.tensor_copy(m.sc, env.ps[:, 6, :]).then_inc(self.bias_taken, 1)
            dve.wait_ge(self.bias_taken, i + 1)
            dve.wait_ge(self.s_ready, i + 1)
            for odd in range(2):
                part = m.sc.rearrange("p (h two c) -> p h two c", two=2, c=NCP)[:, :, odd, :]
                add = nc.vector.tensor_tensor(part, env.ps[:, 7 - 5 * odd, 0:256].rearrange("p (h c) -> p h c", c=NCP),
                                              part, ALU.add)
            add.then_inc(self.s_taken, 1)
            dve.wait_ge(self.s_taken, i + 1)
            step(nc.vector.tensor_reduce(col[:, 0, :], sc, AX, ALU.max))
            step(nc.vector.tensor_scalar(col[:, 0, :], col[:, 0, :], -1e20, None, ALU.max))
            nc.vector.tensor_tensor(sc, sc, wide(col[:, 0, :]), ALU.subtract).then_inc(self.shifted, 1)
            dve.wait_ge(self.p_ready, i + 1)
            step(nc.vector.tensor_reduce(col[:, 1, :], pc, AX, ALU.add))
            step(nc.vector.tensor_scalar(col[:, 1, :], col[:, 1, :], 1e-30, None, ALU.max))
            step(nc.vector.reciprocal(col[:, 2, :], col[:, 1, :]))
            gate = m.gate[:, i, :].rearrange("p (h b) -> p h b", b=3)[:, :, 0]
            step(nc.vector.tensor_tensor(col[:, 2, :], col[:, 2, :], gate, ALU.mult))
            nc.vector.tensor_tensor(pc, pc, wide(col[:, 2, :]), ALU.mult).then_inc(self.p_scaled, 1)
            dve.wait_ge(self.pT_ready, i + 1)
            nc.vector.tensor_copy(m.pcT, env.ps[:, 5, :]).then_inc(self.pT_taken, 1)


class Attend(Stage):

    def __init__(self, env, prefix):
        super().__init__(env)
        s = env.sem
        self.s_ready = s(prefix + "scores_ready")
        self.s_biased = s(prefix + "scores_biased")
        self.p_ready = s(prefix + "probs_ready")
        self.pT_ready = s(prefix + "probsT_ready")
        self.pT_copied = s(prefix + "probsT_copied")
        self.pv_done = s(prefix + "pv_done")
        self.o_taken = s(prefix + "o_taken")


class NsaAttend(Attend):

    def __init__(self, env, m):
        super().__init__(env, "nsa_")
        self.m = m
        self.units = [(i, g, br, j) for i in range(NT) for g in range(GROUPS) for br in range(2) for j in range(HPG)]

    def tensor(self, pe):
        env, nc, m = self.env, self.env.nc, self.m
        n_units = len(self.units)

        def scores(u):
            i, g, br, j = self.units[u]
            h = HPG * g + j
            half = 64 * (h % 2)
            if u >= 2:
                pe.wait_ge(self.s_biased, u - 1)
            nc.tensor.matmul(env.ps[:, u % 2, 0:P * (i + 1)], m.qT[half:half + 64, h // 2, i * P:(i + 1) * P],
                             (m.ksT, m.kwT)[br][half:half + 64, g, 0:P * (i + 1)],
                             start=True, stop=True).then_inc(self.s_ready, 1)

        def turn(u):
            i = self.units[u][0]
            pe.wait_ge(self.p_ready, u + 1)
            if u >= 2:
                pe.wait_ge(self.pT_copied, u - 1)
            for kt in range(i + 1):
                tr = nc.tensor.transpose(env.ps[:, 2 + u % 2, kt * P:(kt + 1) * P], m.p[:, u % 2, kt * P:(kt + 1) * P],
                                         env.ident)
            tr.then_inc(self.pT_ready, 1)

        def values(u):
            i, g, br, j = self.units[u]
            b = u // 8
            pe.wait_ge(self.pT_copied, u + 1)
            if u % 8 == 0 and b >= 2:
                pe.wait_ge(self.o_taken, b - 1)
            v = (m.vs, m.vw)[br]
            for kt in range(i + 1):
                mm = nc.tensor.matmul(env.ps[:, 4 + b % 2, (u % 8) * DH:(u % 8 + 1) * DH],
                                      m.pT[:, u % 2, kt * P:(kt + 1) * P], v[:, kt, g * DH:(g + 1) * DH],
                                      start=(kt == 0), stop=(kt == i))
            mm.then_inc(self.pv_done, 1)

        for u in range(n_units + 2):
            if u < n_units:
                scores(u)
            if 1 <= u <= n_units:
                turn(u - 1)
            if u >= 2:
                values(u - 2)

    def scalar(self, act, step):
        env, nc, m = self.env, self.env.nc, self.m
        for u, (i, g, br, j) in enumerate(self.units):
            n, b = P * (i + 1), u // 8
            act.wait_ge(self.s_biased, u + 1)
            if u >= 2:
                act.wait_ge(self.pT_ready, u - 1)
            if u % 8 == 0 and b >= 2:
                act.wait_ge(self.o_taken, b - 1)
            nc.scalar.activation(m.p[:, u % 2, 0:n], m.s[:, u % 2, 0:n], ACT.Exp, scale=-1.0,
                                 bias=m.nmax[:, u % 16:u % 16 + 1],
                                 accum_out=m.psum[:, u % 16:u % 16 + 1]).then_inc(self.p_ready, 1)

    def vector(self, dve, step):
        env, nc, m = self.env, self.env.nc, self.m
        n_units = len(self.units)

        def bias(u):
            i, g, br, j = self.units[u]
            n = P * (i + 1)
            dve.wait_ge(self.s_ready, u + 1)
            if u >= 2:
                dve.wait_ge(self.p_ready, u - 1)
            nc.vector.tensor_tensor_reduce(m.s[:, u % 2, 0:n], env.ps[:, u % 2, 0:n], m.bias[:, HPG * g + j, T - n:T],
                                           -1.0, 1e38, ALU.add, ALU.min,
                                           m.nmax[:, u % 16:u % 16 + 1]).then_inc(self.s_biased, 1)

        def copy(u):
            n = P * (self.units[u][0] + 1)
            dve.wait_ge(self.pT_ready, u + 1)
            if u >= 2:
                dve.wait_ge(self.pv_done, u - 1)
            nc.vector.tensor_copy(m.pT[:, u % 2, 0:n], env.ps[:, 2 + u % 2, 0:n]).then_inc(self.pT_copied, 1)

        def combine(b):
            i, g = b // GROUPS, b % GROUPS
            dve.wait_ge(self.pv_done, 8 * b + 8)
            at = 8 * (b % 2)
            step(nc.vector.reciprocal(m.scale[:, 0:8], m.psum[:, at:at + 8]))
            gate = m.gate[:, i, 12 * g:12 * g + 12].rearrange("p (j b) -> p b j", b=3)[:, 1:3, :]
            sc = m.scale[:, 0:8].rearrange("p (b j) -> p b j", b=2)
            step(nc.vector.tensor_tensor(sc, sc, gate, ALU.mult))
            step(nc.vector.tensor_tensor(m.otmp.rearrange("p (u d) -> p u d", d=DH),
                                         env.ps[:, 4 + b % 2, :].rearrange("p (u d) -> p u d", d=DH),
                                         m.scale[:, 0:8].unsqueeze(2).to_broadcast([P, 8, DH]), ALU.mult))
            o = m.o[:, i, 256 * g:256 * g + 256]
            step(nc.vector.tensor_tensor(o, o, m.otmp[:, 0:256], ALU.add))
            nc.vector.tensor_tensor(o, o, m.otmp[:, 256:512], ALU.add).then_inc(self.o_taken, 1)
            dve.wait_ge(self.o_taken, b + 1)

        for u in range(n_units + 4):
            if u < n_units:
                bias(u)
            if 1 <= u <= n_units:
                copy(u - 1)
            if u >= 11 and (u - 3) % 8 == 0:
                combine((u - 3) // 8 - 1)


class NsaMemory:
    def __init__(self, env, bias, setup):
        at = env.area

        def take(*shape):
            nonlocal at
            v = env.take(*shape, at=at)
            at += int(np.prod(shape))
            return v
        self.bias = bias
        self.hot, self.table3 = setup.hot, setup.table3
        self.qT = take(KD, T)
        self.ksT, self.kwT = take(GROUPS, T), take(GROUPS, T)
        self.vs, self.vw = take(NT, 256), take(NT, 256)
        w1_at = at
        self.w1 = [take(CMP_K, P), take(CMP_K, P)]
        end = at
        at = w1_at
        self.s, self.p, self.pT = take(2, 512), take(2, 512), take(2, 512)
        self.otmp = take(512)
        at = end
        self.sc, self.pc = take(512), take(512)
        self.pcT = take(512)
        self.vbd = take(GROUPS, 256)
        self.kcmp = take(GROUPS, NCP)
        self.hid = take(2, P)
        self.w2 = take(192)
        self.pe_rows = take(2, P)
        self.pe_cols = take(2 * CMP_K)
        self.hid_bias = take(4)
        self.gate = take(NT, 3 * HEADS)
        self.cstat = take(3, HEADS)
        self.nmax, self.psum, self.scale = take(16), take(16), take(16)
        assert at <= env.words - HEADS * T, at
        self.kcT = env.big[:, 0:2048].rearrange("p (g t) -> p g t", g=GROUPS)
        self.vcT = env.big[:, 2048:4096].rearrange("p (g t) -> p g t", g=GROUPS)
        self.o = env.big.rearrange("p (t d) -> p t d", t=NT)


class Area:

    def __init__(self, env, at=None):
        self.env, self.at = env, env.area if at is None else at

    def __call__(self, *shape):
        v = self.env.take(*shape, at=self.at)
        self.at += int(np.prod(shape))
        return v


class DiffMemory:
    def __init__(self, env, bias):
        take = Area(env)
        self.bias = bias
        self.qT, self.kT, self.v = take(KD, T), take(KD, T), take(NT, D)
        self.s, self.p, self.pT = take(4, 512), take(4, 512), take(2, 512)
        self.lq = take(4, DH)
        self.lprod = take(DH)
        self.dots, self.exps, self.lam = take(2), take(2), take(1)
        self.nmax, self.psum, self.scale = take(4), take(8), take(4)
        self.nstat = take(2, DIFF_HEADS)
        assert take.at <= env.words - HEADS * T, take.at
        self.o = env.big.rearrange("p (t d) -> p t d", t=NT)
        self.sq = take.env.take(D, at=env.area + 3 * 4096)


class DiffProject(Stage):

    def __init__(self, env, m):
        super().__init__(env)
        self.m = m
        self.lds, self.gs = [], []
        for n in range(6):
            self.lds.append(env.load((0, KD, 512, w_cols(env.io["diff_w_in"][0], 512 * n, 512))))
            self.gs.append(env.group(4))
            env.release(self.lds[-1], env.proj_ready, env.groups)
        self.lq_arrived = env.sem("lq_arrived")
        self.dots_ready, self.exps_ready = env.sem("lambda_dots"), env.sem("lambda_exps")

    def gpsimd(self, pool, step):
        for n, name in enumerate(("q1", "k1", "q2", "k2")):
            pool.dma_start(self.m.lq[:, n, :],
                           self.env.io["diff_lambda_" + name][0].partition_broadcast(P)).then_inc(self.lq_arrived, 16)

    def tensor(self, pe):
        env = self.env
        for n in range(6):
            env.wait_load(pe, self.lds[n])
            for j in range(4):
                if n < 4:
                    project_features(env, pe, self.lds[n], j * P, env.uT, self.gs[n] + j)
                else:
                    project_tokens(env, pe, self.lds[n], 0, 512, env.uT, j, self.gs[n] + j)

    def scalar(self, act, step):
        env, nc, m = self.env, self.env.nc, self.m
        for n in range(6):
            for j in range(4):
                g = self.gs[n] + j
                act.wait_ge(env.proj_ready, g + 1)
                dst = (m.qT, m.kT)[n // 2][:, 4 * (n % 2) + j, :] if n < 4 else m.v[:, j, 512 * (n - 4):512 * (n - 3)]
                nc.scalar.activation(dst, env.bank(g), ACT.Copy,
                                     scale=DH ** -0.5 if n < 2 else 1.0).then_inc(env.proj_taken, 1)
        act.wait_ge(self.dots_ready, 1)
        nc.scalar.activation(m.exps, m.dots, ACT.Exp).then_inc(self.exps_ready, 1)

    def vector(self, dve, step):
        nc, m = self.env.nc, self.m
        dve.wait_ge(self.lq_arrived, 64)
        step(nc.vector.tensor_tensor_reduce(m.lprod, m.lq[:, 0, :], m.lq[:, 1, :], 1.0, 0.0, ALU.mult, ALU.add,
                                            m.dots[:, 0:1]))
        nc.vector.tensor_tensor_reduce(m.lprod, m.lq[:, 2, :], m.lq[:, 3, :], 1.0, 0.0, ALU.mult, ALU.add,
                                       m.dots[:, 1:2]).then_inc(self.dots_ready, 1)
        dve.wait_ge(self.exps_ready, 1)
        step(nc.vector.tensor_tensor(m.lam, m.exps[:, 1:2], m.exps[:, 0:1], ALU.subtract))
        step(nc.vector.tensor_scalar(m.lam, m.lam, -LAMBDA_INIT, None, ALU.add))


class DiffAttend(Attend):

    def __init__(self, env, m):
        super().__init__(env, "diff_")
        self.m = m
        self.a_ready = env.sem("diff_combined")
        self.units = [(i, h) for i in range(NT) for h in range(DIFF_HEADS)]

    def tensor(self, pe):
        env, nc, m = self.env, self.env.nc, self.m
        n_units = len(self.units)

        def scores(u):
            i, h = self.units[u]
            if u >= 2:
                pe.wait_ge(self.s_biased, 2 * (u - 1))
            for mp in range(2):
                q = slice(64 * mp, 64 * mp + 64)
                nc.tensor.matmul(env.ps[:, 2 * (u % 2) + mp, 0:P * (i + 1)], m.qT[q, h, i * P:(i + 1) * P],
                                 m.kT[q, h, 0:P * (i + 1)], start=True, stop=True).then_inc(self.s_ready, 1)

        def turn(u):
            i = self.units[u][0]
            pe.wait_ge(self.a_ready, u + 1)
            if u >= 2:
                pe.wait_ge(self.pT_copied, u - 1)
            for kt in range(i + 1):
                tr = nc.tensor.transpose(env.ps[:, 4 + u % 2, kt * P:(kt + 1) * P],
                                         m.p[:, 2 * (u % 2), kt * P:(kt + 1) * P], env.ident)
            tr.then_inc(self.pT_ready, 1)

        def values(u):
            i, h = self.units[u]
            b = u // 4
            pe.wait_ge(self.pT_copied, u + 1)
            if u % 4 == 0 and b >= 2:
                pe.wait_ge(self.o_taken, b - 1)
            for kt in range(i + 1):
                mm = nc.tensor.matmul(env.ps[:, 6 + b % 2, (u % 4) * P:(u % 4 + 1) * P],
                                      m.pT[:, u % 2, kt * P:(kt + 1) * P], m.v[:, kt, h * P:(h + 1) * P],
                                      start=(kt == 0), stop=(kt == i))
            mm.then_inc(self.pv_done, 1)

        for u in range(n_units + 2):
            if u < n_units:
                scores(u)
            if 1 <= u <= n_units:
                turn(u - 1)
            if u >= 2:
                values(u - 2)

    def scalar(self, act, step):
        env, nc, m = self.env, self.env.nc, self.m
        n_units = len(self.units)

        def exps(u):
            n = P * (self.units[u][0] + 1)
            if u >= 2:
                act.wait_ge(self.pT_ready, u - 1)
            for mp in range(2):
                act.wait_ge(self.s_biased, 2 * u + mp + 1)
                at = 2 * (u % 2) + mp
                nc.scalar.activation(m.p[:, at, 0:n], m.s[:, at, 0:n], ACT.Exp, scale=-1.0, bias=m.nmax[:, at:at + 1],
                                     accum_out=m.psum[:, at:at + 1]).then_inc(self.p_ready, 1)

        def copy(u):
            n = P * (self.units[u][0] + 1)
            act.wait_ge(self.pT_ready, u + 1)
            if u >= 2:
                act.wait_ge(self.pv_done, u - 1)
            nc.scalar.activation(m.pT[:, u % 2, 0:n], env.ps[:, 4 + u % 2, 0:n], ACT.Copy).then_inc(self.pT_copied, 1)

        def take(b):
            act.wait_ge(self.pv_done, 4 * b + 4)
            nc.scalar.activation(m.o[:, b // 2, 512 * (b % 2):512 * (b % 2) + 512], env.ps[:, 6 + b % 2, :],
                                 ACT.Copy).then_inc(self.o_taken, 1)

        for u in range(n_units + 3):
            if u < n_units:
                exps(u)
            if 1 <= u <= n_units:
                copy(u - 1)
            if u >= 6 and (u - 2) % 4 == 0:
                take((u - 2) // 4 - 1)

    def vector(self, dve, step):
        env, nc, m = self.env, self.env.nc, self.m
        n_units = len(self.units)

        def bias(u):
            i, h = self.units[u]
            n = P * (i + 1)
            for mp in range(2):
                at = 2 * (u % 2) + mp
                dve.wait_ge(self.s_ready, 2 * u + mp + 1)
                if u >= 2:
                    dve.wait_ge(self.p_ready, 2 * (u - 2) + mp + 1)
                nc.vector.tensor_tensor_reduce(m.s[:, at, 0:n], env.ps[:, at, 0:n], m.bias[:, 2 * h + mp, T - n:T],
                                               -1.0, 1e38, ALU.add, ALU.min,
                                               m.nmax[:, at:at + 1]).then_inc(self.s_biased, 1)

        def combine(u):
            n, at = P * (self.units[u][0] + 1), 2 * (u % 2)
            dve.wait_ge(self.p_ready, 2 * u + 2)
            r = m.scale[:, at:at + 2]
            step(nc.vector.reciprocal(r, m.psum[:, at:at + 2]))
            step(nc.vector.tensor_tensor(r[:, 1:2], r[:, 1:2], m.lam, ALU.mult))
            step(nc.vector.tensor_scalar(m.p[:, at + 1, 0:n], m.p[:, at + 1, 0:n], r[:, 1:2], None, ALU.mult))
            nc.vector.scalar_tensor_tensor(m.p[:, at, 0:n], m.p[:, at, 0:n], r[:, 0:1], m.p[:, at + 1, 0:n],
                                           ALU.mult, ALU.add).then_inc(self.a_ready, 1)

        for u in range(n_units + 1):
            if u < n_units:
                bias(u)
            if u >= 1:
                combine(u - 1)


class DiffNorm(Stage):

    def __init__(self, env, m):
        super().__init__(env)
        self.m = m
        self.row_arrived = env.sem("subln_arrived")
        self.ms_ready, self.rstd_ready = env.sem("subln_ms"), env.sem("subln_rstd")

    def gpsimd(self, pool, step):
        env = self.env
        pool.dma_start(env.grow, env.io["diff_subln"][0].partition_broadcast(P)).then_inc(self.row_arrived, 16)

    def scalar(self, act, step):
        nc, m = self.env.nc, self.m
        for i in range(NT):
            act.wait_ge(self.ms_ready, i + 1)
            nc.scalar.activation(m.nstat[:, 1, :], m.nstat[:, 0, :], ACT.Sqrt).then_inc(self.rstd_ready, 1)

    def vector(self, dve, step):
        env, nc, m = self.env, self.env.nc, self.m
        c2 = (1.0 - LAMBDA_INIT) ** 2
        wide = m.nstat[:, 1, :].unsqueeze(2).to_broadcast([P, DIFF_HEADS, P])
        dve.wait_ge(self.row_arrived, 16)
        for i in range(NT):
            o = m.o[:, i, :]
            step(nc.vector.tensor_tensor(m.sq, o, o, ALU.mult))
            step(nc.vector.tensor_reduce(m.nstat[:, 0, :], m.sq.rearrange("p (h d) -> p h d", d=P), AX, ALU.add))
            step(nc.vector.tensor_scalar(m.nstat[:, 0, :], m.nstat[:, 0, :], 1.0 / (P * c2), EPS / c2, ALU.mult, ALU.add))
            nc.vector.reciprocal(m.nstat[:, 0, :], m.nstat[:, 0, :]).then_inc(self.ms_ready, 1)
            dve.wait_ge(self.rstd_ready, i + 1)
            step(nc.vector.tensor_tensor(o.rearrange("p (h d) -> p h d", d=P), o.rearrange("p (h d) -> p h d", d=P),
                                         wide, ALU.mult))
            step(nc.vector.tensor_tensor(o, o, env.grow, ALU.mult))


class FfnUp(Stage):

    def __init__(self, env, layer, m):
        super().__init__(env)
        self.layer, self.m = layer, m
        w = env.io["w_up_2"][layer]
        self.lds = []
        self.g0 = env.groups
        for j in range(0, FT, 2):
            self.lds.append(env.load((0, KD, 256, w_cols(w, j * P, 256)), (2048, KD, 256, w_cols(w, D_FF + j * P, 256))))
            env.group(4)
            env.release(self.lds[-1], env.proj_ready, env.groups)
        n = str(layer)
        self.scaled = env.sem("up_scaled" + n)
        self.gelu_done, self.act_done = env.sem("gelu_done" + n), env.sem("act_done" + n)

    def tensor(self, pe):
        env = self.env
        for n, ld in enumerate(self.lds):
            env.wait_load(pe, ld)
            for j in range(2):
                for half in range(2):
                    g = self.g0 + 4 * n + 2 * j + half
                    w = env.slot(ld, KD, 256, 2048 * half)
                    env.wait_bank(pe, g)
                    for k in range(KD):
                        mm = env.nc.tensor.matmul(env.bank(g), w[:, k, j * P:(j + 1) * P], env.uT[:, k, :],
                                                  start=(k == 0), stop=(k == KD - 1))
                    mm.then_inc(env.proj_ready, 1)

    def col(self, which, half, j):
        at = V_CONV + 176 * self.layer + 44 * which + FT * half + j
        return self.env.vec[:, at:at + 1]

    def scalar(self, act, step):
        env, nc, m = self.env, self.env.nc, self.m

        def gelu(j):
            act.wait_ge(env.proj_taken, self.g0 + 2 * j + 2)
            if j >= 2:
                act.wait_ge(self.act_done, j - 1)
            nc.scalar.activation(m.gelu[:, j % 2, :], m.conv[:, 2 * (j % 2), :], ACT.Gelu_apprx_tanh).then_inc(self.gelu_done, 1)

        for j in range(FT):
            for half in range(2):
                g = self.g0 + 2 * j + half
                act.wait_ge(env.proj_ready, g + 1)
                if j >= 2:
                    act.wait_ge(self.act_done, j - 1)
                nc.scalar.activation(m.conv[:, 2 * (j % 2) + half, :], env.bank(g), ACT.Identity,
                                     scale=self.col(2, half, j), bias=self.col(3, half, j)).then_inc(self.scaled, 1)
            if j:
                gelu(j - 1)
        gelu(FT - 1)

    def vector(self, dve, step):
        env, nc, m = self.env, self.env.nc, self.m

        def multiply(j):
            dve.wait_ge(self.gelu_done, j + 1)
            dve.wait_ge(env.proj_taken, self.g0 + 2 * j + 2)
            nc.vector.tensor_tensor(m.actT[:, j, :], m.gelu[:, j % 2, :], m.conv[:, 2 * (j % 2) + 1, :],
                                    ALU.mult).then_inc(self.act_done, 1)

        for j in range(FT):
            for half in range(2):
                g = self.g0 + 2 * j + half
                c = m.conv[:, 2 * (j % 2) + half, :]
                dve.wait_ge(self.scaled, 2 * j + half + 1)
                step(nc.vector.scalar_tensor_tensor(c[:, 1:T], env.bank(g)[:, 0:T - 1], self.col(1, half, j), c[:, 1:T],
                                                    ALU.mult, ALU.add))
                nc.vector.scalar_tensor_tensor(c[:, 2:T], env.bank(g)[:, 0:T - 2], self.col(0, half, j), c[:, 2:T],
                                               ALU.mult, ALU.add).then_inc(env.proj_taken, 1)
            if j:
                multiply(j - 1)
        multiply(FT - 1)


class FfnMemory:
    def __init__(self, env):
        take = Area(env)
        self.actT = take(FT, T)
        self.conv, self.gelu = take(4, 512), take(2, 512)


class SwaMemory:
    def __init__(self, env):
        take = Area(env)
        self.kT, self.v = take(GROUPS, T), take(NT, 256)
        self.qT = take(KD, T)
        self.s, self.p, self.pT = take(2, 256), take(2, 256), take(2, 256)
        self.sinks, self.nsinks = take(HEADS), take(HEADS)
        self.nmax, self.psum, self.esink, self.scale = take(16), take(16), take(16), take(16)
        self.o = env.big.rearrange("p (t d) -> p t d", t=NT)


class KvProject(Stage):
    def __init__(self, env, m):
        super().__init__(env)
        self.m = m
        self.ld = env.load((0, KD, 512, w_cols(env.io["w_kv_2"], 0, 512)))
        self.g0 = env.group(6)
        env.release(self.ld, env.proj_ready, env.groups)

    def tensor(self, pe):
        env = self.env
        env.wait_load(pe, self.ld)
        for j in range(2):
            project_features(env, pe, self.ld, j * P, env.uT, self.g0 + j)
        for i in range(NT):
            project_tokens(env, pe, self.ld, 256, 256, env.uT, i, self.g0 + 2 + i)

    def scalar(self, act, step):
        env, nc, m = self.env, self.env.nc, self.m
        for j in range(2):
            g = self.g0 + j
            act.wait_ge(env.proj_ready, g + 1)
            for half in range(2):
                for to in range(2):
                    cp = nc.scalar.activation(m.kT[64 * to:64 * to + 64, 2 * j + half, :],
                                              env.bank(g)[64 * half:64 * half + 64, :], ACT.Copy)
            cp.then_inc(env.proj_taken, 1)
        for i in range(NT):
            g = self.g0 + 2 + i
            act.wait_ge(env.proj_ready, g + 1)
            nc.scalar.activation(m.v[:, i, :], env.bank(g)[:, 0:256], ACT.Copy).then_inc(env.proj_taken, 1)


class SwaProject(Stage):
    def __init__(self, env, m):
        super().__init__(env)
        self.m = m
        self.lds, self.gs = [], []
        for n in range(2):
            self.lds.append(env.load((0, KD, 512, w_cols(env.io["w_q_2"][0], 512 * n, 512))))
            self.gs.append(env.group(4))
            env.release(self.lds[-1], env.proj_ready, env.groups)
        self.sinks_arrived = env.sem("sinks_arrived")

    def gpsimd(self, pool, step):
        pool.dma_start(self.m.sinks, self.env.io["sinks_2"][0].partition_broadcast(P)).then_inc(self.sinks_arrived, 16)

    def tensor(self, pe):
        env = self.env
        for n in range(2):
            env.wait_load(pe, self.lds[n])
            for j in range(4):
                project_features(env, pe, self.lds[n], j * P, env.uT, self.gs[n] + j)

    def scalar(self, act, step):
        env, nc = self.env, self.env.nc
        for n in range(2):
            for j in range(4):
                g = self.gs[n] + j
                act.wait_ge(env.proj_ready, g + 1)
                nc.scalar.activation(self.m.qT[:, 4 * n + j, :], env.bank(g), ACT.Copy,
                                     scale=DH ** -0.5).then_inc(env.proj_taken, 1)

    def vector(self, dve, step):
        dve.wait_ge(self.sinks_arrived, 16)
        step(self.env.nc.vector.tensor_scalar(self.m.nsinks, self.m.sinks, -1.0, None, ALU.mult))


class SwaAttend(Attend):

    def __init__(self, env, m):
        super().__init__(env, "swa_")
        self.m = m
        self.esum_ready, self.esink_ready = env.sem("sink_shifted"), env.sem("sink_exp")
        self.units = [(i, h) for i in range(NT) for h in range(HEADS)]

    def tensor(self, pe):
        env, nc, m = self.env, self.env.nc, self.m
        n_units = len(self.units)

        def scores(u):
            i, h = self.units[u]
            half, lo = 64 * (h % 2), max(i - 1, 0)
            if u >= 2:
                pe.wait_ge(self.s_biased, u - 1)
            nc.tensor.matmul(env.ps[:, u % 2, 0:P * (i + 1 - lo)], m.qT[half:half + 64, h // 2, i * P:(i + 1) * P],
                             m.kT[half:half + 64, h // HPG, P * lo:P * (i + 1)],
                             start=True, stop=True).then_inc(self.s_ready, 1)

        def turn(u):
            i = self.units[u][0]
            pe.wait_ge(self.p_ready, u + 1)
            if u >= 2:
                pe.wait_ge(self.pT_copied, u - 1)
            for kt in range(1 + (i > 0)):
                tr = nc.tensor.transpose(env.ps[:, 2 + u % 2, kt * P:(kt + 1) * P], m.p[:, u % 2, kt * P:(kt + 1) * P],
                                         env.ident)
            tr.then_inc(self.pT_ready, 1)

        def values(u):
            i, h = self.units[u]
            b, g, lo = u // 8, h // HPG, max(i - 1, 0)
            pe.wait_ge(self.pT_copied, u + 1)
            if u % 8 == 0 and b >= 2:
                pe.wait_ge(self.o_taken, b - 1)
            for kt in range(lo, i + 1):
                mm = nc.tensor.matmul(env.ps[:, 4 + b % 2, (u % 8) * DH:(u % 8 + 1) * DH],
                                      m.pT[:, u % 2, (kt - lo) * P:(kt - lo + 1) * P], m.v[:, kt, g * DH:(g + 1) * DH],
                                      start=(kt == lo), stop=(kt == i))
            mm.then_inc(self.pv_done, 1)

        for u in range(n_units + 2):
            if u < n_units:
                scores(u)
            if 1 <= u <= n_units:
                turn(u - 1)
            if u >= 2:
                values(u - 2)

    def scalar(self, act, step):
        env, nc, m = self.env, self.env.nc, self.m
        n_units = len(self.units)

        def exp(u):
            n, b = P * (1 + (self.units[u][0] > 0)), u // 8
            act.wait_ge(self.s_biased, u + 1)
            if u >= 2:
                act.wait_ge(self.pT_ready, u - 1)
            if u % 8 == 0 and b >= 2:
                act.wait_ge(self.o_taken, b - 1)
            nc.scalar.activation(m.p[:, u % 2, 0:n], m.s[:, u % 2, 0:n], ACT.Exp, scale=-1.0,
                                 bias=m.nmax[:, u % 16:u % 16 + 1],
                                 accum_out=m.psum[:, u % 16:u % 16 + 1]).then_inc(self.p_ready, 1)

        for u in range(n_units + 4):
            if u < n_units:
                exp(u)
            if u >= 11 and (u - 3) % 8 == 0:
                b = (u - 3) // 8 - 1
                at = 8 * (b % 2)
                act.wait_ge(self.esum_ready, b + 1)
                nc.scalar.activation(m.esink[:, at:at + 8], m.esink[:, at:at + 8], ACT.Exp).then_inc(self.esink_ready, 1)

    def vector(self, dve, step):
        env, nc, m = self.env, self.env.nc, self.m
        n_units = len(self.units)
        band = env.const[:, C_BAND:C_BAND + 2 * P]

        def bias(u):
            i, h = self.units[u]
            n = P * (1 + (i > 0))
            dve.wait_ge(self.s_ready, u + 1)
            if u >= 2:
                dve.wait_ge(self.p_ready, u - 1)
            nc.vector.tensor_tensor_reduce(m.s[:, u % 2, 0:n], env.ps[:, u % 2, 0:n], band[:, 2 * P - n:2 * P],
                                           -1.0, m.nsinks[:, h:h + 1], ALU.add, ALU.min,
                                           m.nmax[:, u % 16:u % 16 + 1]).then_inc(self.s_biased, 1)

        def copy(u):
            n = P * (1 + (self.units[u][0] > 0))
            dve.wait_ge(self.pT_ready, u + 1)
            if u >= 2:
                dve.wait_ge(self.pv_done, u - 1)
            nc.vector.tensor_copy(m.pT[:, u % 2, 0:n], env.ps[:, 2 + u % 2, 0:n]).then_inc(self.pT_copied, 1)

        def combine(b):
            at, h0 = 8 * (b % 2), 8 * (b % 2)
            dve.wait_ge(self.s_biased, 8 * b + 8)
            nc.vector.tensor_tensor(m.esink[:, at:at + 8], m.nmax[:, at:at + 8], m.sinks[:, h0:h0 + 8],
                                    ALU.add).then_inc(self.esum_ready, 1)
            dve.wait_ge(self.esink_ready, b + 1)
            step(nc.vector.tensor_tensor(m.scale[:, at:at + 8], m.psum[:, at:at + 8], m.esink[:, at:at + 8], ALU.add))
            step(nc.vector.reciprocal(m.scale[:, at:at + 8], m.scale[:, at:at + 8]))
            dve.wait_ge(self.pv_done, 8 * b + 8)
            nc.vector.tensor_tensor(m.o[:, b // 2, 512 * (b % 2):512 * (b % 2) + 512].rearrange("p (u d) -> p u d", d=DH),
                                    env.ps[:, 4 + b % 2, :].rearrange("p (u d) -> p u d", d=DH),
                                    m.scale[:, at:at + 8].unsqueeze(2).to_broadcast([P, 8, DH]),
                                    ALU.mult).then_inc(self.o_taken, 1)

        for u in range(n_units + 4):
            if u < n_units:
                bias(u)
            if 1 <= u <= n_units:
                copy(u - 1)
            if u >= 11 and (u - 3) % 8 == 0:
                combine((u - 3) // 8 - 1)


class RwkvMemory:

    def __init__(self, env):
        take = Area(env)
        self.r, self.k, self.a, self.kk = take(KD, T), take(KD, T), take(KD, T), take(KD, T)
        self.v = take(NT, D)
        l_at = take.at
        self.decay = take(KD, T)
        self.xx = self.decay
        self.v_T = self.v.rearrange("p t (k c) -> p (t k) c", c=T)
        behind = take.at
        self.tanh_w, self.hid_a = self.kk[:, 0, :], self.kk[:, 1, :]
        self.mixes = [self.v_T, env.big.rearrange("p (k c) -> p k c", c=T)]
        core1 = Area(env, l_at)
        u_at = 4096
        core0 = Area(env, u_at)
        self.streams = []
        for take in (core0, core1):
            st = {}
            for name in ("abT", "X", "XT", "Y", "akT", "rbT", "rkT"):
                st[name] = take(4, P)
            st["MT"] = [take(4, P), take(4, P)]
            st["Z"], st["SA"] = take(4, DH), take(4, DH)
            self.streams.append(st)
        self.tok = core0(3, 4, P)
        self.WT = core0(4, P)
        self.S = core0(KD, DH)
        assert core0.at <= u_at + 8192, core0.at
        take = Area(env, core1.at)
        self.sg = take(2, T)
        take = Area(env, env.stat_at + 64)
        self.coef = take(KD, NT)
        self.bonus = take(NT, RH)
        self.mid, self.epos = take(KD, NT), take(KD, NT)
        w = Area(env, u_at)
        self.w = [[w(T) for _ in range(7)] for _ in range(2)]
        self.gn = self.r.rearrange("p k t -> p (k t)")[:, 0:2 * D].rearrange("p (a d) -> p a d", a=2)
        self.tmp = self.k.rearrange("p k t -> p (k t)")[:, 0:D]
        self.mean, self.var = self.mid.rearrange("p a b -> p (a b)")[:, 0:RH], \
            self.mid.rearrange("p a b -> p (a b)")[:, RH:2 * RH]
        self.grstd = self.epos.rearrange("p a b -> p (a b)")[:, 0:RH]
        self.o = env.big.rearrange("p (t d) -> p t d", t=NT)


class RwkvProject(Stage):

    MIXES = [("k", 2), ("r", 0), ("w", 1), ("a", 4), ("g", 5), ("v", 3)]

    def __init__(self, env, m):
        super().__init__(env)
        self.m = m
        io = env.io
        self.lds, self.gs = {}, {}

        def big(name, i):
            for n in range(2):
                self.lds[name, n] = env.load((0, KD, 512, w_cols(io["w_rkv_2"][0, i], 512 * n, 512)))
                self.gs[name, n] = env.group(4)
                env.release(self.lds[name, n], env.proj_ready, env.groups)
        big("k", 1)
        big("r", 0)
        self.lora = env.load((0, KD, 64, w_cols(io["w_decay1_2"][0], 0, 64)), (512, KD, 64, w_cols(io["a1_2"][0], 0, 64)),
                             (1024, KD, 160, w_cols(io["g1_2"][0], 0, 160)))
        self.gs["lora"] = env.group(4)
        env.release(self.lora, env.proj_ready, env.groups)
        big("v", 2)
        self.lora2 = env.load((0, 1, D, io["w_decay2_2"][0].unsqueeze(1)), (1024, 1, D, io["a2_2"][0].unsqueeze(1)))
        self.gs["lora2"] = env.group(16)
        env.release(self.lora2, env.proj_ready, env.groups)
        self.last = [self.gs["k", 1] + 4, self.gs["r", 1] + 4, self.gs["lora"] + 1, self.gs["lora"] + 2]
        self.xx_ready, self.mix_ready = env.sem("xx_ready"), env.sem("mix_ready")

    def vector(self, dve, step):
        env, nc, m = self.env, self.env.nc, self.m
        step(nc.vector.tensor_tensor(m.xx[:, :, 1:T], env.uT[:, :, 0:T - 1], env.uT[:, :, 1:T], ALU.subtract))
        step(nc.vector.tensor_scalar(m.xx[:, :, 0:1], env.uT[:, :, 0:1], -1.0, None, ALU.mult))
        for n, (_, i) in enumerate(self.MIXES):
            if n >= 2:
                dve.wait_ge(env.proj_ready, self.last[n - 2])
            for k in range(KD):
                at = V_MU + 8 * i + k
                nc.vector.scalar_tensor_tensor(m.mixes[n % 2][:, k, :], m.xx[:, k, :], env.vec[:, at:at + 1],
                                               env.uT[:, k, :], ALU.mult, ALU.add).then_inc(self.mix_ready, 1)

    def tensor(self, pe):
        env, nc, m = self.env, self.env.nc, self.m

        def hidden(n, c0, cols, first, width, g):
            w = env.slot(self.lora, KD, width, first)
            env.wait_bank(pe, g)
            for k in range(KD):
                mm = nc.tensor.matmul(env.bank(g)[0:cols], w[:, k, c0:c0 + cols], m.mixes[n % 2][:, k, :],
                                      start=(k == 0), stop=(k == KD - 1))
            mm.then_inc(env.proj_ready, 1)

        for n, (name, _) in enumerate(self.MIXES):
            pe.wait_ge(self.mix_ready, KD * (n + 1))
            if name in "krv":
                for half in range(2):
                    ld, g = self.lds[name, half], self.gs[name, half]
                    env.wait_load(pe, ld)
                    for j in range(4):
                        if name == "v":
                            project_tokens(env, pe, ld, 0, 512, m.mixes[n % 2], j, g + j)
                        else:
                            project_features(env, pe, ld, j * P, m.mixes[n % 2], g + j)
            else:
                env.wait_load(pe, self.lora)
                g = self.gs["lora"]
                if name == "w":
                    hidden(n, 0, 64, 0, 64, g)
                elif name == "a":
                    hidden(n, 0, 64, 512, 64, g + 1)
                else:
                    hidden(n, 0, P, 1024, 160, g + 2)
                    hidden(n, P, 32, 1024, 160, g + 3)
        env.wait_load(pe, self.lora2)
        g = self.gs["lora2"]
        pe.wait_ge(env.proj_taken, self.gs["lora"] + 2)
        for which, hid in enumerate((m.tanh_w, m.hid_a)):
            w = env.slot(self.lora2, 1, D, 1024 * which)
            for k in range(KD):
                gg = g + 8 * which + k
                env.wait_bank(pe, gg)
                nc.tensor.matmul(env.bank(gg), w[0:64, 0, k * P:(k + 1) * P], hid[0:64, :],
                                 start=True, stop=True).then_inc(env.proj_ready, 1)

    def scalar(self, act, step):
        env, nc, m = self.env, self.env.nc, self.m
        for name, dst in (("k", m.k), ("r", m.r)):
            for half in range(2):
                for j in range(4):
                    g = self.gs[name, half] + j
                    act.wait_ge(env.proj_ready, g + 1)
                    nc.scalar.activation(dst[:, 4 * half + j, :], env.bank(g), ACT.Copy).then_inc(env.proj_taken, 1)
        g = self.gs["lora"]
        act.wait_ge(env.proj_ready, g + 1)
        nc.scalar.activation(m.tanh_w[0:64, :], env.bank(g)[0:64, :], ACT.Tanh).then_inc(env.proj_taken, 1)
        act.wait_ge(env.proj_ready, g + 2)
        nc.scalar.activation(m.hid_a[0:64, :], env.bank(g + 1)[0:64, :], ACT.Copy).then_inc(env.proj_taken, 1)
        act.wait_ge(env.proj_ready, g + 3)
        nc.scalar.activation(m.sg[:, 0, :], env.bank(g + 2), ACT.Sigmoid).then_inc(env.proj_taken, 1)
        act.wait_ge(env.proj_ready, g + 4)
        nc.scalar.activation(m.sg[0:32, 1, :], env.bank(g + 3)[0:32, :], ACT.Sigmoid).then_inc(env.proj_taken, 1)
        for half in range(2):
            for j in range(4):
                g = self.gs["v", half] + j
                act.wait_ge(env.proj_ready, g + 1)
                nc.scalar.activation(m.v[:, j, 512 * half:512 * half + 512], env.bank(g), ACT.Copy).then_inc(env.proj_taken, 1)
        act.wait_ge(self.mix_ready, KD * 6)
        for which, (dst, col) in enumerate(((m.decay, V_B), (m.a, V_B + 8))):
            for k in range(KD):
                g = self.gs["lora2"] + 8 * which + k
                act.wait_ge(env.proj_ready, g + 1)
                nc.scalar.activation(dst[:, k, :], env.bank(g), ACT.Sigmoid,
                                     bias=env.vec[:, col + k:col + k + 1]).then_inc(env.proj_taken, 1)


class RwkvPrepare(Stage):

    def __init__(self, env, m):
        super().__init__(env)
        self.m = m
        s = env.sem
        self.sq_ready, self.ss_ready, self.inv_ready = s("kk_sq_ready"), s("kk_ss_ready"), s("kk_inv_ready")
        self.norm_ready, self.mid_ready, self.exps_ready = s("kk_norm_ready"), s("mid_ready"), s("exps_ready")
        self.rk_ready, self.tile_done = s("rk_ready"), s("prep_tile_done")
        self.bonus_ready = s("bonus_ready")

    def tensor(self, pe):
        env, nc, m = self.env, self.env.nc, self.m
        for k in range(KD):
            w = m.w[k % 2]
            pe.wait_ge(self.sq_ready, k + 1)
            nc.tensor.matmul(env.ps[:, k % 2, :], env.const[:, C_HEADSUM:C_HEADSUM + P], w[0],
                             start=True, stop=True).then_inc(self.ss_ready, 1)
            pe.wait_ge(self.rk_ready, k + 1)
            for i in range(NT):
                mm = nc.tensor.matmul(env.ps[:, 7, i * RH + 2 * k:i * RH + 2 * k + 2], w[1][:, i * P:(i + 1) * P],
                                      env.const[:, C_HEADSEL:C_HEADSEL + 2], start=True, stop=True)
            mm.then_inc(self.bonus_ready, 1)

    def scalar(self, act, step):
        env, nc, m = self.env, self.env.nc, self.m
        for k in range(KD):
            w = m.w[k % 2]
            act.wait_ge(self.inv_ready, k + 1)
            nc.scalar.activation(w[2], w[3], ACT.Sqrt).then_inc(self.norm_ready, 1)

    def vector(self, dve, step):
        env, nc, m = self.env, self.env.nc, self.m
        v = nc.vector
        ones = env.const[:, C_ONES:C_ONES + P]
        chunks = lambda x: x.rearrange("p (c t) -> p c t", c=NT)
        for k in range(KD):
            w = m.w[k % 2]
            col = lambda n: env.vec[:, V_B + 8 * n + k:V_B + 8 * n + k + 1]
            kk, kp, a, r = m.kk[:, k, :], m.k[:, k, :], m.a[:, k, :], m.r[:, k, :]
            if k >= 2:
                dve.wait_ge(self.bonus_ready, k - 1)
            step(v.tensor_scalar(kk, kp, col(2), None, ALU.mult))
            v.tensor_tensor(w[0], kk, kk, ALU.mult).then_inc(self.sq_ready, 1)
            step(v.tensor_scalar(w[6], a, 1.0, col(3), ALU.subtract, ALU.mult))
            step(v.scalar_tensor_tensor(kp, w[6], 1.0, kp, ALU.add, ALU.mult))
            v.scalar_tensor_tensor(w[1], r, col(4), kp, ALU.mult, ALU.mult).then_inc(self.rk_ready, 1)
            dve.wait_ge(self.ss_ready, k + 1)
            step(v.tensor_scalar(w[3], env.ps[:, k % 2, :], 1e-24, None, ALU.max))
            v.reciprocal(w[3], w[3]).then_inc(self.inv_ready, 1)
            for c in range(NT):
                last = v.tensor_tensor_scan(w[6][:, c * P:(c + 1) * P], ones, m.decay[:, k, c * P:(c + 1) * P], 0.0,
                                            ALU.mult, ALU.add)
                step(last)
            step(v.tensor_copy(m.mid[:, k, :], w[6][:, P // 2 - 1:T:P]))
            step(v.tensor_tensor(chunks(m.decay[:, k, :]), chunks(w[6]),
                                 m.mid[:, k, :].unsqueeze(2).to_broadcast([P, NT, P]), ALU.subtract))
            dve.wait_ge(self.norm_ready, k + 1)
            step(v.tensor_tensor(kk, kk, w[2], ALU.mult))
            v.tensor_tensor(a, a, kk, ALU.mult).then_inc(self.tile_done, 1)
        dve.wait_ge(self.tile_done, KD)
        dve.wait_ge(self.bonus_ready, KD)
        step(v.tensor_copy(m.bonus.rearrange("p a b -> p (a b)"), env.ps[:, 7, 0:NT * RH]))


class RwkvDecay(Stage):

    def __init__(self, env, m):
        super().__init__(env)
        self.m = m
        self.exps_ready, self.taken = env.sem("decay_exps_ready"), env.sem("decay_exps_taken")
        self.cols_ready = env.sem("decay_cols_ready")

    def scalar(self, act, step):
        env, nc, m = self.env, self.env.nc, self.m
        c = DECAY_SCALE
        step(nc.scalar.activation(m.coef, m.mid, ACT.Exp, scale=-c))
        nc.scalar.activation(m.epos, m.mid, ACT.Exp, scale=c).then_inc(self.cols_ready, 1)
        for k in range(KD):
            w = m.w[k % 2]
            if k >= 2:
                act.wait_ge(self.taken, k - 1)
            nc.scalar.activation(w[0], m.decay[:, k, :], ACT.Exp, scale=-c)
            nc.scalar.activation(w[1], m.decay[:, k, :], ACT.Exp, scale=c).then_inc(self.exps_ready, 1)

    def vector(self, dve, step):
        env, nc, m = self.env, self.env.nc, self.m
        v = nc.vector
        chunks = lambda x: x.rearrange("p (c t) -> p c t", c=NT)
        dve.wait_ge(self.cols_ready, 1)
        for k in range(KD):
            w = m.w[k % 2]
            kk = chunks(m.kk[:, k, :])
            e = chunks(w[0])
            dve.wait_ge(self.exps_ready, k + 1)
            v.tensor_tensor(m.r[:, k, :], m.r[:, k, :], w[0], ALU.mult)
            v.tensor_tensor(m.a[:, k, :], m.a[:, k, :], w[1], ALU.mult)
            v.tensor_tensor(m.k[:, k, :], m.k[:, k, :], w[1], ALU.mult)
            v.scalar_tensor_tensor(kk[:, :, 1:P], kk[:, :, 1:P], -1.0, e[:, :, 0:P - 1], ALU.mult, ALU.mult)
            v.scalar_tensor_tensor(kk[:, :, 0], kk[:, :, 0], -1.0, m.epos[:, k, :], ALU.mult, ALU.mult)
            v.tensor_tensor(m.coef[:, k, 1:NT], m.coef[:, k, 1:NT], e[:, 0:NT - 1, P - 1],
                            ALU.mult).then_inc(self.taken, 1)


class RwkvCore(Stage):

    STEPS = [(c, q) for c in range(NT) for q in range(2)]

    def __init__(self, env, m):
        super().__init__(env)
        self.m = m
        s = env.sem
        self.ready = {"A": s("core_act_ready"), "D": s("core_dve_ready")}
        self.taken = {"A": s("core_act_taken"), "D": s("core_dve_taken")}
        self.part_ready = s("level_part_ready")
        self.start_ready = s("start_ready")
        self.num, count = {}, {"A": 0, "D": 0}

        def put(engine, *key):
            self.num[key] = (engine, count[engine])
            count[engine] += 1
        for w in range(len(self.STEPS)):
            for arr in range(3):
                put("A", w, "tok", arr)
            for st in range(2):
                for name in ("abT", "ab", "akT", "rbT", "rkT"):
                    put("D", w, name, st)
            for st in range(2):
                put("A", w, "Z", st)
            for lv in range(1, LEVELS):
                for st in range(2):
                    put("A", w, "Y", lv, st)
                for st in range(2):
                    if lv < LEVELS - 1:
                        put("D", w, "X", lv, st)
                    put("D", w, "XT", lv, st)
            for st in range(2):
                put("A", w, "WT", st)
            for st in range(2):
                put("A", w, "SA", st)
            for st in range(2):
                put("A", w, "y", st)
            for st in range(2):
                put("D", w, "S", st)

    def bank(self, *key):
        engine, n = self.num[key]
        return self.env.ps[:, n % 4 + (4 if engine == "D" else 0), :]

    def wait_ready(self, eng, *key):
        engine, n = self.num[key]
        eng.wait_ge(self.ready[engine], n + 1)

    def wait_taken(self, eng, *key):
        engine, n = self.num[key]
        eng.wait_ge(self.taken[engine], n + 1)

    def tensor(self, pe):
        env, nc, m = self.env, self.env.nc, self.m
        mmul = nc.tensor.matmul

        def free(*key):
            engine, n = self.num[key]
            if n >= 4:
                pe.wait_ge(self.taken[engine], n - 3)

        def done(ins, *key):
            ins.then_inc(self.ready[self.num[key][0]], 1)

        def cols(key, e, n=P):
            return self.bank(*key)[:, e * n:(e + 1) * n]

        for w, (c, q) in enumerate(self.STEPS):
            tok = slice(c * P, (c + 1) * P)
            for arr, src in enumerate((m.kk, m.a, m.k)):
                key = (w, "tok", arr)
                free(*key)
                for e in range(4):
                    mm = nc.tensor.transpose(cols(key, e), src[:, 4 * q + e, tok], env.ident)
                done(mm, *key)
            for st in range(2):
                half = slice(64 * st, 64 * st + 64)
                for name, lhs, rhs in (("abT", m.a, m.kk), ("ab", m.kk, m.a), ("akT", m.k, m.kk), ("rbT", m.a, m.r),
                                       ("rkT", m.k, m.r)):
                    key = (w, name, st)
                    free(*key)
                    for e in range(4):
                        mm = mmul(cols(key, e), lhs[half, 4 * q + e, tok], rhs[half, 4 * q + e, tok],
                                  start=True, stop=True)
                    done(mm, *key)
            for st in range(2):
                key = (w, "Z", st)
                self.wait_taken(pe, w, "akT", st)
                free(*key)
                for e in range(4):
                    h = 2 * (4 * q + e) + st
                    mm = mmul(cols(key, e, DH), m.streams[st]["akT"][:, e, :], m.v[:, c, h * DH:(h + 1) * DH],
                              start=True, stop=True)
                done(mm, *key)
            for lv in range(1, LEVELS):
                for st in range(2):
                    s = m.streams[st]
                    key = (w, "Y", lv, st)
                    pe.wait_ge(self.part_ready, 12 * w + 2 * (lv - 1) + st + 1)
                    if lv == 1:
                        pe.wait_ge(self.start_ready, 2 * w + st + 1)
                    else:
                        self.wait_taken(pe, w, "XT", lv - 1, st)
                    free(*key)
                    for e in range(4):
                        mm = mmul(cols(key, e), s["MT"][lv % 2][:, e, :], s["X"][:, e, :], start=True, stop=True)
                    done(mm, *key)
                for st in range(2):
                    s = m.streams[st]
                    self.wait_taken(pe, w, "Y", lv, st)
                    if lv < LEVELS - 1:
                        key = (w, "X", lv, st)
                        free(*key)
                        for e in range(4):
                            mm = mmul(cols(key, e), s["XT"][:, e, :], s["Y"][:, e, :], start=True, stop=True)
                        done(mm, *key)
                    key = (w, "XT", lv, st)
                    free(*key)
                    for e in range(4):
                        mm = mmul(cols(key, e), s["Y"][:, e, :], s["XT"][:, e, :], start=True, stop=True)
                    done(mm, *key)
            for st in range(2):
                half = slice(64 * st, 64 * st + 64)
                key = (w, "WT", st)
                self.wait_taken(pe, w, "XT", LEVELS - 1, st)
                self.wait_taken(pe, w, "tok", 0)
                free(*key)
                for e in range(4):
                    mm = mmul(cols(key, e)[half], m.tok[:, 0, e, half], m.streams[st]["XT"][:, e, :],
                              start=True, stop=True)
                done(mm, *key)
            for st in range(2):
                half = slice(64 * st, 64 * st + 64)
                key = (w, "SA", st)
                self.wait_taken(pe, w, "Z", st)
                self.wait_taken(pe, w, "WT", st)
                if w >= 2:
                    self.wait_taken(pe, w - 2, "S", st)
                free(*key)
                for e in range(4):
                    mm = mmul(cols(key, e, DH), m.streams[st]["XT"][:, e, :], m.streams[st]["Z"][:, e, :],
                              start=True, stop=(c == 0))
                    if c:
                        mm = mmul(cols(key, e, DH), m.WT[half, e, :], m.S[half, 4 * q + e, :], start=False, stop=True)
                done(mm, *key)
            for st in range(2):
                half = slice(64 * st, 64 * st + 64)
                s = m.streams[st]
                key = (w, "y", st)
                self.wait_taken(pe, w, "SA", st)
                free(*key)
                for e in range(4):
                    h = 2 * (4 * q + e) + st
                    mmul(cols(key, e, DH), s["rbT"][:, e, :], s["SA"][:, e, :], start=True, stop=False)
                    mm = mmul(cols(key, e, DH), s["rkT"][:, e, :], m.v[:, c, h * DH:(h + 1) * DH],
                              start=False, stop=(c == 0))
                    if c:
                        mm = mmul(cols(key, e, DH), m.r[half, 4 * q + e, tok], m.S[half, 4 * q + e, :],
                                  start=False, stop=True)
                done(mm, *key)
            for st in range(2):
                half = slice(64 * st, 64 * st + 64)
                key = (w, "S", st)
                self.wait_taken(pe, w, "tok", 2)
                free(*key)
                for e in range(4):
                    h = 2 * (4 * q + e) + st
                    out = cols(key, e, DH)[half]
                    mmul(out, m.tok[:, 1, e, half], m.streams[st]["SA"][:, e, :], start=True, stop=False)
                    mm = mmul(out, m.tok[:, 2, e, half], m.v[:, c, h * DH:(h + 1) * DH], start=False, stop=True)
                done(mm, *key)

    def scalar(self, act, step):
        env, nc, m = self.env, self.env.nc, self.m

        def take(dst, src, *key):
            self.wait_ready(act, *key)
            nc.scalar.activation(dst, src, ACT.Copy).then_inc(self.taken["A"], 1)

        four = lambda key, n: self.bank(*key)[:, 0:4 * n].rearrange("p (e n) -> p e n", e=4)
        for w, (c, q) in enumerate(self.STEPS):
            if w:
                self.wait_ready(act, w - 1, "S", 1)
            for arr in range(3):
                key = (w, "tok", arr)
                take(m.tok[:, arr], four(key, P), *key)
            for st in range(2):
                take(m.streams[st]["Z"], four((w, "Z", st), DH), w, "Z", st)
            for lv in range(1, LEVELS):
                for st in range(2):
                    key = (w, "Y", lv, st)
                    if lv > 1:
                        self.wait_ready(act, w, "XT", lv - 1, st)
                    take(m.streams[st]["Y"], four(key, P), *key)
            for st in range(2):
                half = slice(64 * st, 64 * st + 64)
                key = (w, "WT", st)
                take(m.WT[half], four(key, P)[half], *key)
            for st in range(2):
                take(m.streams[st]["SA"], four((w, "SA", st), DH), w, "SA", st)
            for st in range(2):
                dst = m.kk[:, 4 * q:4 * q + 4, c * P + 64 * st:c * P + 64 * st + 64]
                take(dst, four((w, "y", st), DH), w, "y", st)

    def vector(self, dve, step):
        env, nc, m = self.env, self.env.nc, self.m
        v = nc.vector
        mask = lambda at: env.const[:, at:at + P].unsqueeze(1).to_broadcast([P, 4, P])
        four = lambda key, n=P: self.bank(*key)[:, 0:4 * n].rearrange("p (e n) -> p e n", e=4)

        for w, (c, q) in enumerate(self.STEPS):
            if w:
                self.wait_ready(dve, w - 1, "S", 1)
            for st in range(2):
                s = m.streams[st]
                for name, at, dst in (("abT", C_STRICT_T, "abT"), ("ab", C_PAIR, "X"), ("akT", C_STRICT_T, "akT"),
                                      ("rbT", C_INCL_T, "rbT"), ("rkT", C_INCL_T, "rkT")):
                    key = (w, name, st)
                    self.wait_ready(dve, *key)
                    v.tensor_tensor(s[dst], four(key), mask(at), ALU.mult).then_inc(self.taken["D"], 1)
            for lv in range(1, LEVELS):
                for st in range(2):
                    s = m.streams[st]
                    for name in (("X", "XT") if lv < LEVELS - 1 else ("XT",)):
                        key = (w, name, lv, st)
                        if name == "X":
                            self.wait_ready(dve, w, "XT", lv, st)
                        self.wait_ready(dve, *key)
                        v.tensor_tensor(s[name], four(key), s[name], ALU.add).then_inc(self.taken["D"], 1)
            for st in range(2):
                half = slice(64 * st, 64 * st + 64)
                key = (w, "S", st)
                self.wait_ready(dve, *key)
                S = m.S[half, 4 * q:4 * q + 4, :]
                new = four(key, DH)[half]
                if c == 0:
                    v.tensor_tensor(S, new, m.coef[half, 4 * q:4 * q + 4, 1:2].to_broadcast([64, 4, DH]),
                                    ALU.mult).then_inc(self.taken["D"], 1)
                elif c < NT - 1:
                    step(v.tensor_tensor(S, S, new, ALU.add))
                    v.tensor_tensor(S, S, m.coef[half, 4 * q:4 * q + 4, c + 1:c + 2].to_broadcast([64, 4, DH]),
                                    ALU.mult).then_inc(self.taken["D"], 1)
                else:
                    v.tensor_tensor(S, S, new, ALU.add).then_inc(self.taken["D"], 1)

    def gpsimd(self, pool, step):
        env, nc, m = self.env, self.env.nc, self.m
        g = nc.gpsimd
        mask = lambda at: env.const[:, at:at + P].unsqueeze(1).to_broadcast([P, 4, P])
        for w in range(len(self.STEPS)):
            for st in range(2):
                s = m.streams[st]
                self.wait_taken(pool, w, "ab", st)
                step(g.tensor_tensor(s["XT"], s["abT"], mask(C_PAIR_T), ALU.mult))
                step(g.tensor_tensor(s["XT"], s["XT"], mask(C_IDENT), ALU.add))
                g.tensor_tensor(s["X"], s["X"], mask(C_IDENT), ALU.add).then_inc(self.start_ready, 1)
                if st == 0:
                    g.tensor_tensor(s["MT"][1], s["abT"], mask(C_LEVEL_T), ALU.mult).then_inc(self.part_ready, 1)
            g.tensor_tensor(s["MT"][1], s["abT"], mask(C_LEVEL_T), ALU.mult).then_inc(self.part_ready, 1)
            for lv in range(2, LEVELS):
                for st in range(2):
                    s = m.streams[st]
                    if lv > 2:
                        self.wait_ready(pool, w, "Y", lv - 2, st)
                    g.tensor_tensor(s["MT"][lv % 2], s["abT"], mask(C_LEVEL_T + (lv - 1) * P),
                                    ALU.mult).then_inc(self.part_ready, 1)


class RwkvGate(Stage):

    def __init__(self, env, m):
        super().__init__(env)
        self.m = m
        g2 = env.io["g2_2"][0]
        self.ld = env.load((0, 1, D, g2[0:P].unsqueeze(1)), (D, 1, D, g2[P:160].unsqueeze(1)))
        self.g0 = env.group(8)
        env.release(self.ld, env.proj_ready, env.groups)
        self.rows = env.sem("gn_rows")
        self.var_ready, self.std_ready = env.sem("gn_var_ready"), env.sem("gn_std_ready")

    def gpsimd(self, pool, step):
        env, m = self.env, self.m
        pool.dma_start(m.gn[:, 0, :], env.io["gn_g_2"][0].partition_broadcast(P)).then_inc(self.rows, 16)
        pool.dma_start(m.gn[:, 1, :], env.io["gn_b_2"][0].partition_broadcast(P)).then_inc(self.rows, 16)

    def tensor(self, pe):
        env, nc, m = self.env, self.env.nc, self.m
        env.wait_load(pe, self.ld)
        w = env.slot(self.ld, 2, D)
        for i in range(NT):
            tok = slice(i * P, (i + 1) * P)
            for half in range(2):
                g = self.g0 + 2 * i + half
                cols = slice(512 * half, 512 * half + 512)
                env.wait_bank(pe, g)
                nc.tensor.matmul(env.bank(g), m.sg[:, 0, tok], w[:, 0, cols], start=True, stop=False)
                nc.tensor.matmul(env.bank(g), m.sg[0:32, 1, tok], w[0:32, 1, cols],
                                 start=False, stop=True).then_inc(env.proj_ready, 1)

    def scalar(self, act, step):
        env, nc, m = self.env, self.env.nc, self.m
        for i in range(NT):
            act.wait_ge(self.var_ready, i + 1)
            nc.scalar.activation(m.grstd, m.var, ACT.Sqrt).then_inc(self.std_ready, 1)

    def vector(self, dve, step):
        env, nc, m = self.env, self.env.nc, self.m
        v = nc.vector
        wide = lambda c: c.unsqueeze(2).to_broadcast([P, RH, DH])
        dve.wait_ge(self.rows, 32)
        tmp = m.tmp.rearrange("p (h d) -> p h d", d=DH)
        for i in range(NT):
            y = m.kk[:, :, i * P:(i + 1) * P].rearrange("p k (h d) -> p k h d", d=DH)
            o, flat = m.o[:, i, :].rearrange("p (h d) -> p h d", d=DH), m.o[:, i, :]
            step(v.tensor_copy(flat.rearrange("p (k d) -> p k d", d=P), m.kk[:, :, i * P:(i + 1) * P]))
            step(v.tensor_reduce(m.mean, o, AX, ALU.add))
            step(v.tensor_scalar(m.mean, m.mean, 1.0 / DH, None, ALU.mult))
            step(v.tensor_tensor(o, o, wide(m.mean), ALU.subtract))
            step(v.tensor_tensor(m.tmp, flat, flat, ALU.mult))
            step(v.tensor_reduce(m.var, tmp, AX, ALU.add))
            step(v.tensor_scalar(m.var, m.var, 1.0 / DH, GN_EPS, ALU.mult, ALU.add))
            v.reciprocal(m.var, m.var).then_inc(self.var_ready, 1)
            dve.wait_ge(self.std_ready, i + 1)
            step(v.tensor_tensor(o, o, wide(m.grstd), ALU.mult))
            step(v.tensor_tensor(flat, flat, m.gn[:, 0, :], ALU.mult))
            step(v.tensor_tensor(flat, flat, m.gn[:, 1, :], ALU.add))
            step(v.tensor_tensor(tmp, m.v[:, i, :].rearrange("p (h d) -> p h d", d=DH), wide(m.bonus[:, i, :]), ALU.mult))
            step(v.tensor_tensor(flat, flat, m.tmp, ALU.add))
            for half in range(2):
                g = self.g0 + 2 * i + half
                cols = slice(512 * half, 512 * half + 512)
                dve.wait_ge(env.proj_ready, g + 1)
                v.tensor_tensor(flat[:, cols], env.bank(g), flat[:, cols], ALU.mult).then_inc(env.proj_taken, 1)
        dve.wait_ge(env.proj_taken, self.g0 + 8)


def rwkv_stages(env, io):
    m = RwkvMemory(env)
    return [
        Norm(env, V_G),
        RwkvProject(env, m),
        RwkvPrepare(env, m),
        RwkvDecay(env, m),
        RwkvCore(env, m),
        RwkvGate(env, m),
        Output(env, io["w_o_rwkv_2"][0], io["norm_g_2"][0, 1], env.uT, m.o),
    ]


def end_stage(env, eng, s):
    eng.drain().then_inc(env.stage_done, 1)
    eng.wait_ge(env.stage_done, 4 * (s + 1))


def build(nc, io, out, n_stages=None, skip_rwkv=False):
    with ExitStack() as ctx:
        env = Env(nc, ctx, io)
        setup = Setup(env)
        m = NsaMemory(env, setup.bias, setup)
        stages = [
            setup,
            Norm(env, V_PRE, setup.x_arrived),
            NsaProject(env, m),
            NsaCompress(env, m),
            NsaCompressed(env, m),
            NsaAttend(env, m),
            Output(env, io["nsa_w_out"][0], io["norm_post"][0], m.qT, m.o, (io["nsa_w_in"][0], NSA_IN - D)),
        ]
        dm = DiffMemory(env, setup.bias)
        fm = FfnMemory(env)
        sm = SwaMemory(env)
        stages += [
            Norm(env, V_PRE + KD),
            DiffProject(env, dm),
            DiffAttend(env, dm),
            DiffNorm(env, dm),
            Output(env, io["diff_w_out"][0], io["norm_post"][1], dm.qT, dm.o, (io["diff_w_in"][0], 3 * D)),
        ]
        if not skip_rwkv:
            stages += rwkv_stages(env, io)
        g = io["norm_g_2"]
        stages += [
            Norm(env, V_G + 2 * KD),
            FfnUp(env, 0, fm),
            Output(env, io["w_down_2"][0], g[0, 3], fm.actT, kd=FT),
            Norm(env, V_B + 5 * KD),
            KvProject(env, sm),
            Norm(env, V_G + 4 * KD),
            SwaProject(env, sm),
            SwaAttend(env, sm),
            Output(env, io["w_o_attn_2"][0], g[1, 1], env.uT, sm.o),
            Norm(env, V_G + 6 * KD),
            FfnUp(env, 1, fm),
            Output(env, io["w_down_2"][1], g[1, 3], fm.actT, kd=FT),
        ]
        used = len(stages) if n_stages is None else n_stages
        n_loads = len(env.loads)
        stages = stages[:used]
        block = ctx.enter_context(nc.Block())

        @block.sync
        def _(sp):
            setup.load(sp)
            for n, (parts, sem, value) in enumerate(env.loads[:n_loads]):
                if n >= env.RING:
                    sp.wait_ge(env.loads[n - env.RING][1], env.loads[n - env.RING][2])
                for first, k, cols, src in parts:
                    rows = src.shape[0]
                    dst = env.slot(n, k, cols, first)
                    sp.dma_start(dst[0:rows], src).then_inc(env.w_arrived[n % env.RING], 16)
            sp.wait_ge(env.stage_done, 4 * len(stages))
            sp.dma_start(out.rearrange("b (t p) d -> p (b t) d", p=P), env.x).then_inc(env.stored, 16)
            sp.wait_ge(env.stored, 16)

        @block.tensor
        def _(pe):
            for s, stage in enumerate(stages):
                stage.tensor(pe)
                end_stage(env, pe, s)

        @block.scalar
        def _(act):
            step = Steps(act, env.act_step)
            for s, stage in enumerate(stages):
                stage.scalar(act, step)
                end_stage(env, act, s)

        @block.vector
        def _(dve):
            step = Steps(dve, env.dve_step)
            for s, stage in enumerate(stages):
                stage.vector(dve, step)
                end_stage(env, dve, s)

        @block.gpsimd
        def _(pool):
            step = Steps(pool, env.pool_step)
            for s, stage in enumerate(stages):
                stage.gpsimd(pool, step)
                end_stage(env, pool, s)


def declare(nc, inputs, n_stages=None, skip_rwkv=False):
    arrays, io = {}, {}
    given = dict(inputs)
    given["shape_constants"] = shape_constants()
    given["distance_one_hot"] = distance_one_hot().astype("bfloat16")
    for name, a in given.items():
        a = np.ascontiguousarray(a)
        arrays["in_" + name] = a
        io[name] = nc.dram_tensor("in_" + name, a.shape, mybir.dt.from_np(a.dtype), kind="ExternalInput").ap()
    out = nc.dram_tensor("out", (1, T, D), F32, kind="ExternalOutput").ap()
    build(nc, io, out, n_stages, skip_rwkv)
    return arrays


def kernel(**inputs):
    import concourse.bacc as _bacc
    from concourse.bass_utils import run_bass_kernel_spmd as _run

    nc = _bacc.Bacc("TRN2", target_bir_lowering=False, num_devices=1)
    arrays = declare(nc, inputs)
    r = _run(nc, [arrays], core_ids=[0])
    return r.results[0]["out"]
```

```python
from contextlib import ExitStack

import numpy as np

import concourse.bass as bass
from concourse import mybir

ALU = mybir.AluOpType
ACT = mybir.ActivationFunctionType
AX = mybir.AxisListType.X
F32 = mybir.dt.float32
BF16 = mybir.dt.bfloat16
F32R = mybir.dt.float32r

P = 128
T = 512
NT = T // P
D = 1024
KD = D // P
NEG = -1e30
EPS = 1e-6

HEADS, GROUPS, HPG, DH = 16, 4, 4, 64
BUCKETS, MAX_DIST = 32, 128
CMP_BLOCK, CMP_STRIDE = 32, 16
NC = (T - CMP_BLOCK) // CMP_STRIDE + 1
NCP = 32
CMP_K = CMP_BLOCK * DH // P
DIFF_HEADS = 8
LAMBDA_INIT = 0.8 - 0.6 * float(np.exp(-0.3))
NSA_IN = D + 6 * 256 + 3 * HEADS + D
D_FF = 2816
FT = D_FF // P
RH = 16
GN_EPS = 64e-5
DECAY_SCALE = float(np.exp(-0.5))
LEVELS = 7

DIST0 = (NCP - 1) * CMP_STRIDE + CMP_BLOCK - 1 + 1
NDIST = DIST0 + T


def distance_one_hot():
    n = np.arange(NDIST) - DIST0
    exact = BUCKETS // 2
    nf = np.maximum(n, 1)
    large = exact + (np.log(nf / exact) / np.log(MAX_DIST / exact) * (BUCKETS - exact) + 1e-9).astype(np.int64)
    bucket = np.where(n < exact, np.maximum(n, 0), np.minimum(large, BUCKETS - 1))
    table = np.zeros((P, NDIST), np.float32)
    for part in range(3):
        table[32 * part + bucket, np.arange(NDIST)] = n >= 0
    table[96] = n < 0
    return table


C_IDENT = 0
C_HEADSUM = C_IDENT + P
C_HEADSEL = C_HEADSUM + P
C_BAND = C_HEADSEL + 2
C_STRICT_T = C_BAND + 2 * P
C_INCL_T = C_STRICT_T + P
C_PAIR = C_INCL_T + P
C_PAIR_T = C_PAIR + P
C_ONES = C_PAIR_T + P
C_LEVEL_T = C_ONES + P
N_CONST = C_LEVEL_T + (LEVELS - 1) * P


def shape_constants():
    c = np.zeros((P, N_CONST), np.float32)
    r = np.arange(P)
    c[:, C_IDENT:C_IDENT + P] = np.eye(P)
    c[:, C_HEADSUM:C_HEADSUM + P] = (r[:, None] // DH) == (r[None] // DH)
    c[:, C_HEADSEL:C_HEADSEL + 2] = (r[:, None] // DH) == np.arange(2)[None]
    c[:, C_BAND:C_BAND + P] = np.where(r[None] > r[:, None], 0.0, NEG)
    c[:, C_BAND + P:C_BAND + 2 * P] = np.where(r[None] <= r[:, None], 0.0, NEG)
    c[:, C_STRICT_T:C_STRICT_T + P] = r[:, None] < r[None]
    c[:, C_INCL_T:C_INCL_T + P] = r[:, None] <= r[None]
    pair = (r[None] == r[:, None] - 1) & (r[:, None] % 2 == 1)
    c[:, C_PAIR:C_PAIR + P] = pair
    c[:, C_PAIR_T:C_PAIR_T + P] = pair.T
    c[:, C_ONES:C_ONES + P] = 1.0
    for lv in range(1, LEVELS):
        b = 1 << lv
        low = (r[:, None] // (2 * b) == r[None] // (2 * b)) & (r[:, None] // b % 2 == 1) & (r[None] // b % 2 == 0)
        c[:, C_LEVEL_T + (lv - 1) * P:C_LEVEL_T + lv * P] = low.T
    return c


V_PRE = 0
V_G = 16
V_MU = 80
V_B = 128
V_CONV = 176
N_VEC = V_CONV + 2 * 176


WARM_UP = 16


class Env:

    RAW = 3
    SLOT = 1024
    def __init__(self, nc, ctx, io):
        self.nc, self.ctx, self.io = nc, ctx, io
        words = 52496
        self.arena_base = -(-nc.sbuf_base // 32) * 32
        ctx.enter_context(nc.sbuf_tensor("arena", [P, words], F32))
        self.buffers = 0
        self.words = words
        self.ps = ctx.enter_context(nc.psum_tensor("ps", [P, 8, 512], F32))
        self.at = 0
        self.x = self.take(NT, D)
        self.uT_at = self.at
        self.uT = self.take(KD, T)
        self.big_at = self.at
        self.big = self.take(4096)
        self.raw = self.take(self.RAW, self.SLOT)
        self.part_hi = self.take_r("weights_hi", 2, self.SLOT)
        self.part_lo = self.take_r("weights_lo", 2, self.SLOT)
        self.const = self.take(N_CONST)
        self.vec = self.take(N_VEC)
        self.grow = self.take(D)
        self.stat_at = self.at
        self.stat = self.take(256)
        self.junk = self.take(512)
        self.junk2 = self.take(2, 512)
        self.gates_at = self.at
        self.at += 288
        self.area = self.at = -(-self.at // 8) * 8
        self.ident = self.const[:, C_IDENT:C_IDENT + P]
        self.proj_ready = self.sem("proj_ready")
        self.proj_taken = self.sem("proj_taken")
        self.groups = 0
        self.raw_arrived = [self.sem(f"raw_arrived{r}") for r in range(self.RAW)]
        self.hi_ready = self.sem("weights_hi_ready")
        self.lo_ready = self.sem("weights_lo_ready")
        self.slot_done = self.sem("slot_done")
        self.loads = []
        self.splits = []
        self.hi_issued = self.lo_issued = 0
        self.slots_done = 0
        self.aux_arrived = self.sem("aux_arrived")
        self.stage_done = self.sem("stage_done")
        self.dve_step = self.sem("dve_step")
        self.act_step = self.sem("act_step")
        self.pool_step = self.sem("pool_step")
        self.rms_ready = self.sem("rms_ready")
        self.un_ready = self.sem("un_ready")
        self.un_turned = self.sem("un_turned")
        self.uhi_ready = self.sem("uhi_ready")
        self.uT_ready = self.sem("uT_ready")
        self.next_g_arrived = self.sem("next_g_arrived")
        self.norms = self.uhis = self.repeats = 0
        self.next_g = self.junk2.rearrange("p a b -> p (a b)")
        self.eps = self.stat[:, 12:13]
        self.tr_ready = self.sem("tr_ready")
        self.oT_ready = self.sem("oT_ready")
        self.otmp_ready, self.oT_hi_ready = self.sem("otmp_ready"), self.sem("oT_hi_ready")
        self.yrms_ready = self.sem("yrms_ready")
        self.g_arrived = self.sem("g_arrived")
        self.outs = 0
        self.trs = 0
        self.ots = 0
        self.stored = self.sem("stored")
        self.aux = 0
        self.x_added = self.sem("x_added")

    def sem(self, name):
        return self.ctx.enter_context(self.nc.semaphore(name))

    def take(self, *shape, at=None):
        n = int(np.prod(shape))
        if at is None:
            at = self.at
            self.at += n + -n % 8
        assert at + n <= self.words, (at + n, self.words)
        self.buffers += 1
        v = self.nc.alloc_sbuf_tensor_at(f"buffer{self.buffers}", [P, n], F32, offset=self.arena_base + 4 * at)[:]
        if len(shape) == 2:
            v = v.rearrange("p (a b) -> p a b", a=shape[0])
        if len(shape) == 3:
            v = v.rearrange("p (a b c) -> p a b c", a=shape[0], b=shape[1])
        return v

    def take_r(self, name, a, b, at=None):
        if at is None:
            at = self.at
            self.at += a * b
        assert at + a * b <= self.words, (at + a * b, self.words)
        return self.nc.alloc_sbuf_tensor_at(name, [P, a, b], F32R, offset=self.arena_base + 4 * at)[:]

    def load(self, src, split=True):
        self.loads.append([src, src.shape[1], src.shape[2], len(self.splits) if split else None, None])
        if split:
            self.splits.append(len(self.loads) - 1)
        return len(self.loads) - 1

    def release(self, ld, sem, value):
        self.loads[ld][4] = (sem, value)

    def release_slot(self, ld):
        self.slots_done += 1
        self.release(ld, self.slot_done, self.slots_done)

    def whole(self, ld):
        k, n = self.loads[ld][1:3]
        return self.raw[:, ld % self.RAW, 0:k * n].rearrange("p (k n) -> p k n", k=k)

    def parts(self, ld):
        k, n, part = self.loads[ld][1:4]
        return [ring[:, part % 2, 0:k * n].rearrange("p (k n) -> p k n", k=k) for ring in (self.part_hi, self.part_lo)]

    def wait_whole(self, eng, ld):
        eng.wait_ge(self.raw_arrived[ld % self.RAW], 16 * (ld // self.RAW + 1))

    def wait_hi(self, pe, ld):
        pe.wait_ge(self.hi_ready, self.loads[ld][3] + 1)

    def wait_lo(self, pe, ld):
        pe.wait_ge(self.lo_ready, self.loads[ld][3] + 1)

    def fetch(self, sp, ld):
        src, k, n, _, _ = self.loads[ld]
        if ld >= self.RAW:
            _, _, _, part, release = self.loads[ld - self.RAW]
            if part is None:
                sp.wait_ge(*release)
            else:
                sp.wait_ge(self.lo_ready, part + 1)
        sp.dma_start(self.whole(ld)[0:src.shape[0]], src).then_inc(self.raw_arrived[ld % self.RAW], 16)

    def split_hi(self, act, upto):
        while self.hi_issued < len(self.splits) and self.splits[self.hi_issued] <= upto:
            part = self.hi_issued
            ld = self.splits[part]
            n = self.loads[ld][1] * self.loads[ld][2]
            self.wait_whole(act, ld)
            if part >= 2:
                act.wait_ge(*self.loads[self.splits[part - 2]][4])
            self.nc.scalar.activation(self.part_hi[:, part % 2, 0:n], self.raw[:, ld % self.RAW, 0:n],
                                      ACT.Copy).then_inc(self.hi_ready, 1)
            self.hi_issued += 1

    def split_lo(self, pool, upto):
        while self.lo_issued < len(self.splits) and self.splits[self.lo_issued] <= upto:
            part = self.lo_issued
            ld = self.splits[part]
            n = self.loads[ld][1] * self.loads[ld][2]
            pool.wait_ge(self.hi_ready, part + 1)
            self.nc.gpsimd.tensor_tensor(self.part_lo[:, part % 2, 0:n], self.raw[:, ld % self.RAW, 0:n],
                                         self.part_hi[:, part % 2, 0:n].bitcast(F32),
                                         ALU.subtract).then_inc(self.lo_ready, 1)
            self.lo_issued += 1

    def group(self, n=1):
        g = self.groups
        self.groups += n
        return g

    def bank(self, g):
        return self.ps[:, g % 4, :]

    def wait_bank(self, pe, g):
        if g >= 4:
            pe.wait_ge(self.proj_taken, g - 3)


class Steps:

    def __init__(self, eng, sem):
        self.eng, self.sem, self.n = eng, sem, 0

    def __call__(self, ins):
        self.n += 1
        ins.then_inc(self.sem, 1)
        self.eng.wait_ge(self.sem, self.n)


def w_cols(w, c0, n):
    return w.rearrange("(k p) m -> p k m", p=P)[:, :, c0:c0 + n]


def project_features(env, pe, ld, rhs, g, cols=P):
    nc = env.nc
    hi, lo = env.parts(ld)
    out = env.bank(g)[0:cols]
    env.wait_bank(pe, g)
    env.wait_hi(pe, ld)
    for k in range(KD):
        nc.tensor.matmul(out, hi[:, k, :], rhs[0][:, k, :], start=(k == 0), stop=False)
        nc.tensor.matmul(out, hi[:, k, :], rhs[1][:, k, :], start=False, stop=False)
    env.wait_lo(pe, ld)
    for k in range(KD):
        mm = nc.tensor.matmul(out, lo[:, k, :], rhs[0][:, k, :], start=False, stop=(k == KD - 1))
    mm.then_inc(env.proj_ready, 1)


def project_tokens(env, pe, lds, lhs, g, kd=KD):
    nc = env.nc
    m, n = env.loads[lds[0]][1:3]
    banks = -(-n // 512)
    width = n // banks

    def out(i, b):
        return env.ps[:, 2 * i + b, :] if banks == 2 else env.bank(g + i)[:, 0:n]

    def highs(index, i):
        hi = env.parts(lds[index])[0]
        for k in range(m):
            for part in range(2):
                for b in range(banks):
                    nc.tensor.matmul(out(i, b), lhs[part][:, index * m + k, i * P:(i + 1) * P],
                                     hi[:, k, b * width:(b + 1) * width],
                                     start=(index + k == 0 and part == 0), stop=False)

    def lows(index, i):
        lo = env.parts(lds[index])[1]
        for k in range(m):
            for b in range(banks):
                stop = index * m + k == kd - 1
                mm = nc.tensor.matmul(out(i, b), lhs[0][:, index * m + k, i * P:(i + 1) * P],
                                      lo[:, k, b * width:(b + 1) * width], start=False, stop=stop)
                if stop:
                    mm.then_inc(env.proj_ready, 1)
        if i == NT - 1 and index < len(lds) - 1:
            mm.then_inc(env.slot_done, 1)

    if g:
        pe.wait_ge(env.proj_taken, g)
    apart = len(lds) - 2 if banks == 2 else len(lds)
    for index in range(apart):
        env.wait_hi(pe, lds[index])
        for i in range(NT):
            highs(index, i)
        env.wait_lo(pe, lds[index])
        for i in range(NT):
            lows(index, i)
    if apart < len(lds):
        a, b = apart, apart + 1
        env.wait_lo(pe, lds[a])
        for index, i in ((a, 0), (a, 1), (a, 2), (b, 0), (a, 3), (b, 1), (b, 2), (b, 3)):
            if (index, i) == (b, 0):
                env.wait_lo(pe, lds[b])
            highs(index, i)
            lows(index, i)


def load_tokens(env, w, c0, n, kd=KD):
    m = env.SLOT // n
    lds = []
    for k in range(0, kd, m):
        lds.append(env.load(w_cols(w, c0, n)[:, k:k + m, :]))
        if k + m < kd:
            env.release_slot(lds[-1])
    g = env.group(NT * -(-n // 512))
    env.release(lds[-1], env.proj_ready, env.groups)
    return lds, g


def load_features(env, w, c0, n, cols=P):
    out = []
    for c in range(c0, c0 + n, cols):
        ld = env.load(w_cols(w, c, cols))
        g = env.group()
        env.release(ld, env.proj_ready, env.groups)
        out.append((ld, g))
    return out


class Stage:
    def __init__(self, env):
        self.env = env

    def tensor(self, pe):
        pass

    def scalar(self, act, step):
        pass

    def vector(self, dve, step):
        pass

    def gpsimd(self, pool, step):
        pass


class Setup(Stage):

    def __init__(self, env):
        super().__init__(env)
        self.bias = env.take(HEADS, T, at=env.words - HEADS * T)
        at = env.area
        self.rows = env.take(6, P, at=at)
        self.tab = env.take(HEADS, at=at + 1000)
        self.tab_rest = env.take(HEADS, at=at + 1016)
        self.hot = env.ctx.enter_context(env.nc.sbuf_tensor("one_hot", [P, NDIST], BF16))
        self.tab_hi = env.ctx.enter_context(env.nc.sbuf_tensor("table_parts", [P, 3, HEADS], BF16))
        self.table3 = env.ctx.enter_context(env.nc.sbuf_tensor("table3", [P, HEADS], BF16))
        self.x_arrived = env.sem("x_arrived")
        self.table_ready = env.sem("table_ready")
        self.rows_zeroed = env.sem("rows_zeroed")
        self.bias_ready = env.sem("bias_ready")
        self.bias_taken = env.sem("bias_taken")
        self.vec_ready = env.sem("vec_ready")
        self.vec_taken = env.sem("vec_taken")
        self.rows_arrived = env.sem("rows_arrived")
        self.tab_arrived = env.sem("tab_arrived")
        self.const_arrived = env.sem("const_arrived")

    def load(self, sp):
        env, io, nc = self.env, self.env.io, self.env.nc
        sp.dma_start(env.x, io["x"].rearrange("b (t p) d -> p (b t) d", p=P)).then_inc(self.x_arrived, 16)
        sp.dma_start(env.const, io["shape_constants"]).then_inc(self.const_arrived, 16)
        sp.wait_ge(self.rows_zeroed, 1)
        for part in range(3):
            sp.dma_start(self.tab[32 * part:32 * part + 32, :], io["rel_bias_table"]).then_inc(self.tab_arrived, 16)
        sp.dma_start(self.hot[:], io["distance_one_hot"]).then_inc(self.tab_arrived, 16)
        r = self.rows
        vec = lambda a: a.rearrange("(k p) -> k p", p=P)
        put = lambda row, at, n, src: sp.dma_start(r[at:at + n, row, :], src).then_inc(self.rows_arrived, 16)
        put(0, 0, 16, io["norm_pre"].rearrange("l (k p) -> (l k) p", p=P))
        put(0, 16, 64, io["norm_g_2"].rearrange("l w (k p) -> (l w k) p", p=P))
        put(0, 80, 48, io["mu_2"].rearrange("a i (k p) -> (a i k) p", p=P))
        for n, name in enumerate(["w_decay0_2", "a0_2", "k_k_2", "k_a_2"]):
            put(1, 8 * n, 8, io[name].rearrange("a (k p) -> (a k) p", p=P))
        put(1, 32, 8, io["r_k_2"].rearrange("a (k h) n -> (a k) (h n)", h=2))
        put(1, 40, 8, vec(io["kv_g_2"]))
        for l in range(2):
            w = io["conv_w_2"][l].rearrange("w (k p) -> (w k) p", p=P)
            put(2 + 2 * l, 0, 88, w[0:88])
            put(3 + 2 * l, 0, 44, w[88:132])
            put(3 + 2 * l, 44, 44, vec(io["conv_b_2"][l]))
    N_ROWS = 3 + 4 + 2 + 6

    def tensor(self, pe):
        env, nc = self.env, self.env.nc
        pe.wait_ge(self.rows_arrived, 16 * self.N_ROWS)
        pe.wait_ge(self.const_arrived, 16)
        for n in range(6):
            size = [128, 48, 88, 88, 88, 88][n]
            tr = nc.tensor.transpose(env.ps[:, n // 4, (n % 4) * P:(n % 4) * P + size], self.rows[0:size, n, :],
                                     env.ident[0:size, 0:size])
        tr.then_inc(self.vec_ready, 1)
        pe.wait_ge(self.table_ready, 1)
        pe.wait_ge(self.tab_arrived, 64)
        pe.wait_ge(self.vec_taken, 1)
        for i in range(8):
            for c in range(32):
                at = DIST0 + P - c - 32 * i
                mm = nc.tensor.matmul(env.ps[:, i, c * HEADS:(c + 1) * HEADS], self.hot[:, at:at + P],
                                      self.table3[:], start=True, stop=True)
            mm.then_inc(self.bias_ready, 1)

    def vector(self, dve, step):
        env, nc = self.env, self.env.nc
        nc.vector.memset(env.eps, EPS)
        nc.vector.memset(self.tab[:], 0.0).then_inc(self.rows_zeroed, 1)
        dve.wait_ge(self.tab_arrived, 64)
        dve.wait_ge(self.rows_zeroed, 1)
        step(nc.vector.tensor_copy(self.tab_hi[:, 0, :], self.tab))
        step(nc.vector.tensor_tensor(self.tab_rest, self.tab, self.tab_hi[:, 0, :], ALU.subtract))
        step(nc.vector.tensor_copy(self.tab_hi[:, 1, :], self.tab_rest))
        step(nc.vector.tensor_tensor(self.tab_rest, self.tab_rest, self.tab_hi[:, 1, :], ALU.subtract))
        step(nc.vector.tensor_copy(self.tab_hi[:, 2, :], self.tab_rest))
        for part in range(3):
            q = slice(32 * part, 32 * part + 32)
            nc.vector.tensor_copy(self.table3[q, :], self.tab_hi[q, part, :])
        nc.vector.memset(self.table3[96:128, :], NEG).then_inc(self.table_ready, 1)
        dve.wait_ge(self.vec_ready, 1)
        o = 0
        for n in range(6):
            size = [128, 48, 88, 88, 88, 88][n]
            step(nc.vector.tensor_copy(env.vec[:, o:o + size], env.ps[:, n // 4, (n % 4) * P:(n % 4) * P + size]))
            o += size
        nc.vector.memset(self.tab_rest, 0.0).then_inc(self.vec_taken, 1)
        for i in range(8):
            dve.wait_ge(self.bias_ready, i + 1)
            nc.vector.tensor_copy(
                self.bias.rearrange("p h c -> p c h")[:, 2 * P + 32 * i:2 * P + 32 * (i + 1), :],
                env.ps[:, i, :].rearrange("p (c h) -> p c h", h=HEADS)).then_inc(self.bias_taken, 1)
        dve.wait_ge(self.bias_taken, 8)
        step(nc.vector.tensor_copy(self.bias[:, :, 0:2 * P],
                                   self.bias[:, :, 2 * P:2 * P + 1].to_broadcast([P, HEADS, 2 * P])))


class Renorm:

    def __init__(self, env, g_row, u):
        self.env, self.g_row, self.u = env, g_row, u
        self.rms_n = env.norms - NT * env.repeats
        self.n, self.hi_n, self.g_n = env.norms, env.uhis, env.norms // NT + 1
        env.norms += NT
        if len(u) == 2:
            env.uhis += NT
        self.un = env.big.rearrange("p (t d) -> p t d", t=NT)
        self.ssq, self.rms, self.rstd = env.stat[:, 0:4], env.stat[:, 4:8], env.stat[:, 8:12]

    def fetch(self, pool):
        env = self.env
        pool.dma_start(env.next_g, self.g_row.partition_broadcast(P)).then_inc(env.next_g_arrived, 16)

    def square(self, act, step, i):
        env, nc = self.env, self.env.nc
        step(nc.scalar.activation(self.un[:, i, :], env.x[:, i, :], ACT.Square, accum_out=self.ssq[:, i:i + 1]))
        nc.scalar.activation(self.rms[:, i:i + 1], self.ssq[:, i:i + 1], ACT.Sqrt, scale=1.0 / D,
                             bias=env.eps).then_inc(env.rms_ready, 1)

    def scale(self, dve, step, i, again=False):
        env, nc = self.env, self.env.nc
        if not again:
            dve.wait_ge(env.rms_ready, self.rms_n + i + 1)
            step(nc.vector.reciprocal(self.rstd[:, i:i + 1], self.rms[:, i:i + 1]))
        dve.wait_ge(env.next_g_arrived, 16 * self.g_n)
        nc.vector.scalar_tensor_tensor(self.un[:, i, :], env.x[:, i, :], self.rstd[:, i:i + 1], env.next_g,
                                       ALU.mult, ALU.mult).then_inc(env.un_ready, 1)

    def turn(self, pe, i):
        env, nc = self.env, self.env.nc
        pe.wait_ge(env.un_ready, self.n + i + 1)
        for k in range(KD):
            tr = nc.tensor.transpose(env.ps[:, 2 * i + k // 4, (k % 4) * P:(k % 4 + 1) * P],
                                     self.un[:, i, k * P:(k + 1) * P], env.ident)
        tr.then_inc(env.un_turned, 1)

    def turned(self, i):
        return self.env.ps[:, 2 * i:2 * i + 2, :].rearrange("p b (k t) -> p (b k) t", t=P)

    def high(self, act, i):
        env, nc = self.env, self.env.nc
        act.wait_ge(env.un_turned, self.n + i + 1)
        nc.scalar.activation(self.u[0][:, :, i * P:(i + 1) * P], self.turned(i),
                             ACT.Copy).then_inc(env.uhi_ready if len(self.u) == 2 else env.uT_ready, 1)

    def low(self, dve, i):
        env, nc = self.env, self.env.nc
        if len(self.u) == 2:
            dve.wait_ge(env.uhi_ready, self.hi_n + i + 1)
            nc.vector.tensor_tensor(self.u[1][:, :, i * P:(i + 1) * P], self.turned(i),
                                    self.u[0][:, :, i * P:(i + 1) * P].bitcast(F32),
                                    ALU.subtract).then_inc(env.uT_ready, 1)

    def wait(self, pe):
        pe.wait_ge(self.env.uT_ready, self.n + NT)


class Norm(Stage):

    def __init__(self, env, g_row, u, x_arrived):
        super().__init__(env)
        self.norm, self.x_arrived = Renorm(env, g_row, u), x_arrived

    def gpsimd(self, pool, step):
        self.norm.fetch(pool)
        self.env.split_lo(pool, 1)

    def scalar(self, act, step):
        act.wait_ge(self.x_arrived, 16)
        for i in range(NT):
            self.norm.square(act, step, i)
        self.env.split_hi(act, 1)
        for i in range(NT):
            self.norm.high(act, i)

    def vector(self, dve, step):
        for i in range(NT):
            self.norm.scale(dve, step, i)
        for i in range(NT):
            self.norm.low(dve, i)

    def tensor(self, pe):
        for i in range(NT):
            self.norm.turn(pe, i)
        self.norm.wait(pe)


class NormAgain(Stage):

    def __init__(self, env, norm):
        super().__init__(env)
        self.norm = norm

    def scalar(self, act, step):
        for i in range(NT):
            self.norm.high(act, i)

    def vector(self, dve, step):
        for i in range(NT):
            self.norm.low(dve, i)

    def tensor(self, pe):
        for i in range(NT):
            self.norm.turn(pe, i)
        self.norm.wait(pe)


class Output(Stage):

    def __init__(self, env, w_out, g_row, oT, o=None, z=None, kd=KD, following=None):
        super().__init__(env)
        self.o, self.oT, self.kd, self.g_row, self.z = o, oT, kd, g_row, z
        self.n = env.outs
        env.outs += 1
        self.ot0, self.tr0 = env.ots, env.trs
        if o is not None:
            env.ots += KD
            env.trs += KD
        self.lds, self.g0 = load_tokens(env, w_out, 0, D, kd)
        self.y = env.big.rearrange("p (t d) -> p t d", t=NT)
        self.ssq, self.rms, self.rstd = env.stat[:, 16:20], env.stat[:, 20:24], env.stat[:, 24:28]
        self.tmp = env.junk2
        self.norm = Renorm(env, *following) if following else None

    def tensor(self, pe):
        env, nc = self.env, self.env.nc
        if self.o is not None:
            for k in range(KD):
                if k >= 2:
                    pe.wait_ge(env.otmp_ready, self.ot0 + k - 1)
                for t in range(NT):
                    tr = nc.tensor.transpose(env.ps[:, 6 + k % 2, t * P:(t + 1) * P],
                                             self.o[:, t, k * P:(k + 1) * P], env.ident)
                tr.then_inc(env.tr_ready, 1)
            pe.wait_ge(env.oT_ready, self.ot0 + KD)
        project_tokens(env, pe, self.lds, self.oT, self.g0, self.kd)
        if self.norm:
            for i in range(NT):
                self.norm.turn(pe, i)
            self.norm.wait(pe)

    def scalar(self, act, step):
        env, nc = self.env, self.env.nc
        env.split_hi(act, self.lds[0])
        for k in range(KD if self.o is not None else 0):
            act.wait_ge(env.otmp_ready, self.ot0 + k + 1)
            nc.scalar.activation(self.oT[0][:, k, :], self.tmp[:, k % 2, :], ACT.Copy).then_inc(env.oT_hi_ready, 1)
        env.split_hi(act, self.lds[-1])
        for i in range(NT + 3):
            if i < NT:
                act.wait_ge(env.proj_ready, self.g0 + 2 * i + 2)
                step(nc.scalar.activation(self.y[:, i, :].rearrange("p (b n) -> p b n", b=2),
                                          env.ps[:, 2 * i:2 * i + 2, :], ACT.Square,
                                          accum_out=self.ssq[:, i:i + 1]))
                nc.scalar.activation(self.rms[:, i:i + 1], self.ssq[:, i:i + 1], ACT.Sqrt, scale=1.0 / D,
                                     bias=env.eps).then_inc(env.yrms_ready, 1)
            if self.norm and 1 <= i <= NT:
                act.wait_ge(env.x_added, NT * self.n + i)
                self.norm.square(act, step, i - 1)
            if self.norm and i >= 3:
                self.norm.high(act, i - 3)
                env.split_hi(act, self.lds[-1] + min(i - 2, 2))

    def gpsimd(self, pool, step):
        env = self.env
        pool.dma_start(env.grow, self.g_row.partition_broadcast(P)).then_inc(env.g_arrived, 16)
        if self.norm:
            env.split_lo(pool, self.lds[0])
            if self.o is not None:
                pool.wait_ge(env.oT_ready, self.ot0 + KD)
            self.norm.fetch(pool)
        env.split_lo(pool, self.lds[-1] + 2)

    def vector(self, dve, step):
        env, nc = self.env, self.env.nc
        for k in range(KD if self.o is not None else 0):
            tr, tmp = env.ps[:, 6 + k % 2, :], self.tmp[:, k % 2, :]
            dve.wait_ge(env.tr_ready, self.tr0 + k + 1)
            if k >= 2:
                dve.wait_ge(env.oT_ready, self.ot0 + k - 1)
            if self.z is not None:
                nc.vector.tensor_tensor(tmp, tr, self.z[:, k, :], ALU.mult).then_inc(env.otmp_ready, 1)
            else:
                nc.vector.tensor_copy(tmp, tr).then_inc(env.otmp_ready, 1)
            if k:
                self.low(dve, k - 1)
        if self.o is not None:
            self.low(dve, KD - 1)
        dve.wait_ge(env.g_arrived, 16 * (self.n + 1))
        for i in range(NT + 3):
            if i < NT:
                dve.wait_ge(env.yrms_ready, NT * self.n + i + 1)
                step(nc.vector.reciprocal(self.rstd[:, i:i + 1], self.rms[:, i:i + 1]))
                y = self.y[:, i, :]
                nc.vector.scalar_tensor_tensor(y, env.ps[:, 2 * i:2 * i + 2, :].rearrange("p b n -> p (b n)"),
                                               self.rstd[:, i:i + 1], env.grow, ALU.mult,
                                               ALU.mult).then_inc(env.proj_taken, 2)
                dve.wait_ge(env.proj_taken, self.g0 + 2 * i + 2)
                nc.vector.tensor_tensor(env.x[:, i, :], env.x[:, i, :], y, ALU.add).then_inc(env.x_added, 1)
            if self.norm and 1 <= i <= NT:
                self.norm.scale(dve, step, i - 1)
            if self.norm and i >= 3:
                self.norm.low(dve, i - 3)

    def low(self, dve, k):
        env = self.env
        dve.wait_ge(env.oT_hi_ready, self.ot0 + k + 1)
        env.nc.vector.tensor_tensor(self.oT[1][:, k, :], self.tmp[:, k % 2, :], self.oT[0][:, k, :].bitcast(F32),
                                    ALU.subtract).then_inc(env.oT_ready, 1)


class NsaProject(Stage):

    def __init__(self, env, m):
        super().__init__(env)
        self.m = m
        w = env.io["nsa_w_in"][0]
        width = GROUPS * DH
        self.q = load_features(env, w, 0, D)
        self.kvc = load_features(env, w, D, 2 * width)
        self.branches = []
        for br in range(2):
            at = D + (2 + 2 * br) * width
            self.branches.append((load_features(env, w, at, width), load_tokens(env, w, at + width, width)))
        at = D + 6 * width
        self.gates = (env.load(w_cols(w, at, 3 * HEADS)), env.group(NT))
        env.release(self.gates[0], env.proj_ready, env.groups)
        self.z = load_features(env, w, at + 3 * HEADS, D)

    def tensor(self, pe):
        env, nc = self.env, self.env.nc
        u = self.m.u
        for ld, g in self.q + self.kvc:
            project_features(env, pe, ld, u, g)
        for keys, (lds, g) in self.branches:
            for ld, gk in keys:
                project_features(env, pe, ld, u, gk)
            project_tokens(env, pe, lds, u, g)
        ld, g = self.gates
        project_tokens(env, pe, [ld], u, g)
        for ld, g in self.z:
            project_features(env, pe, ld, u, g)

    def gpsimd(self, pool, step):
        self.env.split_lo(pool, self.z[-1][0] + 2)

    def scalar(self, act, step):
        env, nc, m = self.env, self.env.nc, self.m
        env.split_hi(act, self.q[0][0])
        for j, (ld, g) in enumerate(self.q):
            env.split_hi(act, ld + 1)
            act.wait_ge(env.proj_ready, g + 1)
            nc.scalar.activation(m.qT[:, j, :], env.bank(g), ACT.Copy, scale=DH ** -0.5).then_inc(env.proj_taken, 1)
        for j, (ld, g) in enumerate(self.kvc):
            env.split_hi(act, ld + 1)
            dst = (m.kcT, m.vcT)[j // 2]
            act.wait_ge(env.proj_ready, g + 1)
            for half in range(2):
                src = env.bank(g)[64 * half:64 * half + 64, :]
                grp = 2 * (j % 2) + half
                nc.scalar.activation(dst[0:64, grp, :], src, ACT.Copy)
                cp = nc.scalar.activation(dst[64:128, grp, 0:T - 1], src[:, 1:T], ACT.Copy)
            cp.then_inc(env.proj_taken, 1)
        for (keys, (lds, g)), (kT, v) in zip(self.branches, ((m.ksT, m.vs), (m.kwT, m.vw))):
            for j, (ld, gk) in enumerate(keys):
                env.split_hi(act, ld + 1)
                act.wait_ge(env.proj_ready, gk + 1)
                for half in range(2):
                    for to in range(2):
                        cp = nc.scalar.activation(kT[64 * to:64 * to + 64, 2 * j + half, :],
                                                  env.bank(gk)[64 * half:64 * half + 64, :], ACT.Copy)
                cp.then_inc(env.proj_taken, 1)
            env.split_hi(act, lds[-1] + 1)
            for i in range(NT):
                act.wait_ge(env.proj_ready, g + i + 1)
                nc.scalar.activation(v[:, i, :], env.bank(g + i)[:, 0:256], ACT.Copy).then_inc(env.proj_taken, 1)
        ld, g = self.gates
        env.split_hi(act, ld + 1)
        for i in range(NT):
            act.wait_ge(env.proj_ready, g + i + 1)
            nc.scalar.activation(m.gate[:, i, :], env.bank(g + i)[:, 0:3 * HEADS],
                                 ACT.Sigmoid).then_inc(env.proj_taken, 1)
        for k, (ld, g) in enumerate(self.z):
            env.split_hi(act, ld + 1)
            act.wait_ge(env.proj_ready, g + 1)
            nc.scalar.activation(m.z[:, k, :], env.bank(g), ACT.Silu).then_inc(env.proj_taken, 1)
        env.split_hi(act, self.z[-1][0] + 2)


class NsaCompress(Stage):

    def __init__(self, env, m):
        super().__init__(env)
        self.m = m
        self.aux = env.sem("cmp_weights")
        self.pe_rows_ready = env.sem("pe_cols_ready")
        self.pe_cols = env.sem("pe_cols_taken")
        self.hid_bias = env.sem("hid_bias")
        self.hid_bias_taken = env.sem("hid_bias_taken")
        self.hid_ready = env.sem("hid_ready")
        self.hid_taken = env.sem("hid_taken")
        self.cmp_ready = env.sem("cmp_ready")
        self.vbd_zeroed = env.sem("vbd_zeroed")

    def gpsimd(self, pool, step):
        env, m, io = self.env, self.m, self.env.io
        pool.dma_start(m.w1[0], io["nsa_cmp_w1_k"][0].rearrange("(k p) n -> p k n", p=P)).then_inc(self.aux, 16)
        pool.dma_start(m.w1[1], io["nsa_cmp_w1_v"][0].rearrange("(k p) n -> p k n", p=P)).then_inc(self.aux, 16)
        for to in range(2):
            pool.dma_start(m.w2[:, 64 * to:64 * to + 64], io["nsa_cmp_w2_k"][0]).then_inc(self.aux, 16)
        pool.dma_start(m.w2[:, 128:192], io["nsa_cmp_w2_v"][0]).then_inc(self.aux, 16)
        for kv, name in enumerate(("nsa_cmp_pe_k", "nsa_cmp_pe_v")):
            pool.dma_start(m.pe_rows[0:CMP_K, kv, :],
                           io[name][0].rearrange("(k two) d -> k (two d)", two=2)).then_inc(self.aux, 16)

    def tensor(self, pe):
        env, nc, m = self.env, self.env.nc, self.m
        pe.wait_ge(self.aux, 16 * 7)
        for kv in range(2):
            tr = nc.tensor.transpose(env.ps[:, 4, kv * CMP_K:(kv + 1) * CMP_K], m.pe_rows[0:CMP_K, kv, :],
                                     env.ident[0:CMP_K, 0:CMP_K])
        tr.then_inc(self.pe_rows_ready, 1)
        pe.wait_ge(self.pe_cols, 1)
        for kv in range(2):
            for k in range(CMP_K):
                mm = nc.tensor.matmul(env.ps[:, 5, 2 * kv:2 * kv + 2], m.w1[kv][:, k, :],
                                      m.pe_cols[:, kv * CMP_K + k:kv * CMP_K + k + 1].to_broadcast([P, 2]),
                                      start=(k == 0), stop=(k == CMP_K - 1))
        mm.then_inc(self.hid_bias, 1)
        for kv, src in enumerate((m.kcT, m.vcT)):
            for k in range(CMP_K):
                rhs = src[:, :, 2 * k:2 * k + CMP_STRIDE * (NC - 1) + 1:CMP_STRIDE]
                mm = nc.tensor.matmul(env.ps[:, 6 + kv, 0:GROUPS * NC], m.w1[kv][:, k, :], rhs,
                                      start=(k == 0), stop=(k == CMP_K - 1))
            mm.then_inc(self.hid_ready, 1)
        pe.wait_ge(self.hid_taken, 2)
        nc.tensor.matmul(env.ps[:, 4, 0:GROUPS * NC], m.w2[:, 0:128], m.hid[:, 0, 0:GROUPS * NC], start=True, stop=True)
        for g in range(GROUPS):
            mm = nc.tensor.matmul(env.ps[0:NC, 5, g * DH:(g + 1) * DH], m.hid[:, 1, g * NC:(g + 1) * NC],
                                  m.w2[:, 128:192], start=True, stop=True)
        mm.then_inc(self.cmp_ready, 1)

    def scalar(self, act, step):
        env, nc, m = self.env, self.env.nc, self.m
        act.wait_ge(self.hid_bias_taken, 1)
        for kv in range(2):
            act.wait_ge(self.hid_ready, kv + 1)
            nc.scalar.activation(m.hid[:, kv, 0:GROUPS * NC], env.ps[:, 6 + kv, 0:GROUPS * NC], ACT.Silu,
                                 bias=m.hid_bias[:, 2 * kv:2 * kv + 1]).then_inc(self.hid_taken, 1)

    def vector(self, dve, step):
        env, nc, m = self.env, self.env.nc, self.m
        nc.vector.memset(m.vbd, 0.0)
        step(nc.vector.memset(m.kcmp, 0.0))
        dve.wait_ge(self.pe_rows_ready, 1)
        nc.vector.tensor_copy(m.pe_cols, env.ps[:, 4, 0:2 * CMP_K]).then_inc(self.pe_cols, 1)
        dve.wait_ge(self.hid_bias, 1)
        nc.vector.tensor_copy(m.hid_bias, env.ps[:, 5, 0:4]).then_inc(self.hid_bias_taken, 1)
        dve.wait_ge(self.cmp_ready, 1)
        step(nc.vector.tensor_copy(m.kcmp[:, :, 0:NC], env.ps[:, 4, 0:GROUPS * NC].rearrange("p (g c) -> p g c", c=NC)))
        for j in range(HPG):
            step(nc.vector.tensor_copy(m.vbd[32 * j:32 * j + NC, :, DH * j:DH * j + DH],
                                       env.ps[0:NC, 5, 0:GROUPS * DH].rearrange("p (g d) -> p g d", d=DH)))


class NsaCompressed(Stage):

    def __init__(self, env, m):
        super().__init__(env)
        self.m = m
        self.bias_ready, self.bias_taken = env.sem("cbias_ready"), env.sem("cbias_taken")
        self.s_ready, self.s_taken = env.sem("cs_ready"), env.sem("cs_taken")
        self.shifted, self.p_ready, self.p_scaled = env.sem("c_shifted"), env.sem("cp_ready"), env.sem("cp_scaled")
        self.pT_ready, self.pT_taken = env.sem("cpT_ready"), env.sem("cpT_taken")
        self.o_ready, self.o_taken = env.sem("co_ready"), env.sem("co_taken")

    def tensor(self, pe):
        env, nc, m = self.env, self.env.nc, self.m
        for i in range(NT):
            if i:
                pe.wait_ge(self.bias_taken, i)
            out = env.ps[:, 6, :].rearrange("p (h c) -> p h c", c=NCP)
            for c in range(NCP):
                at = DIST0 + P * i - CMP_STRIDE * c - (CMP_BLOCK - 1)
                mm = nc.tensor.matmul(out[:, :, c], m.hot[:, at:at + P], m.table3[:], start=True, stop=True)
            mm.then_inc(self.bias_ready, 1)
            if i:
                pe.wait_ge(self.s_taken, i)
            for h in range(HEADS):
                half = 64 * (h % 2)
                mm = nc.tensor.matmul(env.ps[:, 7 - 5 * (h % 2), h // 2 * NCP:(h // 2 + 1) * NCP],
                                      m.qT[half:half + 64, h // 2, i * P:(i + 1) * P],
                                      m.kcmp[half:half + 64, h // HPG, :], start=True, stop=True)
            mm.then_inc(self.s_ready, 1)
            pe.wait_ge(self.p_scaled, i + 1)
            if i:
                pe.wait_ge(self.pT_taken, i)
            for g in range(GROUPS):
                tr = nc.tensor.transpose(env.ps[:, 5, g * P:(g + 1) * P], m.pc[:, g * P:(g + 1) * P], env.ident)
            tr.then_inc(self.pT_ready, 1)
            pe.wait_ge(self.pT_taken, i + 1)
            if i:
                pe.wait_ge(self.o_taken, i)
            for g in range(GROUPS):
                mm = nc.tensor.matmul(env.ps[:, 3 + g // 2, (g % 2) * 256:(g % 2) * 256 + 256],
                                      m.pcT[:, g * P:(g + 1) * P], m.vbd[:, g, :], start=True, stop=True)
            mm.then_inc(self.o_ready, 1)

    def gpsimd(self, pool, step):
        nc, m = self.env.nc, self.m
        nc.gpsimd.memset(m.q_odd[0:64], 0.0)
        step(nc.gpsimd.tensor_copy(m.q_odd[64:128], m.qT[64:128]))
        pool.wait_ge(self.s_ready, NT)
        nc.gpsimd.memset(m.qT[64:128], 0.0)

    def scalar(self, act, step):
        env, nc, m = self.env, self.env.nc, self.m
        for i in range(NT):
            act.wait_ge(self.shifted, i + 1)
            nc.scalar.activation(m.pc, m.sc, ACT.Exp).then_inc(self.p_ready, 1)
            act.wait_ge(self.o_ready, i + 1)
            nc.scalar.activation(m.o[:, i, :].rearrange("p (b n) -> p b n", b=2), env.ps[:, 3:5, :],
                                 ACT.Copy).then_inc(self.o_taken, 1)

    def vector(self, dve, step):
        env, nc, m = self.env, self.env.nc, self.m
        sc, pc = (v.rearrange("p (h c) -> p h c", c=NCP) for v in (m.sc, m.pc))
        col = m.cstat
        wide = lambda v: v.unsqueeze(2).to_broadcast([P, HEADS, NCP])
        for i in range(NT):
            dve.wait_ge(self.bias_ready, i + 1)
            nc.vector.tensor_copy(m.sc, env.ps[:, 6, :]).then_inc(self.bias_taken, 1)
            dve.wait_ge(self.bias_taken, i + 1)
            dve.wait_ge(self.s_ready, i + 1)
            for odd in range(2):
                part = m.sc.rearrange("p (h two c) -> p h two c", two=2, c=NCP)[:, :, odd, :]
                add = nc.vector.tensor_tensor(part, env.ps[:, 7 - 5 * odd, 0:256].rearrange("p (h c) -> p h c", c=NCP),
                                              part, ALU.add)
            add.then_inc(self.s_taken, 1)
            dve.wait_ge(self.s_taken, i + 1)
            step(nc.vector.tensor_reduce(col[:, 0, :], sc, AX, ALU.max))
            step(nc.vector.tensor_scalar(col[:, 0, :], col[:, 0, :], -1e20, None, ALU.max))
            nc.vector.tensor_tensor(sc, sc, wide(col[:, 0, :]), ALU.subtract).then_inc(self.shifted, 1)
            dve.wait_ge(self.p_ready, i + 1)
            step(nc.vector.tensor_reduce(col[:, 1, :], pc, AX, ALU.add))
            step(nc.vector.tensor_scalar(col[:, 1, :], col[:, 1, :], 1e-30, None, ALU.max))
            step(nc.vector.reciprocal(col[:, 2, :], col[:, 1, :]))
            gate = m.gate[:, i, :].rearrange("p (h b) -> p h b", b=3)[:, :, 0]
            step(nc.vector.tensor_tensor(col[:, 2, :], col[:, 2, :], gate, ALU.mult))
            nc.vector.tensor_tensor(pc, pc, wide(col[:, 2, :]), ALU.mult).then_inc(self.p_scaled, 1)
            dve.wait_ge(self.pT_ready, i + 1)
            nc.vector.tensor_copy(m.pcT, env.ps[:, 5, :]).then_inc(self.pT_taken, 1)


class Attend(Stage):

    def __init__(self, env, prefix):
        super().__init__(env)
        s = env.sem
        self.s_ready = s(prefix + "scores_ready")
        self.s_biased = s(prefix + "scores_biased")
        self.p_ready = s(prefix + "probs_ready")
        self.pT_ready = s(prefix + "probsT_ready")
        self.pT_copied = s(prefix + "probsT_copied")
        self.pv_done = s(prefix + "pv_done")
        self.o_taken = s(prefix + "o_taken")


class NsaAttend(Attend):

    def __init__(self, env, m):
        super().__init__(env, "nsa_")
        self.m = m
        self.o_added = env.sem("nsa_o_added")
        self.odd_copied = env.sem("nsa_odd_probsT_copied")
        self.units = [(i, g, br, j) for i in reversed(range(NT)) for g in range(GROUPS) for br in range(2) for j in range(HPG)]

    def tensor(self, pe):
        env, nc, m = self.env, self.env.nc, self.m
        n_units = len(self.units)

        def scores(u):
            i, g, br, j = self.units[u]
            h = HPG * g + j
            if u >= 3:
                pe.wait_ge(self.s_biased, u - 2)
            nc.tensor.matmul(env.ps[:, u % 3, 0:P * (i + 1)], (m.qT, m.q_odd)[h % 2][:, h // 2, i * P:(i + 1) * P],
                             (m.ksT, m.kwT)[br][:, g, 0:P * (i + 1)],
                             start=True, stop=True).then_inc(self.s_ready, 1)

        def turn(u):
            i = self.units[u][0]
            pe.wait_ge(self.p_ready, u + 1)
            if u >= 3:
                self.copied(pe, u - 3)
            for kt in range(i + 1):
                tr = nc.tensor.transpose(env.ps[:, 3 + u % 3, kt * P:(kt + 1) * P], m.p[:, u % 4, kt * P:(kt + 1) * P],
                                         env.ident)
            tr.then_inc(self.pT_ready, 1)

        def values(u):
            i, g, br, j = self.units[u]
            b = u // 8
            self.copied(pe, u)
            if u % 8 == 0 and b >= 2:
                pe.wait_ge(self.o_taken, b - 1)
            v = (m.vs, m.vw)[br]
            for kt in range(i + 1):
                mm = nc.tensor.matmul(env.ps[:, 6 + b % 2, (u % 8) * DH:(u % 8 + 1) * DH],
                                      m.pT[:, u % 3, kt * P:(kt + 1) * P], v[:, kt, g * DH:(g + 1) * DH],
                                      start=(kt == 0), stop=(kt == i))
            mm.then_inc(self.pv_done, 1)

        for _ in range(WARM_UP):
            nc.tensor.matmul(env.ps[:, 7, :], m.hot[:, 0:P], m.hot[:, 0:512], start=True, stop=True)
        for u in range(n_units + 3):
            if u < n_units:
                scores(u)
            if 2 <= u <= n_units + 1:
                turn(u - 2)
            if u >= 3:
                values(u - 3)

    def copied(self, eng, u):
        if u % 2:
            eng.wait_ge(self.odd_copied, u // 2 + 1)
        else:
            eng.wait_ge(self.pT_copied, u // 2 + 1)

    def scalar(self, act, step):
        env, nc, m = self.env, self.env.nc, self.m
        n_units = len(self.units)

        def exp(u):
            n, b = P * (self.units[u][0] + 1), u // 8
            act.wait_ge(self.s_biased, u + 1)
            if u % 8 == 0 and b >= 2:
                act.wait_ge(self.o_taken, b - 1)
            nc.scalar.activation(m.p[:, u % 4, 0:n], m.p[:, u % 4, 0:n], ACT.Exp, scale=-1.0,
                                 bias=m.nmax[:, u % 16:u % 16 + 1],
                                 accum_out=m.psum[:, u % 16:u % 16 + 1]).then_inc(self.p_ready, 1)

        def copy(u):
            n = P * (self.units[u][0] + 1)
            act.wait_ge(self.pT_ready, u + 1)
            if u >= 3:
                act.wait_ge(self.pv_done, u - 2)
            nc.scalar.activation(m.pT[:, u % 3, 0:n], env.ps[:, 3 + u % 3, 0:n], ACT.Copy).then_inc(self.odd_copied, 1)

        for u in range(n_units + 2):
            if u >= 2 and u % 2:
                copy(u - 2)
            if u < n_units:
                exp(u)

    def gpsimd(self, pool, step):
        nc, m = self.env.nc, self.m
        for b in range(len(self.units) // 8):
            i, g = self.units[8 * b][0:2]
            o = m.o[:, i, 256 * g:256 * g + 256]
            pool.wait_ge(self.o_taken, b + 1)
            step(nc.gpsimd.tensor_tensor(o, o, m.otmp[:, 0:256], ALU.add))
            nc.gpsimd.tensor_tensor(o, o, m.otmp[:, 256:512], ALU.add).then_inc(self.o_added, 1)

    def vector(self, dve, step):
        env, nc, m = self.env, self.env.nc, self.m
        n_units = len(self.units)

        def bias(u):
            i, g, br, j = self.units[u]
            n = P * (i + 1)
            dve.wait_ge(self.s_ready, u + 1)
            if u >= 4:
                dve.wait_ge(self.pT_ready, u - 3)
            nc.vector.tensor_tensor_reduce(m.p[:, u % 4, 0:n], env.ps[:, u % 3, 0:n], m.bias[:, HPG * g + j, T - n:T],
                                           -1.0, 1e38, ALU.add, ALU.min,
                                           m.nmax[:, u % 16:u % 16 + 1]).then_inc(self.s_biased, 1)

        def copy(u):
            n = P * (self.units[u][0] + 1)
            dve.wait_ge(self.pT_ready, u + 1)
            if u >= 3:
                dve.wait_ge(self.pv_done, u - 2)
            nc.vector.tensor_copy(m.pT[:, u % 3, 0:n], env.ps[:, 3 + u % 3, 0:n]).then_inc(self.pT_copied, 1)

        def combine(b):
            i, g = self.units[8 * b][0:2]
            dve.wait_ge(self.pv_done, 8 * b + 8)
            at = 8 * (b % 2)
            step(nc.vector.reciprocal(m.scale[:, 0:8], m.psum[:, at:at + 8]))
            gate = m.gate[:, i, 12 * g:12 * g + 12].rearrange("p (j b) -> p b j", b=3)[:, 1:3, :]
            sc = m.scale[:, 0:8].rearrange("p (b j) -> p b j", b=2)
            step(nc.vector.tensor_tensor(sc, sc, gate, ALU.mult))
            if b:
                dve.wait_ge(self.o_added, b)
            nc.vector.tensor_tensor(m.otmp.rearrange("p (u d) -> p u d", d=DH),
                                    env.ps[:, 6 + b % 2, :].rearrange("p (u d) -> p u d", d=DH),
                                    m.scale[:, 0:8].unsqueeze(2).to_broadcast([P, 8, DH]),
                                    ALU.mult).then_inc(self.o_taken, 1)

        for u in range(n_units + 5):
            if u < n_units:
                bias(u)
            if 2 <= u <= n_units + 1 and u % 2 == 0:
                copy(u - 2)
            if u >= 12 and (u - 4) % 8 == 0:
                combine((u - 4) // 8 - 1)


class NsaMemory:
    def __init__(self, env, bias, setup):
        at = env.area

        def take(*shape):
            nonlocal at
            v = env.take(*shape, at=at)
            at += int(np.prod(shape))
            return v
        self.bias = bias
        self.hot, self.table3 = setup.hot, setup.table3
        self.qT = take(KD, T)
        self.ksT, self.kwT = take(GROUPS, T), take(GROUPS, T)
        self.z = take(KD, T)
        lo_at = at
        at += KD * T
        self.vs, self.vw = take(NT, 256), take(NT, 256)
        assert at <= env.words - HEADS * T
        at = lo_at
        self.u = [env.take_r("nsa_u_hi", KD, T, at=env.uT_at), env.take_r("nsa_u_lo", KD, T, at=lo_at)]
        w1 = Area(env, env.uT_at)
        self.w1 = [w1(CMP_K, P), w1(CMP_K, P)]
        self.sc, self.pc = take(512), take(512)
        self.pcT = take(512)
        self.vbd = take(GROUPS, 256)
        self.kcmp = take(GROUPS, NCP)
        self.hid = take(2, P)
        self.w2 = take(192)
        self.pe_rows = take(2, P)
        self.pe_cols = take(2 * CMP_K)
        self.hid_bias = take(4)
        assert at <= lo_at + KD * T
        at = lo_at
        self.p, self.pT, self.otmp = take(4, 512), take(3, 512), take(512)
        assert at <= lo_at + KD * T
        self.q_odd = env.take(KD, T, at=env.uT_at)
        small = Area(env, env.gates_at)
        self.gate = small(NT, 3 * HEADS)
        self.cstat = small(3, HEADS)
        self.nmax, self.psum, self.scale = small(16), small(16), small(16)
        self.kcT = env.big[:, 0:2048].rearrange("p (g t) -> p g t", g=GROUPS)
        self.vcT = env.big[:, 2048:4096].rearrange("p (g t) -> p g t", g=GROUPS)
        self.o = env.big.rearrange("p (t d) -> p t d", t=NT)


class Area:

    def __init__(self, env, at=None):
        self.env, self.at = env, env.area if at is None else at

    def __call__(self, *shape):
        v = self.env.take(*shape, at=self.at)
        n = int(np.prod(shape))
        self.at += n + -n % 8
        return v


class DiffMemory:
    def __init__(self, env, bias):
        take = Area(env)
        self.bias = bias
        self.qT, self.kT, self.v = take(KD, T), take(KD, T), take(NT, D)
        self.u = [env.take_r("diff_u_hi", KD, T, at=env.uT_at), env.take_r("diff_u_lo", KD, T, at=take.at)]
        self.oT = [env.take_r("diff_o_hi", KD, T, at=env.area), env.take_r("diff_o_lo", KD, T, at=env.area + KD * T)]
        self.z = env.big.rearrange("p (k t) -> p k t", k=KD)
        self.sq = env.take(D, at=take.at)
        self.p, self.pT = take(6, 512), take(2, 512)
        assert take.at <= env.words - HEADS * T, take.at
        self.o = env.uT.rearrange("p k t -> p (k t)").rearrange("p (t d) -> p t d", t=NT)
        small = Area(env, env.gates_at)
        self.dots, self.exps, self.lam = small(2), small(2), small(1)
        self.nmax, self.psum, self.scale, self.inv = small(6), small(6), small(6), small(8)
        self.nstat = small(2, DIFF_HEADS)
        self.lq, self.lprod = env.junk[:, 0:4 * DH].rearrange("p (a b) -> p a b", a=4), env.junk[:, 4 * DH:5 * DH]


class DiffProject(Stage):

    def __init__(self, env, m):
        super().__init__(env)
        self.m = m
        w = env.io["diff_w_in"][0]
        self.qk = load_features(env, w, 0, 2 * D)
        self.v = load_tokens(env, w, 2 * D, D)
        self.z = load_features(env, w, 3 * D, D)
        self.lq_arrived = env.sem("lq_arrived")
        self.dots_ready, self.exps_ready = env.sem("lambda_dots"), env.sem("lambda_exps")

    def gpsimd(self, pool, step):
        for n, name in enumerate(("q1", "k1", "q2", "k2")):
            pool.dma_start(self.m.lq[:, n, :],
                           self.env.io["diff_lambda_" + name][0].partition_broadcast(P)).then_inc(self.lq_arrived, 16)
        self.env.split_lo(pool, self.z[-1][0] + 2)

    def tensor(self, pe):
        env, u = self.env, self.m.u
        for ld, g in self.qk:
            project_features(env, pe, ld, u, g)
        lds, g = self.v
        project_tokens(env, pe, lds, u, g)
        for ld, g in self.z:
            project_features(env, pe, ld, u, g)

    def scalar(self, act, step):
        env, nc, m = self.env, self.env.nc, self.m
        env.split_hi(act, self.qk[0][0])
        for j, (ld, g) in enumerate(self.qk):
            env.split_hi(act, ld + 1)
            act.wait_ge(env.proj_ready, g + 1)
            nc.scalar.activation((m.qT, m.kT)[j // KD][:, j % KD, :], env.bank(g), ACT.Copy,
                                 scale=DH ** -0.5 if j < KD else 1.0).then_inc(env.proj_taken, 1)
        lds, g = self.v
        env.split_hi(act, lds[-1] + 1)
        for n in range(2 * NT):
            act.wait_ge(env.proj_ready, g + n + 1)
            nc.scalar.activation(m.v[:, n // 2, 512 * (n % 2):512 * (n % 2) + 512], env.ps[:, n, :],
                                 ACT.Copy).then_inc(env.proj_taken, 1)
        for k, (ld, g) in enumerate(self.z):
            env.split_hi(act, ld + 1)
            act.wait_ge(env.proj_ready, g + 1)
            nc.scalar.activation(m.z[:, k, :], env.bank(g), ACT.Silu).then_inc(env.proj_taken, 1)
        env.split_hi(act, self.z[-1][0] + 2)
        act.wait_ge(self.dots_ready, 1)
        nc.scalar.activation(m.exps, m.dots, ACT.Exp).then_inc(self.exps_ready, 1)

    def vector(self, dve, step):
        nc, m = self.env.nc, self.m
        dve.wait_ge(self.lq_arrived, 64)
        step(nc.vector.tensor_tensor_reduce(m.lprod, m.lq[:, 0, :], m.lq[:, 1, :], 1.0, 0.0, ALU.mult, ALU.add,
                                            m.dots[:, 0:1]))
        nc.vector.tensor_tensor_reduce(m.lprod, m.lq[:, 2, :], m.lq[:, 3, :], 1.0, 0.0, ALU.mult, ALU.add,
                                       m.dots[:, 1:2]).then_inc(self.dots_ready, 1)
        dve.wait_ge(self.exps_ready, 1)
        step(nc.vector.tensor_tensor(m.lam, m.exps[:, 1:2], m.exps[:, 0:1], ALU.subtract))
        step(nc.vector.tensor_scalar(m.lam, m.lam, -LAMBDA_INIT, None, ALU.add))


class DiffAttend(Attend):

    def __init__(self, env, m):
        super().__init__(env, "diff_")
        self.m = m
        self.a_ready = env.sem("diff_combined")
        self.units = [(i, h) for i in reversed(range(NT)) for h in range(DIFF_HEADS)]

    def tensor(self, pe):
        env, nc, m = self.env, self.env.nc, self.m
        n_units = len(self.units)

        def scores(u):
            i, h = self.units[u]
            if u >= 2:
                pe.wait_ge(self.s_biased, 2 * (u - 1))
            for mp in range(2):
                q = slice(64 * mp, 64 * mp + 64)
                nc.tensor.matmul(env.ps[:, 2 * (u % 2) + mp, 0:P * (i + 1)], m.qT[q, h, i * P:(i + 1) * P],
                                 m.kT[q, h, 0:P * (i + 1)], start=True, stop=True).then_inc(self.s_ready, 1)

        def turn(u):
            i = self.units[u][0]
            pe.wait_ge(self.a_ready, u + 1)
            if u >= 2:
                pe.wait_ge(self.pT_copied, u - 1)
            for kt in range(i + 1):
                tr = nc.tensor.transpose(env.ps[:, 4 + u % 2, kt * P:(kt + 1) * P],
                                         m.p[:, 2 * (u % 3), kt * P:(kt + 1) * P], env.ident)
            tr.then_inc(self.pT_ready, 1)

        def values(u):
            i, h = self.units[u]
            b = u // 4
            pe.wait_ge(self.pT_copied, u + 1)
            if u % 4 == 0 and b >= 2:
                pe.wait_ge(self.o_taken, b - 1)
            for kt in range(i + 1):
                mm = nc.tensor.matmul(env.ps[:, 6 + b % 2, (u % 4) * P:(u % 4 + 1) * P],
                                      m.pT[:, u % 2, kt * P:(kt + 1) * P], m.v[:, kt, h * P:(h + 1) * P],
                                      start=(kt == 0), stop=(kt == i))
            mm.then_inc(self.pv_done, 1)

        for u in range(n_units + 3):
            if u < n_units:
                scores(u)
            if 2 <= u <= n_units + 1:
                turn(u - 2)
            if u >= 3:
                values(u - 3)

    def scalar(self, act, step):
        env, nc, m = self.env, self.env.nc, self.m
        n_units = len(self.units)

        def exps(u):
            n = P * (self.units[u][0] + 1)
            for mp in range(2):
                act.wait_ge(self.s_biased, 2 * u + mp + 1)
                at = 2 * (u % 3) + mp
                nc.scalar.activation(m.p[:, at, 0:n], m.p[:, at, 0:n], ACT.Exp, scale=-1.0, bias=m.nmax[:, at:at + 1],
                                     accum_out=m.psum[:, at:at + 1]).then_inc(self.p_ready, 1)

        def copy(u):
            n = P * (self.units[u][0] + 1)
            act.wait_ge(self.pT_ready, u + 1)
            if u >= 2:
                act.wait_ge(self.pv_done, u - 1)
            nc.scalar.activation(m.pT[:, u % 2, 0:n], env.ps[:, 4 + u % 2, 0:n], ACT.Copy).then_inc(self.pT_copied, 1)

        for u in range(n_units + 2):
            if u < n_units:
                exps(u)
            if u >= 2:
                copy(u - 2)

    def vector(self, dve, step):
        env, nc, m = self.env, self.env.nc, self.m
        n_units = len(self.units)

        def bias(u):
            i, h = self.units[u]
            n = P * (i + 1)
            if u >= 3:
                dve.wait_ge(self.pT_ready, u - 2)
            for mp in range(2):
                bank, at = 2 * (u % 2) + mp, 2 * (u % 3) + mp
                dve.wait_ge(self.s_ready, 2 * u + mp + 1)
                nc.vector.tensor_tensor_reduce(m.p[:, at, 0:n], env.ps[:, bank, 0:n], m.bias[:, 2 * h + mp, T - n:T],
                                               -1.0, 1e38, ALU.add, ALU.min,
                                               m.nmax[:, at:at + 1]).then_inc(self.s_biased, 1)

        def combine(u):
            n, at = P * (self.units[u][0] + 1), 2 * (u % 3)
            dve.wait_ge(self.p_ready, 2 * u + 2)
            sums, r = m.psum[:, at:at + 2], m.scale[:, at:at + 2]
            step(nc.vector.reciprocal(r, sums))
            nc.vector.tensor_copy(m.inv[:, u % 8:u % 8 + 1], r[:, 0:1])
            step(nc.vector.scalar_tensor_tensor(r[:, 1:2], r[:, 1:2], m.lam, sums[:, 0:1], ALU.mult, ALU.mult))
            nc.vector.scalar_tensor_tensor(m.p[:, at, 0:n], m.p[:, at + 1, 0:n], r[:, 1:2], m.p[:, at, 0:n],
                                           ALU.mult, ALU.add).then_inc(self.a_ready, 1)

        def take(b):
            dve.wait_ge(self.pv_done, 4 * b + 4)
            nc.vector.tensor_tensor(
                m.o[:, self.units[4 * b][0], 512 * (b % 2):512 * (b % 2) + 512].rearrange("p (u d) -> p u d", d=P),
                env.ps[:, 6 + b % 2, :].rearrange("p (u d) -> p u d", d=P),
                m.inv[:, 4 * (b % 2):4 * (b % 2) + 4].unsqueeze(2).to_broadcast([P, 4, P]),
                ALU.mult).then_inc(self.o_taken, 1)

        for u in range(n_units + 4):
            if u < n_units:
                bias(u)
            if u >= 7 and (u - 3) % 4 == 0:
                take((u - 3) // 4 - 1)
            if 1 <= u <= n_units:
                combine(u - 1)


class DiffNorm(Stage):

    def __init__(self, env, m):
        super().__init__(env)
        self.m = m
        self.row_arrived = env.sem("subln_arrived")
        self.ms_ready, self.rstd_ready = env.sem("subln_ms"), env.sem("subln_rstd")

    def gpsimd(self, pool, step):
        env = self.env
        pool.dma_start(env.grow, env.io["diff_subln"][0].partition_broadcast(P)).then_inc(self.row_arrived, 16)

    def scalar(self, act, step):
        nc, m = self.env.nc, self.m
        for i in range(NT):
            act.wait_ge(self.ms_ready, i + 1)
            nc.scalar.activation(m.nstat[:, 1, :], m.nstat[:, 0, :], ACT.Sqrt).then_inc(self.rstd_ready, 1)

    def vector(self, dve, step):
        env, nc, m = self.env, self.env.nc, self.m
        c2 = (1.0 - LAMBDA_INIT) ** 2
        wide = m.nstat[:, 1, :].unsqueeze(2).to_broadcast([P, DIFF_HEADS, P])
        dve.wait_ge(self.row_arrived, 16)
        for i in range(NT):
            o = m.o[:, i, :]
            step(nc.vector.tensor_tensor(m.sq, o, o, ALU.mult))
            step(nc.vector.tensor_reduce(m.nstat[:, 0, :], m.sq.rearrange("p (h d) -> p h d", d=P), AX, ALU.add))
            step(nc.vector.tensor_scalar(m.nstat[:, 0, :], m.nstat[:, 0, :], 1.0 / (P * c2), EPS / c2, ALU.mult, ALU.add))
            nc.vector.reciprocal(m.nstat[:, 0, :], m.nstat[:, 0, :]).then_inc(self.ms_ready, 1)
            dve.wait_ge(self.rstd_ready, i + 1)
            step(nc.vector.tensor_tensor(o.rearrange("p (h d) -> p h d", d=P), o.rearrange("p (h d) -> p h d", d=P),
                                         wide, ALU.mult))
            step(nc.vector.tensor_tensor(o, o, env.grow, ALU.mult))


class FfnUp(Stage):

    def __init__(self, env, layer, m):
        super().__init__(env)
        self.layer, self.m = layer, m
        w = env.io["w_up_2"][layer]
        self.lds = []
        self.g0 = env.groups
        for j in range(FT):
            for half in range(2):
                self.lds += [ld for ld, _ in load_features(env, w, half * D_FF + j * P, P)]
        n = str(layer)
        self.scaled = env.sem("up_scaled" + n)
        self.gelu_done, self.product_ready = env.sem("gelu_done" + n), env.sem("product_ready" + n)
        self.act_hi_ready, self.act_done = env.sem("act_hi_ready" + n), env.sem("act_done" + n)

    def tensor(self, pe):
        env, nc = self.env, self.env.nc
        for n, ld in enumerate(self.lds):
            project_features(env, pe, ld, self.m.u, self.g0 + n)

    def col(self, which, half, j):
        at = V_CONV + 176 * self.layer + 44 * which + FT * half + j
        return self.env.vec[:, at:at + 1]

    def gpsimd(self, pool, step):
        self.env.split_lo(pool, self.lds[-1] + 2)

    def scalar(self, act, step):
        env, nc, m = self.env, self.env.nc, self.m

        def gelu(j):
            act.wait_ge(env.proj_taken, self.g0 + 2 * j + 2)
            if j >= 2:
                act.wait_ge(self.act_done, j - 1)
            nc.scalar.activation(m.gelu[:, j % 2, :], m.conv[:, 2 * (j % 2), :], ACT.Gelu_apprx_tanh).then_inc(self.gelu_done, 1)

        def act_hi(j):
            act.wait_ge(self.product_ready, j + 1)
            nc.scalar.activation(m.act[0][:, j, :], m.gelu[:, j % 2, :], ACT.Copy).then_inc(self.act_hi_ready, 1)

        env.split_hi(act, self.lds[0])
        for j in range(FT):
            for half in range(2):
                n = 2 * j + half
                env.split_hi(act, self.lds[n] + 1)
                g = self.g0 + n
                act.wait_ge(env.proj_ready, g + 1)
                if j >= 2:
                    act.wait_ge(self.product_ready, j - 1)
                nc.scalar.activation(m.conv[:, 2 * (j % 2) + half, :], env.bank(g), ACT.Identity,
                                     scale=self.col(2, half, j), bias=self.col(3, half, j)).then_inc(self.scaled, 1)
            if j:
                gelu(j - 1)
            if j >= 2:
                act_hi(j - 2)
        gelu(FT - 1)
        act_hi(FT - 2)
        env.split_hi(act, self.lds[-1] + 2)
        act_hi(FT - 1)

    def vector(self, dve, step):
        env, nc, m = self.env, self.env.nc, self.m

        def multiply(j):
            dve.wait_ge(self.gelu_done, j + 1)
            dve.wait_ge(env.proj_taken, self.g0 + 2 * j + 2)
            nc.vector.tensor_tensor(m.gelu[:, j % 2, :], m.gelu[:, j % 2, :], m.conv[:, 2 * (j % 2) + 1, :],
                                    ALU.mult).then_inc(self.product_ready, 1)

        def act_lo(j):
            dve.wait_ge(self.act_hi_ready, j + 1)
            nc.vector.tensor_tensor(m.act[1][:, j, :], m.gelu[:, j % 2, :], m.act[0][:, j, :].bitcast(F32),
                                    ALU.subtract).then_inc(self.act_done, 1)

        for j in range(FT):
            for half in range(2):
                g = self.g0 + 2 * j + half
                c = m.conv[:, 2 * (j % 2) + half, :]
                dve.wait_ge(self.scaled, 2 * j + half + 1)
                step(nc.vector.scalar_tensor_tensor(c[:, 1:T], env.bank(g)[:, 0:T - 1], self.col(1, half, j), c[:, 1:T],
                                                    ALU.mult, ALU.add))
                nc.vector.scalar_tensor_tensor(c[:, 2:T], env.bank(g)[:, 0:T - 2], self.col(0, half, j), c[:, 2:T],
                                               ALU.mult, ALU.add).then_inc(env.proj_taken, 1)
            if j:
                multiply(j - 1)
            if j >= 2:
                act_lo(j - 2)
        multiply(FT - 1)
        act_lo(FT - 2)
        act_lo(FT - 1)


class FfnMemory:

    def __init__(self, env):
        at = env.area
        self.act = [env.take_r("act_hi", FT, T, at=at), env.take_r("act_lo", FT, T, at=at + FT * T)]
        self.u = [env.take_r("u_hi", KD, T, at=env.uT_at), env.take_r("u_lo", KD, T, at=at + 2 * FT * T)]
        assert at + 2 * FT * T + KD * T <= env.words
        take = Area(env, env.big_at)
        self.conv, self.gelu = take(4, 512), take(2, 512)


class SwaMemory:
    def __init__(self, env):
        take = Area(env)
        lo_at = env.area + 2 * FT * T
        self.u = [env.take_r("swa_u_hi", KD, T, at=env.uT_at), env.take_r("swa_u_lo", KD, T, at=lo_at)]
        self.kT, self.v = take(GROUPS, T), take(NT, 256)
        self.q = [take(KD, T), take(KD, T)]
        self.s, self.p, self.pT = take(3, 256), take(3, 256), take(3, 256)
        self.sinks, self.nsinks = take(HEADS), take(HEADS)
        self.nmax, self.psum, self.esink, self.scale = take(16), take(16), take(16), take(16)
        self.o = env.big.rearrange("p (t d) -> p t d", t=NT)


class KvProject(Stage):

    def __init__(self, env, m, g_row):
        super().__init__(env)
        self.again = Renorm(env, g_row, m.u)
        env.repeats += 1
        self.m = m
        width = GROUPS * DH
        self.keys = load_features(env, env.io["w_kv_2"], 0, width)
        self.values = load_tokens(env, env.io["w_kv_2"], width, width)

    def tensor(self, pe):
        env = self.env
        for ld, g in self.keys:
            project_features(env, pe, ld, self.m.u, g)
        project_tokens(env, pe, self.values[0], self.m.u, self.values[1])

    def gpsimd(self, pool, step):
        self.again.fetch(pool)
        self.env.split_lo(pool, self.values[0][-1] + 2)

    def vector(self, dve, step):
        for i in range(NT):
            self.again.scale(dve, step, i, again=True)

    def scalar(self, act, step):
        env, nc, m = self.env, self.env.nc, self.m
        env.split_hi(act, self.keys[0][0])
        for j, (ld, g) in enumerate(self.keys):
            env.split_hi(act, ld + 1)
            act.wait_ge(env.proj_ready, g + 1)
            for half in range(2):
                for to in range(2):
                    cp = nc.scalar.activation(m.kT[64 * to:64 * to + 64, 2 * j + half, :],
                                              env.bank(g)[64 * half:64 * half + 64, :], ACT.Copy)
            cp.then_inc(env.proj_taken, 1)
        lds, g = self.values
        env.split_hi(act, lds[-1] + 1)
        for i in range(NT):
            act.wait_ge(env.proj_ready, g + i + 1)
            nc.scalar.activation(m.v[:, i, :], env.bank(g + i)[:, 0:256], ACT.Copy).then_inc(env.proj_taken, 1)
        env.split_hi(act, lds[-1] + 2)


class SwaProject(Stage):
    def __init__(self, env, m):
        super().__init__(env)
        self.m = m
        self.q = load_features(env, env.io["w_q_2"][0], 0, D)
        self.sinks_arrived = env.sem("sinks_arrived")

    def gpsimd(self, pool, step):
        pool.dma_start(self.m.sinks, self.env.io["sinks_2"][0].partition_broadcast(P)).then_inc(self.sinks_arrived, 16)
        self.env.split_lo(pool, self.q[-1][0] + 2)

    def tensor(self, pe):
        for ld, g in self.q:
            project_features(self.env, pe, ld, self.m.u, g)

    def scalar(self, act, step):
        env, nc = self.env, self.env.nc
        env.split_hi(act, self.q[0][0])
        for j, (ld, g) in enumerate(self.q):
            env.split_hi(act, ld + 1)
            act.wait_ge(env.proj_ready, g + 1)
            for odd in range(2):
                rows = slice(64 * odd, 64 * odd + 64)
                cp = nc.scalar.activation(self.m.q[odd][rows, j, :], env.bank(g)[rows], ACT.Copy, scale=DH ** -0.5)
            cp.then_inc(env.proj_taken, 1)
        env.split_hi(act, self.q[-1][0] + 2)

    def vector(self, dve, step):
        self.env.nc.vector.memset(self.m.q[0][64:128], 0.0)
        self.env.nc.vector.memset(self.m.q[1][0:64], 0.0)
        dve.wait_ge(self.sinks_arrived, 16)
        step(self.env.nc.vector.tensor_scalar(self.m.nsinks, self.m.sinks, -1.0, None, ALU.mult))


class SwaAttend(Attend):

    def __init__(self, env, m):
        super().__init__(env, "swa_")
        self.m = m
        self.esum_ready, self.esink_ready = env.sem("sink_shifted"), env.sem("sink_exp")
        self.units = [(i, h) for i in reversed(range(NT)) for h in range(HEADS)]

    def tensor(self, pe):
        env, nc, m = self.env, self.env.nc, self.m
        n_units = len(self.units)

        def scores(u):
            i, h = self.units[u]
            lo = max(i - 1, 0)
            if u >= 3:
                pe.wait_ge(self.s_biased, u - 2)
            nc.tensor.matmul(env.ps[:, u % 3, 0:P * (i + 1 - lo)], m.q[h % 2][:, h // 2, i * P:(i + 1) * P],
                             m.kT[:, h // HPG, P * lo:P * (i + 1)],
                             start=True, stop=True).then_inc(self.s_ready, 1)

        def turn(u):
            i = self.units[u][0]
            pe.wait_ge(self.p_ready, u + 1)
            if u >= 3:
                pe.wait_ge(self.pT_copied, u - 2)
            for kt in range(1 + (i > 0)):
                tr = nc.tensor.transpose(env.ps[:, 3 + u % 3, kt * P:(kt + 1) * P], m.p[:, u % 3, kt * P:(kt + 1) * P],
                                         env.ident)
            tr.then_inc(self.pT_ready, 1)

        def values(u):
            i, h = self.units[u]
            b, g, lo = u // 8, h // HPG, max(i - 1, 0)
            pe.wait_ge(self.pT_copied, u + 1)
            if u % 8 == 0 and b >= 2:
                pe.wait_ge(self.o_taken, b - 1)
            for kt in range(lo, i + 1):
                mm = nc.tensor.matmul(env.ps[:, 6 + b % 2, (u % 8) * DH:(u % 8 + 1) * DH],
                                      m.pT[:, u % 3, (kt - lo) * P:(kt - lo + 1) * P], m.v[:, kt, g * DH:(g + 1) * DH],
                                      start=(kt == lo), stop=(kt == i))
            mm.then_inc(self.pv_done, 1)

        for u in range(n_units + 3):
            if u < n_units:
                scores(u)
            if 2 <= u <= n_units + 1:
                turn(u - 2)
            if u >= 3:
                values(u - 3)

    def scalar(self, act, step):
        env, nc, m = self.env, self.env.nc, self.m
        n_units = len(self.units)

        def exp(u):
            n, b = P * (1 + (self.units[u][0] > 0)), u // 8
            act.wait_ge(self.s_biased, u + 1)
            if u >= 3:
                act.wait_ge(self.pT_ready, u - 2)
            if u % 8 == 0 and b >= 2:
                act.wait_ge(self.o_taken, b - 1)
            nc.scalar.activation(m.p[:, u % 3, 0:n], m.s[:, u % 3, 0:n], ACT.Exp, scale=-1.0,
                                 bias=m.nmax[:, u % 16:u % 16 + 1],
                                 accum_out=m.psum[:, u % 16:u % 16 + 1]).then_inc(self.p_ready, 1)

        for u in range(n_units + 5):
            if u < n_units:
                exp(u)
            if u >= 12 and (u - 4) % 8 == 0:
                b = (u - 4) // 8 - 1
                at = 8 * (b % 2)
                act.wait_ge(self.esum_ready, b + 1)
                nc.scalar.activation(m.esink[:, at:at + 8], m.esink[:, at:at + 8], ACT.Exp).then_inc(self.esink_ready, 1)

    def vector(self, dve, step):
        env, nc, m = self.env, self.env.nc, self.m
        n_units = len(self.units)
        band = env.const[:, C_BAND:C_BAND + 2 * P]

        def bias(u):
            i, h = self.units[u]
            n = P * (1 + (i > 0))
            dve.wait_ge(self.s_ready, u + 1)
            if u >= 3:
                dve.wait_ge(self.p_ready, u - 2)
            nc.vector.tensor_tensor_reduce(m.s[:, u % 3, 0:n], env.ps[:, u % 3, 0:n], band[:, 2 * P - n:2 * P],
                                           -1.0, m.nsinks[:, h:h + 1], ALU.add, ALU.min,
                                           m.nmax[:, u % 16:u % 16 + 1]).then_inc(self.s_biased, 1)

        def copy(u):
            n = P * (1 + (self.units[u][0] > 0))
            dve.wait_ge(self.pT_ready, u + 1)
            if u >= 3:
                dve.wait_ge(self.pv_done, u - 2)
            nc.vector.tensor_copy(m.pT[:, u % 3, 0:n], env.ps[:, 3 + u % 3, 0:n]).then_inc(self.pT_copied, 1)

        def combine(b):
            at, h0 = 8 * (b % 2), 8 * (b % 2)
            dve.wait_ge(self.s_biased, 8 * b + 8)
            nc.vector.tensor_tensor(m.esink[:, at:at + 8], m.nmax[:, at:at + 8], m.sinks[:, h0:h0 + 8],
                                    ALU.add).then_inc(self.esum_ready, 1)
            dve.wait_ge(self.esink_ready, b + 1)
            step(nc.vector.tensor_tensor(m.scale[:, at:at + 8], m.psum[:, at:at + 8], m.esink[:, at:at + 8], ALU.add))
            step(nc.vector.reciprocal(m.scale[:, at:at + 8], m.scale[:, at:at + 8]))
            dve.wait_ge(self.pv_done, 8 * b + 8)
            nc.vector.tensor_tensor(m.o[:, self.units[8 * b][0], 512 * (b % 2):512 * (b % 2) + 512].rearrange("p (u d) -> p u d", d=DH),
                                    env.ps[:, 6 + b % 2, :].rearrange("p (u d) -> p u d", d=DH),
                                    m.scale[:, at:at + 8].unsqueeze(2).to_broadcast([P, 8, DH]),
                                    ALU.mult).then_inc(self.o_taken, 1)

        for u in range(n_units + 5):
            if u < n_units:
                bias(u)
            if 2 <= u <= n_units + 1:
                copy(u - 2)
            if u >= 12 and (u - 4) % 8 == 0:
                combine((u - 4) // 8 - 1)


class RwkvMemory:

    def __init__(self, env):
        take = Area(env)
        self.r, self.k, self.a, self.kk = take(KD, T), take(KD, T), take(KD, T), take(KD, T)
        self.v = take(NT, D)
        l_at = take.at
        self.decay = take(KD, T)
        self.xx = self.decay
        hid = Area(env, l_at + KD * T)
        self.tanh_w, self.hid_a = hid(T), hid(T)
        a_at = env.area + 2 * KD * T
        self.mixes = [[env.take_r("mix0_hi", KD, T, at=env.big_at), env.take_r("mix0_lo", KD, T, at=a_at + 2 * KD * T)],
                      [env.take_r("mix1_hi", KD, T, at=a_at), env.take_r("mix1_lo", KD, T, at=a_at + KD * T)]]
        self.oT = [env.take_r("rwkv_o_hi", KD, T, at=env.uT_at), env.take_r("rwkv_o_lo", KD, T, at=a_at)]
        core1 = Area(env, l_at)
        u_at = 4096
        core0 = Area(env, u_at)
        self.streams = []
        for take in (core0, core1):
            st = {}
            for name in ("abT", "X", "XT", "Y", "akT", "rbT", "rkT"):
                st[name] = take(4, P)
            st["MT"] = [take(4, P), take(4, P)]
            st["Z"], st["SA"] = take(4, DH), take(4, DH)
            self.streams.append(st)
        self.tok = core0(3, 4, P)
        self.WT = core0(4, P)
        self.S = core0(KD, DH)
        assert core0.at <= u_at + 8192, core0.at
        take = Area(env, core1.at)
        self.sg = take(2, T)
        take = Area(env, env.stat_at + 64)
        self.coef = take(KD, NT)
        self.bonus = take(NT, RH)
        self.mid, self.epos = take(KD, NT), take(KD, NT)
        self.keep = take(KD)
        w = Area(env, u_at)
        self.w = [[w(T) for _ in range(7)] for _ in range(2)]
        self.gn = self.r.rearrange("p k t -> p (k t)")[:, 0:2 * D].rearrange("p (a d) -> p a d", a=2)
        self.tmp = self.k.rearrange("p k t -> p (k t)")[:, 0:D]
        self.mean, self.var = self.mid.rearrange("p a b -> p (a b)")[:, 0:RH], \
            self.mid.rearrange("p a b -> p (a b)")[:, RH:2 * RH]
        self.grstd = self.epos.rearrange("p a b -> p (a b)")[:, 0:RH]
        self.o = env.big.rearrange("p (t d) -> p t d", t=NT)


class RwkvProject(Stage):

    MIXES = [1, 2, 4, 0, 5, 3]

    def __init__(self, env, m):
        super().__init__(env)
        self.m = m
        io = env.io
        w = io["w_rkv_2"][0]
        self.w1 = load_features(env, io["w_decay1_2"][0], 0, 64, 64)[0]
        self.k = load_features(env, w[1], 0, D)
        self.a1 = load_features(env, io["a1_2"][0], 0, 64, 64)[0]
        self.r = load_features(env, w[0], 0, D)
        self.g1 = load_features(env, io["g1_2"][0], 0, P) + load_features(env, io["g1_2"][0], P, 32, 32)
        self.v = load_tokens(env, w[2], 0, D)
        self.second = []
        for name in ("w_decay2_2", "a2_2"):
            ld, g = env.load(io[name][0].unsqueeze(1), split=False), env.group(KD)
            env.release(ld, env.proj_ready, env.groups)
            self.second.append((ld, g))
        self.last = [self.w1[1], self.k[-1][1], self.a1[1], self.r[-1][1]]
        self.mixed, self.mix_hi_ready, self.mix_ready = env.sem("mixed"), env.sem("mix_hi_ready"), env.sem("mix_ready")

    def vector(self, dve, step):
        env, nc, m = self.env, self.env.nc, self.m
        step(nc.vector.tensor_tensor(m.xx[:, :, 1:T], env.uT[:, :, 0:T - 1], env.uT[:, :, 1:T], ALU.subtract))
        step(nc.vector.tensor_scalar(m.xx[:, :, 0:1], env.uT[:, :, 0:1], -1.0, None, ALU.mult))

        def low(n, k):
            dve.wait_ge(self.mix_hi_ready, KD * n + k + 1)
            nc.vector.tensor_tensor(m.mixes[n % 2][1][:, k, :], env.junk2[:, k % 2, :],
                                    m.mixes[n % 2][0][:, k, :].bitcast(F32), ALU.subtract).then_inc(self.mix_ready, 1)

        for n, i in enumerate(self.MIXES):
            for k in range(KD):
                at = V_MU + 8 * i + k
                if KD * n + k >= 2:
                    dve.wait_ge(self.mix_ready, KD * n + k - 1)
                nc.vector.scalar_tensor_tensor(env.junk2[:, k % 2, :], m.xx[:, k, :], env.vec[:, at:at + 1],
                                               env.uT[:, k, :], ALU.mult, ALU.add).then_inc(self.mixed, 1)
                if k:
                    low(n, k - 1)
            low(n, KD - 1)

    def gpsimd(self, pool, step):
        self.env.split_lo(pool, self.v[0][-1] + 4)

    def tensor(self, pe):
        env, nc, m = self.env, self.env.nc, self.m
        for n, lds in enumerate(([self.w1], self.k, [self.a1], self.r, self.g1)):
            pe.wait_ge(self.mix_ready, KD * (n + 1))
            for ld, g in lds:
                project_features(env, pe, ld, m.mixes[n % 2], g, env.loads[ld][2])
        pe.wait_ge(self.mix_ready, KD * 6)
        project_tokens(env, pe, self.v[0], m.mixes[1], self.v[1])
        pe.wait_ge(env.proj_taken, self.a1[1] + 1)
        for (ld, g), hid in zip(self.second, (m.tanh_w, m.hid_a)):
            env.wait_whole(pe, ld)
            for k in range(KD):
                env.wait_bank(pe, g + k)
                nc.tensor.matmul(env.bank(g + k), env.whole(ld)[0:64, 0, k * P:(k + 1) * P], hid[0:64, :],
                                 start=True, stop=True).then_inc(env.proj_ready, 1)

    def scalar(self, act, step):
        env, nc, m = self.env, self.env.nc, self.m

        def high(n, k):
            if n >= 2 and k == 0:
                act.wait_ge(env.proj_ready, self.last[n - 2] + 1)
            act.wait_ge(self.mixed, KD * n + k + 1)
            nc.scalar.activation(m.mixes[n % 2][0][:, k, :], env.junk2[:, k % 2, :],
                                 ACT.Copy).then_inc(self.mix_hi_ready, 1)

        def take(entry, dst, func, rows=P):
            ld, g = entry
            env.split_hi(act, ld + 1)
            act.wait_ge(env.proj_ready, g + 1)
            nc.scalar.activation(dst, env.bank(g)[0:rows, :], func).then_inc(env.proj_taken, 1)

        env.split_hi(act, self.w1[0])
        for k in range(KD):
            high(0, k)
        env.split_hi(act, self.k[0][0])
        for k in range(KD):
            high(1, k)
        take(self.w1, m.tanh_w[0:64, :], ACT.Tanh, 64)
        for j, entry in enumerate(self.k):
            high(2, j)
            take(entry, m.k[:, j, :], ACT.Copy)
        for k in range(KD):
            high(3, k)
        take(self.a1, m.hid_a[0:64, :], ACT.Copy, 64)
        for j, entry in enumerate(self.r):
            high(4, j)
            take(entry, m.r[:, j, :], ACT.Copy)
        env.split_hi(act, self.g1[1][0])
        for k in range(KD):
            high(5, k)
        take(self.g1[0], m.sg[:, 0, :], ACT.Sigmoid)
        take(self.g1[1], m.sg[0:32, 1, :], ACT.Sigmoid, 32)
        lds, g = self.v
        env.split_hi(act, lds[-1])
        for n in range(2 * NT):
            act.wait_ge(env.proj_ready, g + n + 1)
            nc.scalar.activation(m.v[:, n // 2, 512 * (n % 2):512 * (n % 2) + 512], env.ps[:, n, :],
                                 ACT.Copy).then_inc(env.proj_taken, 1)
        act.wait_ge(self.mix_ready, KD * 6)
        for (ld, g), dst, col in zip(self.second, (m.decay, m.a), (V_B, V_B + 8)):
            for k in range(KD):
                act.wait_ge(env.proj_ready, g + k + 1)
                nc.scalar.activation(dst[:, k, :], env.bank(g + k), ACT.Sigmoid,
                                     bias=env.vec[:, col + k:col + k + 1]).then_inc(env.proj_taken, 1)


class RwkvPrepare(Stage):

    def __init__(self, env, m):
        super().__init__(env)
        self.m = m
        s = env.sem
        self.sq_ready, self.ss_ready, self.inv_ready = s("kk_sq_ready"), s("kk_ss_ready"), s("kk_inv_ready")
        self.norm_ready, self.mid_ready, self.exps_ready = s("kk_norm_ready"), s("mid_ready"), s("exps_ready")
        self.rk_ready, self.tile_done = s("rk_ready"), s("prep_tile_done")
        self.bonus_ready = s("bonus_ready")
        self.mix_ready, self.kk_ready, self.scanned = s("k_mix_ready"), s("kk_ready"), s("scanned")

    def tensor(self, pe):
        env, nc, m = self.env, self.env.nc, self.m
        for k in range(KD):
            w = m.w[k % 2]
            pe.wait_ge(self.sq_ready, k + 1)
            nc.tensor.matmul(env.ps[:, k % 2, :], env.const[:, C_HEADSUM:C_HEADSUM + P], w[0],
                             start=True, stop=True).then_inc(self.ss_ready, 1)
            pe.wait_ge(self.rk_ready, k + 1)
            for i in range(NT):
                mm = nc.tensor.matmul(env.ps[:, 7, i * RH + 2 * k:i * RH + 2 * k + 2], w[1][:, i * P:(i + 1) * P],
                                      env.const[:, C_HEADSEL:C_HEADSEL + 2], start=True, stop=True)
            mm.then_inc(self.bonus_ready, 1)

    def scalar(self, act, step):
        env, nc, m = self.env, self.env.nc, self.m
        step(nc.scalar.activation(m.keep, env.vec[:, V_B + 24:V_B + 32], ACT.Copy, scale=-1.0, bias=1.0))

        def first(k):
            w = m.w[k % 2]
            col = lambda n: env.vec[:, V_B + 8 * n + k:V_B + 8 * n + k + 1]
            if k >= 2:
                act.wait_ge(self.rk_ready, k - 1)
                act.wait_ge(self.ss_ready, k - 1)
            nc.scalar.activation(m.kk[:, k, :], m.k[:, k, :], ACT.Copy, scale=col(2))
            nc.scalar.activation(w[0], m.k[:, k, :], ACT.Square, scale=col(2)).then_inc(self.sq_ready, 1)
            nc.scalar.activation(w[5], m.a[:, k, :], ACT.Identity, scale=col(3),
                                 bias=m.keep[:, k:k + 1]).then_inc(self.mix_ready, 1)

        first(0)
        for k in range(KD):
            w = m.w[k % 2]
            if k + 1 < KD:
                first(k + 1)
            act.wait_ge(self.inv_ready, k + 1)
            nc.scalar.activation(w[2], w[3], ACT.Sqrt).then_inc(self.norm_ready, 1)

    def vector(self, dve, step):
        env, nc, m = self.env, self.env.nc, self.m
        v = nc.vector
        ones = env.const[:, C_ONES:C_ONES + P]

        def last(k):
            dve.wait_ge(self.norm_ready, k + 1)
            v.tensor_tensor(m.kk[:, k, :], m.kk[:, k, :], m.w[k % 2][2], ALU.mult).then_inc(self.kk_ready, 1)

        for k in range(KD):
            w = m.w[k % 2]
            kp, r = m.k[:, k, :], m.r[:, k, :]
            dve.wait_ge(self.mix_ready, k + 1)
            step(v.tensor_tensor(kp, w[5], kp, ALU.mult))
            if k >= 2:
                dve.wait_ge(self.bonus_ready, k - 1)
            v.scalar_tensor_tensor(w[1], r, env.vec[:, V_B + 32 + k:V_B + 33 + k], kp, ALU.mult,
                                   ALU.mult).then_inc(self.rk_ready, 1)
            if k >= 2:
                dve.wait_ge(self.tile_done, k - 1)
            for c in range(NT):
                v.tensor_tensor_scan(w[6][:, c * P:(c + 1) * P], ones, m.decay[:, k, c * P:(c + 1) * P], 0.0,
                                     ALU.mult, ALU.add).then_inc(self.scanned, 1)
            if k:
                last(k - 1)
            dve.wait_ge(self.scanned, NT * (k + 1))
            v.tensor_copy(m.mid[:, k, :], w[6][:, P // 2 - 1:T:P]).then_inc(self.mid_ready, 1)
            dve.wait_ge(self.ss_ready, k + 1)
            step(v.tensor_scalar(w[3], env.ps[:, k % 2, :], 1e-24, None, ALU.max))
            v.reciprocal(w[3], w[3]).then_inc(self.inv_ready, 1)
        last(KD - 1)
        dve.wait_ge(self.bonus_ready, KD)
        step(v.tensor_copy(m.bonus.rearrange("p a b -> p (a b)"), env.ps[:, 7, 0:NT * RH]))

    def gpsimd(self, pool, step):
        env, nc, m = self.env, self.env.nc, self.m
        chunks = lambda x: x.rearrange("p (c t) -> p c t", c=NT)

        def product(k):
            pool.wait_ge(self.kk_ready, k + 1)
            nc.gpsimd.tensor_tensor(m.a[:, k, :], m.a[:, k, :], m.kk[:, k, :], ALU.mult)

        for k in range(KD):
            pool.wait_ge(self.mid_ready, k + 1)
            nc.gpsimd.tensor_tensor(chunks(m.decay[:, k, :]), chunks(m.w[k % 2][6]),
                                    m.mid[:, k, :].unsqueeze(2).to_broadcast([P, NT, P]),
                                    ALU.subtract).then_inc(self.tile_done, 1)
            if k:
                product(k - 1)
        product(KD - 1)


class RwkvDecay(Stage):

    def __init__(self, env, m):
        super().__init__(env)
        self.m = m
        self.exps_ready, self.taken = env.sem("decay_exps_ready"), env.sem("decay_exps_taken")
        self.cols_ready = env.sem("decay_cols_ready")

    def scalar(self, act, step):
        env, nc, m = self.env, self.env.nc, self.m
        c = DECAY_SCALE
        step(nc.scalar.activation(m.coef, m.mid, ACT.Exp, scale=-c))
        nc.scalar.activation(m.epos, m.mid, ACT.Exp, scale=c).then_inc(self.cols_ready, 1)
        for k in range(KD):
            w = m.w[k % 2]
            if k >= 2:
                act.wait_ge(self.taken, k - 1)
            nc.scalar.activation(w[0], m.decay[:, k, :], ACT.Exp, scale=-c)
            nc.scalar.activation(w[1], m.decay[:, k, :], ACT.Exp, scale=c).then_inc(self.exps_ready, 1)

    def vector(self, dve, step):
        env, nc, m = self.env, self.env.nc, self.m
        v = nc.vector
        chunks = lambda x: x.rearrange("p (c t) -> p c t", c=NT)
        dve.wait_ge(self.cols_ready, 1)
        for k in range(KD):
            w = m.w[k % 2]
            kk = chunks(m.kk[:, k, :])
            e = chunks(w[0])
            dve.wait_ge(self.exps_ready, k + 1)
            v.tensor_tensor(m.r[:, k, :], m.r[:, k, :], w[0], ALU.mult)
            v.tensor_tensor(m.a[:, k, :], m.a[:, k, :], w[1], ALU.mult)
            v.tensor_tensor(m.k[:, k, :], m.k[:, k, :], w[1], ALU.mult)
            v.scalar_tensor_tensor(kk[:, :, 1:P], kk[:, :, 1:P], -1.0, e[:, :, 0:P - 1], ALU.mult, ALU.mult)
            v.scalar_tensor_tensor(kk[:, :, 0], kk[:, :, 0], -1.0, m.epos[:, k, :], ALU.mult, ALU.mult)
            v.tensor_tensor(m.coef[:, k, 1:NT], m.coef[:, k, 1:NT], e[:, 0:NT - 1, P - 1],
                            ALU.mult).then_inc(self.taken, 1)


class RwkvCore(Stage):

    STEPS = [(c, q) for c in range(NT) for q in range(2)]

    def __init__(self, env, m):
        super().__init__(env)
        self.m = m
        s = env.sem
        self.ready = {"A": s("core_act_ready"), "D": s("core_dve_ready")}
        self.taken = {"A": s("core_act_taken"), "D": s("core_dve_taken")}
        self.part_ready = s("level_part_ready")
        self.start_ready = s("start_ready")
        self.start_T_ready = s("start_T_ready")
        self.order = [(0, name, st) for st in range(2) for name in ("abT", "ab", "akT")] + self.late(0)
        last = len(self.STEPS) - 1
        for w in range(last + 1):
            for lv in range(1, LEVELS):
                self.order += [(w, "Y", lv, st) for st in range(2)]
                for st in range(2):
                    self.order += [(w, name, lv, st) for name in (("X", "XT") if lv < LEVELS - 1 else ("XT",))]
            fill = [] if w == last else [[(w + 1, "abT", 0), (w + 1, "ab", 0)], [(w + 1, "akT", 0), (w + 1, "abT", 1)],
                                         [(w + 1, "ab", 1), (w + 1, "akT", 1)], self.late(w + 1)]
            for name in ("WT", "SA", "y", "S"):
                self.order += [(w, name, st) for st in range(2)]
                if fill:
                    self.order += fill.pop(0)
        self.num, count = {}, {"A": 0, "D": 0}
        for key in self.order:
            engine = "A" if key[1] in ("tok", "Z", "Y", "WT", "SA", "y") else "D"
            self.num[key] = (engine, count[engine])
            count[engine] += 1

    @staticmethod
    def late(w):
        return ([(w, "tok", arr) for arr in range(3)] + [(w, name, st) for st in range(2) for name in ("rbT", "rkT")]
                + [(w, "Z", st) for st in range(2)])

    def bank(self, key):
        engine, n = self.num[key]
        return self.env.ps[:, n % 4 + (4 if engine == "D" else 0), :]

    def wait_ready(self, eng, *key):
        engine, n = self.num[key]
        eng.wait_ge(self.ready[engine], n + 1)

    def wait_taken(self, eng, *key):
        engine, n = self.num[key]
        eng.wait_ge(self.taken[engine], n + 1)

    def tensor(self, pe):
        env, nc, m = self.env, self.env.nc, self.m
        mmul = nc.tensor.matmul
        operands = {"abT": (m.a, m.kk), "ab": (m.kk, m.a), "akT": (m.k, m.kk), "rbT": (m.a, m.r), "rkT": (m.k, m.r)}
        for key in self.order:
            w, name, st = key[0], key[1], key[-1]
            c, q = self.STEPS[w]
            tok, half = slice(c * P, (c + 1) * P), slice(64 * st, 64 * st + 64)
            s = m.streams[st] if name != "tok" else None
            lv = key[2]
            if name == "Z":
                self.wait_taken(pe, w, "akT", st)
            elif name == "Y":
                pe.wait_ge(self.part_ready, 12 * w + 2 * (lv - 1) + st + 1)
                if lv == 1:
                    pe.wait_ge(self.start_ready, 2 * w + st + 1)
                else:
                    self.wait_taken(pe, w, "X", lv - 1, st)
            elif name == "X" or (name == "XT" and lv == LEVELS - 1):
                self.wait_taken(pe, w, "Y", lv, st)
                if lv == 1:
                    pe.wait_ge(self.start_T_ready, 2 * w + st + 1)
                else:
                    self.wait_taken(pe, w, "XT", lv - 1, st)
            elif name == "WT":
                self.wait_taken(pe, w, "XT", LEVELS - 1, st)
                self.wait_taken(pe, w, "tok", 0)
            elif name == "SA":
                self.wait_taken(pe, w, "Z", st)
                self.wait_taken(pe, w, "WT", st)
                if w >= 2:
                    self.wait_taken(pe, w - 2, "S", st)
            elif name == "y":
                self.wait_taken(pe, w, "SA", st)
                self.wait_taken(pe, w, "rkT", st)
            elif name == "S":
                self.wait_taken(pe, w, "tok", 2)
            engine, n = self.num[key]
            if n >= 4:
                pe.wait_ge(self.taken[engine], n - 3)
            for e in range(4):
                k, h = 4 * q + e, 2 * (4 * q + e) + st
                wide, thin = self.bank(key)[:, e * P:(e + 1) * P], self.bank(key)[:, e * DH:(e + 1) * DH]
                v = m.v[:, c, h * DH:(h + 1) * DH] if name != "tok" else None
                if name == "tok":
                    mm = nc.tensor.transpose(wide, (m.kk, m.a, m.k)[st][:, k, tok], env.ident)
                elif name in operands:
                    lhs, rhs = operands[name]
                    mm = mmul(wide, lhs[half, k, tok], rhs[half, k, tok], start=True, stop=True)
                elif name == "Z":
                    mm = mmul(thin, s["akT"][:, e, :], v, start=True, stop=True)
                elif name == "Y":
                    mm = mmul(wide, s["MT"][lv % 2][:, e, :], s["X"][:, e, :], start=True, stop=True)
                elif name == "X":
                    mm = mmul(wide, s["XT"][:, e, :], s["Y"][:, e, :], start=True, stop=True)
                elif name == "XT":
                    mm = mmul(wide, s["Y"][:, e, :], s["XT"][:, e, :], start=True, stop=True)
                elif name == "WT":
                    mm = mmul(wide[half], m.tok[:, 0, e, half], s["XT"][:, e, :], start=True, stop=True)
                elif name == "SA":
                    mm = mmul(thin, s["XT"][:, e, :], s["Z"][:, e, :], start=True, stop=(c == 0))
                    if c:
                        mm = mmul(thin, m.WT[half, e, :], m.S[half, k, :], start=False, stop=True)
                elif name == "y":
                    mmul(thin, s["rbT"][:, e, :], s["SA"][:, e, :], start=True, stop=False)
                    mm = mmul(thin, s["rkT"][:, e, :], v, start=False, stop=(c == 0))
                    if c:
                        mm = mmul(thin, m.r[half, k, tok], m.S[half, k, :], start=False, stop=True)
                else:
                    mmul(thin[half], m.tok[:, 1, e, half], s["SA"][:, e, :], start=True, stop=False)
                    mm = mmul(thin[half], m.tok[:, 2, e, half], v, start=False, stop=True)
            mm.then_inc(self.ready[engine], 1)

    def four(self, key, n=P):
        return self.bank(key)[:, 0:4 * n].rearrange("p (e n) -> p e n", e=4)

    def scalar(self, act, step):
        env, nc, m = self.env, self.env.nc, self.m
        for key in self.order:
            w, name, st = key[0], key[1], key[-1]
            if self.num[key][0] != "A":
                continue
            c, q = self.STEPS[w]
            half = slice(64 * st, 64 * st + 64)
            if name == "tok":
                dst, src = m.tok[:, st], self.four(key)
            elif name == "Y":
                if key[2] > 1:
                    self.wait_ready(act, w, "XT", key[2] - 1, st)
                dst, src = m.streams[st]["Y"], self.four(key)
            elif name == "WT":
                dst, src = m.WT[half], self.four(key)[half]
            elif name == "y":
                dst = m.kk[:, 4 * q:4 * q + 4, c * P + 64 * st:c * P + 64 * st + 64]
                src = self.four(key, DH)
            else:
                dst, src = m.streams[st][name], self.four(key, DH)
            self.wait_ready(act, *key)
            nc.scalar.activation(dst, src, ACT.Copy).then_inc(self.taken["A"], 1)

    def vector(self, dve, step):
        env, nc, m = self.env, self.env.nc, self.m
        v = nc.vector
        mask = lambda at: env.const[:, at:at + P].unsqueeze(1).to_broadcast([P, 4, P])
        masked = {"abT": (C_STRICT_T, "abT"), "ab": (C_PAIR, "X"), "akT": (C_STRICT_T, "akT"),
                  "rbT": (C_INCL_T, "rbT"), "rkT": (C_INCL_T, "rkT")}
        for key in self.order:
            w, name, st = key[0], key[1], key[-1]
            if self.num[key][0] != "D":
                continue
            c, q = self.STEPS[w]
            s = m.streams[st]
            if name in masked:
                at, dst = masked[name]
                if w:
                    if name == "abT":
                        dve.wait_ge(self.part_ready, 12 * w)
                    else:
                        self.wait_ready(dve, w - 1, *{"ab": ("Y", LEVELS - 1), "akT": ("Z",), "rbT": ("y",),
                                                      "rkT": ("y",)}[name], st)
                self.wait_ready(dve, *key)
                v.tensor_tensor(s[dst], self.four(key), mask(at), ALU.mult).then_inc(self.taken["D"], 1)
            elif name in ("X", "XT"):
                self.wait_ready(dve, *key)
                v.tensor_tensor(s[name], self.four(key), s[name], ALU.add).then_inc(self.taken["D"], 1)
            else:
                half = slice(64 * st, 64 * st + 64)
                self.wait_ready(dve, *key)
                S = m.S[half, 4 * q:4 * q + 4, :]
                new = self.four(key, DH)[half]
                coef = m.coef[half, 4 * q:4 * q + 4, c + 1:c + 2].to_broadcast([64, 4, DH]) if c < NT - 1 else None
                if c == 0:
                    v.tensor_tensor(S, new, coef, ALU.mult).then_inc(self.taken["D"], 1)
                elif c < NT - 1:
                    step(v.tensor_tensor(S, S, new, ALU.add))
                    v.tensor_tensor(S, S, coef, ALU.mult).then_inc(self.taken["D"], 1)
                else:
                    v.tensor_tensor(S, S, new, ALU.add).then_inc(self.taken["D"], 1)

    def gpsimd(self, pool, step):
        env, nc, m = self.env, self.env.nc, self.m
        g = nc.gpsimd
        mask = lambda at: env.const[:, at:at + P].unsqueeze(1).to_broadcast([P, 4, P])
        for w in range(len(self.STEPS)):
            for st in range(2):
                s = m.streams[st]
                self.wait_taken(pool, w, "ab", st)
                g.tensor_tensor(s["X"], s["X"], mask(C_IDENT), ALU.add).then_inc(self.start_ready, 1)
                g.tensor_tensor(s["MT"][1], s["abT"], mask(C_LEVEL_T), ALU.mult).then_inc(self.part_ready, 1)
            for st in range(2):
                s = m.streams[st]
                if w:
                    self.wait_ready(pool, w - 1, "SA", st)
                step(g.tensor_tensor(s["XT"], s["abT"], mask(C_PAIR_T), ALU.mult))
                g.tensor_tensor(s["XT"], s["XT"], mask(C_IDENT), ALU.add).then_inc(self.start_T_ready, 1)
            for lv in range(2, LEVELS):
                for st in range(2):
                    s = m.streams[st]
                    if lv > 2:
                        self.wait_ready(pool, w, "Y", lv - 2, st)
                    g.tensor_tensor(s["MT"][lv % 2], s["abT"], mask(C_LEVEL_T + (lv - 1) * P),
                                    ALU.mult).then_inc(self.part_ready, 1)


class RwkvGate(Stage):

    def __init__(self, env, m):
        super().__init__(env)
        self.m = m
        g2 = env.io["g2_2"][0]
        self.lds = [env.load(g2[0:P].unsqueeze(1), split=False), env.load(g2[P:160].unsqueeze(1), split=False)]
        self.g0 = env.group(8)
        for ld in self.lds:
            env.release(ld, env.proj_ready, env.groups)
        self.rows = env.sem("gn_rows")
        self.var_ready, self.std_ready = env.sem("gn_var_ready"), env.sem("gn_std_ready")

    def gpsimd(self, pool, step):
        env, m = self.env, self.m
        pool.dma_start(m.gn[:, 0, :], env.io["gn_g_2"][0].partition_broadcast(P)).then_inc(self.rows, 16)
        pool.dma_start(m.gn[:, 1, :], env.io["gn_b_2"][0].partition_broadcast(P)).then_inc(self.rows, 16)

    def tensor(self, pe):
        env, nc, m = self.env, self.env.nc, self.m
        for ld in self.lds:
            env.wait_whole(pe, ld)
        w = [env.whole(ld)[:, 0, :] for ld in self.lds]
        for i in range(NT):
            tok = slice(i * P, (i + 1) * P)
            for half in range(2):
                g = self.g0 + 2 * i + half
                cols = slice(512 * half, 512 * half + 512)
                env.wait_bank(pe, g)
                nc.tensor.matmul(env.bank(g), m.sg[:, 0, tok], w[0][:, cols], start=True, stop=False)
                nc.tensor.matmul(env.bank(g), m.sg[0:32, 1, tok], w[1][0:32, cols],
                                 start=False, stop=True).then_inc(env.proj_ready, 1)

    def scalar(self, act, step):
        env, nc, m = self.env, self.env.nc, self.m
        for i in range(NT):
            act.wait_ge(self.var_ready, i + 1)
            nc.scalar.activation(m.grstd, m.var, ACT.Sqrt).then_inc(self.std_ready, 1)

    def vector(self, dve, step):
        env, nc, m = self.env, self.env.nc, self.m
        v = nc.vector
        wide = lambda c: c.unsqueeze(2).to_broadcast([P, RH, DH])
        dve.wait_ge(self.rows, 32)
        tmp = m.tmp.rearrange("p (h d) -> p h d", d=DH)
        for i in range(NT):
            y = m.kk[:, :, i * P:(i + 1) * P].rearrange("p k (h d) -> p k h d", d=DH)
            o, flat = m.o[:, i, :].rearrange("p (h d) -> p h d", d=DH), m.o[:, i, :]
            step(v.tensor_copy(flat.rearrange("p (k d) -> p k d", d=P), m.kk[:, :, i * P:(i + 1) * P]))
            step(v.tensor_reduce(m.mean, o, AX, ALU.add))
            step(v.tensor_scalar(m.mean, m.mean, 1.0 / DH, None, ALU.mult))
            step(v.tensor_tensor(o, o, wide(m.mean), ALU.subtract))
            step(v.tensor_tensor(m.tmp, flat, flat, ALU.mult))
            step(v.tensor_reduce(m.var, tmp, AX, ALU.add))
            step(v.tensor_scalar(m.var, m.var, 1.0 / DH, GN_EPS, ALU.mult, ALU.add))
            v.reciprocal(m.var, m.var).then_inc(self.var_ready, 1)
            dve.wait_ge(self.std_ready, i + 1)
            step(v.tensor_tensor(o, o, wide(m.grstd), ALU.mult))
            step(v.tensor_tensor(flat, flat, m.gn[:, 0, :], ALU.mult))
            step(v.tensor_tensor(flat, flat, m.gn[:, 1, :], ALU.add))
            step(v.tensor_tensor(tmp, m.v[:, i, :].rearrange("p (h d) -> p h d", d=DH), wide(m.bonus[:, i, :]), ALU.mult))
            step(v.tensor_tensor(flat, flat, m.tmp, ALU.add))
            for half in range(2):
                g = self.g0 + 2 * i + half
                cols = slice(512 * half, 512 * half + 512)
                dve.wait_ge(env.proj_ready, g + 1)
                v.tensor_tensor(flat[:, cols], env.bank(g), flat[:, cols], ALU.mult).then_inc(env.proj_taken, 1)
        dve.wait_ge(env.proj_taken, self.g0 + 8)


def end_stage(env, eng, s):
    eng.drain().then_inc(env.stage_done, 1)
    eng.wait_ge(env.stage_done, 4 * (s + 1))


def build(nc, io, out, n_stages=None, skip_rwkv=False):
    with ExitStack() as ctx:
        env = Env(nc, ctx, io)
        setup = Setup(env)
        m = NsaMemory(env, setup.bias, setup)
        dm = DiffMemory(env, setup.bias)
        rm = RwkvMemory(env)
        fm = FfnMemory(env)
        sm = SwaMemory(env)
        pre, post, g = io["norm_pre"], io["norm_post"], io["norm_g_2"]
        stages = [
            setup,
            Norm(env, pre[0], m.u, setup.x_arrived),
            NsaProject(env, m),
            NsaCompress(env, m),
            NsaCompressed(env, m),
            NsaAttend(env, m),
            Output(env, io["nsa_w_out"][0], post[0], m.u, m.o, m.z, following=(pre[1], dm.u)),
            DiffProject(env, dm),
            DiffAttend(env, dm),
            DiffNorm(env, dm),
            Output(env, io["diff_w_out"][0], post[1], dm.oT, dm.o, dm.z, following=(g[0, 0], [env.uT])),
            RwkvProject(env, rm),
            RwkvPrepare(env, rm),
            RwkvDecay(env, rm),
            RwkvCore(env, rm),
            RwkvGate(env, rm),
            Output(env, io["w_o_rwkv_2"][0], g[0, 1], rm.oT, rm.o, following=(g[0, 2], fm.u)),
            FfnUp(env, 0, fm),
            Output(env, io["w_down_2"][0], g[0, 3], fm.act, kd=FT, following=(io["kv_g_2"], sm.u)),
        ]
        kv = KvProject(env, sm, g[1, 0])
        stages += [
            kv,
            NormAgain(env, kv.again),
            SwaProject(env, sm),
            SwaAttend(env, sm),
            Output(env, io["w_o_attn_2"][0], g[1, 1], sm.u, sm.o, following=(g[1, 2], fm.u)),
            FfnUp(env, 1, fm),
            Output(env, io["w_down_2"][1], g[1, 3], fm.act, kd=FT),
        ]
        used = len(stages) if n_stages is None else n_stages
        stages = stages[:used]
        block = ctx.enter_context(nc.Block())

        @block.sync
        def _(sp):
            setup.load(sp)
            for ld in range(len(env.loads)):
                env.fetch(sp, ld)
            for i in range(NT):
                sp.wait_ge(env.x_added, NT * (env.outs - 1) + i + 1)
                sp.dma_start(out[0, i * P:(i + 1) * P, :], env.x[:, i, :]).then_inc(env.stored, 16)
            sp.wait_ge(env.stored, 16 * NT)
            sp.wait_ge(env.stage_done, 4 * len(stages))

        @block.tensor
        def _(pe):
            for s, stage in enumerate(stages):
                stage.tensor(pe)
                end_stage(env, pe, s)

        @block.scalar
        def _(act):
            step = Steps(act, env.act_step)
            for s, stage in enumerate(stages):
                stage.scalar(act, step)
                end_stage(env, act, s)

        @block.vector
        def _(dve):
            step = Steps(dve, env.dve_step)
            for s, stage in enumerate(stages):
                stage.vector(dve, step)
                end_stage(env, dve, s)

        @block.gpsimd
        def _(pool):
            step = Steps(pool, env.pool_step)
            for s, stage in enumerate(stages):
                stage.gpsimd(pool, step)
                end_stage(env, pool, s)


def declare(nc, inputs, n_stages=None, skip_rwkv=False):
    arrays, io = {}, {}
    given = dict(inputs)
    given["shape_constants"] = shape_constants()
    given["distance_one_hot"] = distance_one_hot().astype("bfloat16")
    for name, a in given.items():
        a = np.ascontiguousarray(a)
        arrays["in_" + name] = a
        io[name] = nc.dram_tensor("in_" + name, a.shape, mybir.dt.from_np(a.dtype), kind="ExternalInput").ap()
    out = nc.dram_tensor("out", (1, T, D), F32, kind="ExternalOutput").ap()
    build(nc, io, out, n_stages, skip_rwkv)
    return arrays


def kernel(**inputs):
    import concourse.bacc as _bacc
    from concourse.bass_utils import run_bass_kernel_spmd as _run

    nc = _bacc.Bacc("TRN2", target_bir_lowering=False, num_devices=1)
    arrays = declare(nc, inputs)
    r = _run(nc, [arrays], core_ids=[0])
    return r.results[0]["out"]
```

```python
from contextlib import ExitStack

import numpy as np

import concourse.bass as bass
from concourse import mybir

ALU = mybir.AluOpType
ACT = mybir.ActivationFunctionType
AX = mybir.AxisListType.X
F32 = mybir.dt.float32
BF16 = mybir.dt.bfloat16
F32R = mybir.dt.float32r

P = 128
T = 512
NT = T // P
D = 1024
KD = D // P
NEG = -1e30
EPS = 1e-6

HEADS, GROUPS, HPG, DH = 16, 4, 4, 64
BUCKETS, MAX_DIST = 32, 128
CMP_BLOCK, CMP_STRIDE = 32, 16
NC = (T - CMP_BLOCK) // CMP_STRIDE + 1
NCP = 32
CMP_K = CMP_BLOCK * DH // P
DIFF_HEADS = 8
LAMBDA_INIT = 0.8 - 0.6 * float(np.exp(-0.3))
NSA_IN = D + 6 * 256 + 3 * HEADS + D
D_FF = 2816
FT = D_FF // P
RH = 16
GN_EPS = 64e-5
DECAY_SCALE = float(np.exp(-0.5))
LEVELS = 7

DIST0 = (NCP - 1) * CMP_STRIDE + CMP_BLOCK - 1 + 1
NDIST = DIST0 + T


def distance_one_hot():
    n = np.arange(NDIST) - DIST0
    exact = BUCKETS // 2
    nf = np.maximum(n, 1)
    large = exact + (np.log(nf / exact) / np.log(MAX_DIST / exact) * (BUCKETS - exact) + 1e-9).astype(np.int64)
    bucket = np.where(n < exact, np.maximum(n, 0), np.minimum(large, BUCKETS - 1))
    table = np.zeros((P, NDIST), np.float32)
    for part in range(3):
        table[32 * part + bucket, np.arange(NDIST)] = n >= 0
    table[96] = n < 0
    return table


C_IDENT = 0
C_HEADROW = C_IDENT + P
C_HEADSEL = C_HEADROW + 32
C_BAND = C_HEADSEL + 2
C_STRICT_T = C_BAND + 2 * P
C_INCL_T = C_STRICT_T + P
C_PAIR = C_INCL_T + P
C_PAIR_T = C_PAIR + P
C_ONES = C_PAIR_T + P
C_LEVEL_T = C_ONES + P
N_CONST = C_LEVEL_T + (LEVELS - 1) * P


def shape_constants():
    c = np.zeros((P, N_CONST), np.float32)
    r = np.arange(P)
    c[:, C_IDENT:C_IDENT + P] = np.eye(P)
    c[:, C_HEADROW:C_HEADROW + 4 * KD - 2] = (r[:, None] // DH) == np.arange(4 * KD - 2)[None] - 2 * (KD - 1)
    c[:, C_HEADSEL:C_HEADSEL + 2] = (r[:, None] // DH) == np.arange(2)[None]
    c[:, C_BAND:C_BAND + P] = np.where(r[None] > r[:, None], 0.0, NEG)
    c[:, C_BAND + P:C_BAND + 2 * P] = np.where(r[None] <= r[:, None], 0.0, NEG)
    c[:, C_STRICT_T:C_STRICT_T + P] = r[:, None] < r[None]
    c[:, C_INCL_T:C_INCL_T + P] = r[:, None] <= r[None]
    pair = (r[None] == r[:, None] - 1) & (r[:, None] % 2 == 1)
    c[:, C_PAIR:C_PAIR + P] = pair
    c[:, C_PAIR_T:C_PAIR_T + P] = pair.T
    c[:, C_ONES:C_ONES + P] = 1.0
    for lv in range(1, LEVELS):
        b = 1 << lv
        low = (r[:, None] // (2 * b) == r[None] // (2 * b)) & (r[:, None] // b % 2 == 1) & (r[None] // b % 2 == 0)
        c[:, C_LEVEL_T + (lv - 1) * P:C_LEVEL_T + lv * P] = low.T
    return c


V_PRE = 0
V_G = 16
V_MU = 80
V_B = 128
V_SUBLN = 176
V_CONV = 184
N_VEC = V_CONV + 2 * 176


WARM_UP = 16


class Env:

    RAW = 3
    SLOT = 1024

    def __init__(self, nc, ctx, io):
        self.nc, self.ctx, self.io = nc, ctx, io
        words = 52496
        self.arena_base = -(-nc.sbuf_base // 32) * 32
        ctx.enter_context(nc.sbuf_tensor("arena", [P, words], F32))
        self.buffers = 0
        self.words = words
        self.ps = ctx.enter_context(nc.psum_tensor("ps", [P, 8, 512], F32))
        self.at = 0
        self.x = self.take(NT, D)
        self.uT_at = self.at
        self.uT = self.take(KD, T)
        self.big_at = self.at
        self.big = self.take(NT * D)
        self.raw = self.take(self.RAW, self.SLOT)
        self.part_hi = self.take_r("weights_hi", 2, self.SLOT)
        self.part_lo = self.take_r("weights_lo", 2, self.SLOT)
        self.const = self.take(N_CONST)
        self.vec = self.take(N_VEC)
        self.post_g_at = self.at
        self.post_g = self.take(D)
        self.stat_at = self.at
        self.stat = self.take(256)
        self.lambda_work = self.take(T)
        self.pair_tmp = self.take(2, T)
        self.small_at = self.at
        self.at += 288
        self.area = self.at = -(-self.at // 8) * 8
        self.ident = self.const[:, C_IDENT:C_IDENT + P]
        self.proj_ready = self.sem("proj_ready")
        self.proj_taken = self.sem("proj_taken")
        self.groups = 0
        self.raw_arrived = [self.sem(f"raw_arrived{r}") for r in range(self.RAW)]
        self.hi_ready = self.sem("weights_hi_ready")
        self.lo_ready = self.sem("weights_lo_ready")
        self.slot_done = self.sem("slot_done")
        self.loads = []
        self.splits = []
        self.hi_issued = self.lo_issued = 0
        self.slots_done = 0
        self.stage_done = self.sem("stage_done")
        self.dve_step = self.sem("dve_step")
        self.act_step = self.sem("act_step")
        self.pool_step = self.sem("pool_step")
        self.rms_ready = self.sem("rms_ready")
        self.un_ready = self.sem("un_ready")
        self.un_turned = self.sem("un_turned")
        self.uhi_ready = self.sem("uhi_ready")
        self.uT_ready = self.sem("uT_ready")
        self.next_g_arrived = self.sem("next_g_arrived")
        self.norms = self.uhis = self.repeats = 0
        self.next_g = self.pair_tmp.rearrange("p a b -> p (a b)")
        self.eps, self.sqrt_junk = self.stat[:, 12:13], self.stat[:, 13:14]
        self.tr_ready = self.sem("tr_ready")
        self.oT_ready = self.sem("oT_ready")
        self.otmp_ready, self.oT_hi_ready = self.sem("otmp_ready"), self.sem("oT_hi_ready")
        self.yrms_ready = self.sem("yrms_ready")
        self.g_arrived = self.sem("g_arrived")
        self.outs = 0
        self.trs = 0
        self.ots = 0
        self.stored = self.sem("stored")
        self.x_edge_added = self.sem("x_edge_added")
        self.x_added = self.sem("x_added")

    def sem(self, name):
        return self.ctx.enter_context(self.nc.semaphore(name))

    def take(self, *shape, at=None):
        n = int(np.prod(shape))
        if at is None:
            at = self.at
            self.at += n + -n % 8
        assert at + n <= self.words, (at + n, self.words)
        self.buffers += 1
        v = self.nc.alloc_sbuf_tensor_at(f"buffer{self.buffers}", [P, n], F32, offset=self.arena_base + 4 * at)[:]
        if len(shape) == 2:
            v = v.rearrange("p (a b) -> p a b", a=shape[0])
        if len(shape) == 3:
            v = v.rearrange("p (a b c) -> p a b c", a=shape[0], b=shape[1])
        return v

    def take_r(self, name, a, b, at=None):
        if at is None:
            at = self.at
            self.at += a * b
        assert at + a * b <= self.words, (at + a * b, self.words)
        return self.nc.alloc_sbuf_tensor_at(name, [P, a, b], F32R, offset=self.arena_base + 4 * at)[:]

    def load(self, src, split=True):
        self.loads.append([src, src.shape[1], src.shape[2], len(self.splits) if split else None, None])
        if split:
            self.splits.append(len(self.loads) - 1)
        return len(self.loads) - 1

    def release(self, ld, sem, value):
        self.loads[ld][4] = (sem, value)

    def release_slot(self, ld):
        self.slots_done += 1
        self.release(ld, self.slot_done, self.slots_done)

    def whole(self, ld):
        k, n = self.loads[ld][1:3]
        return self.raw[:, ld % self.RAW, 0:k * n].rearrange("p (k n) -> p k n", k=k)

    def parts(self, ld):
        k, n, part = self.loads[ld][1:4]
        return [ring[:, part % 2, 0:k * n].rearrange("p (k n) -> p k n", k=k) for ring in (self.part_hi, self.part_lo)]

    def wait_whole(self, eng, ld):
        eng.wait_ge(self.raw_arrived[ld % self.RAW], 16 * (ld // self.RAW + 1))

    def wait_hi(self, pe, ld):
        pe.wait_ge(self.hi_ready, self.loads[ld][3] + 1)

    def wait_lo(self, pe, ld):
        pe.wait_ge(self.lo_ready, self.loads[ld][3] + 1)

    def fetch(self, sp, ld):
        src, k, n, _, _ = self.loads[ld]
        if ld >= self.RAW:
            _, _, _, part, release = self.loads[ld - self.RAW]
            if part is None:
                sp.wait_ge(*release)
            else:
                sp.wait_ge(self.lo_ready, part + 1)
        sp.dma_start(self.whole(ld)[0:src.shape[0]], src).then_inc(self.raw_arrived[ld % self.RAW], 16)

    def split_hi(self, act, upto):
        while self.hi_issued < len(self.splits) and self.splits[self.hi_issued] <= upto:
            part = self.hi_issued
            ld = self.splits[part]
            n = self.loads[ld][1] * self.loads[ld][2]
            self.wait_whole(act, ld)
            if part >= 2:
                act.wait_ge(*self.loads[self.splits[part - 2]][4])
            self.nc.scalar.activation(self.part_hi[:, part % 2, 0:n], self.raw[:, ld % self.RAW, 0:n],
                                      ACT.Copy).then_inc(self.hi_ready, 1)
            self.hi_issued += 1

    def split_lo(self, pool, upto):
        while self.lo_issued < len(self.splits) and self.splits[self.lo_issued] <= upto:
            part = self.lo_issued
            ld = self.splits[part]
            n = self.loads[ld][1] * self.loads[ld][2]
            pool.wait_ge(self.hi_ready, part + 1)
            self.nc.gpsimd.tensor_tensor(self.part_lo[:, part % 2, 0:n], self.raw[:, ld % self.RAW, 0:n],
                                         self.part_hi[:, part % 2, 0:n].bitcast(F32),
                                         ALU.subtract).then_inc(self.lo_ready, 1)
            self.lo_issued += 1

    def group(self, n=1):
        g = self.groups
        self.groups += n
        return g

    def warm_up(self):
        for _ in range(WARM_UP):
            self.nc.tensor.matmul(self.ps[:, 7, :], self.hot[:, 0:P], self.hot[:, 0:512], start=True, stop=True)

    def wait_x(self, eng, n, i):
        if i in (0, NT - 1):
            eng.wait_ge(self.x_edge_added, 2 * n + 1 + (i > 0))
        else:
            eng.wait_ge(self.x_added, (NT - 2) * n + i)

    def bank(self, g):
        return self.ps[:, g % 4, :]

    def wait_bank(self, pe, g):
        if g >= 4:
            pe.wait_ge(self.proj_taken, g - 3)


class Steps:

    def __init__(self, eng, sem):
        self.eng, self.sem, self.n = eng, sem, 0

    def __call__(self, ins):
        self.n += 1
        ins.then_inc(self.sem, 1)
        self.eng.wait_ge(self.sem, self.n)


def w_cols(w, c0, n):
    return w.rearrange("(k p) m -> p k m", p=P)[:, :, c0:c0 + n]


def project_features(env, pe, ld, rhs, g, cols=P, ready=None):
    nc = env.nc
    hi, lo = env.parts(ld)
    out = env.bank(g)[0:cols]
    env.wait_bank(pe, g)
    env.wait_hi(pe, ld)
    for k in range(KD):
        if ready:
            ready(k)
        nc.tensor.matmul(out, hi[:, k, :], rhs[0][:, k, :], start=(k == 0), stop=False)
        nc.tensor.matmul(out, hi[:, k, :], rhs[1][:, k, :], start=False, stop=False)
    env.wait_lo(pe, ld)
    for k in range(KD):
        mm = nc.tensor.matmul(out, lo[:, k, :], rhs[0][:, k, :], start=False, stop=(k == KD - 1))
    mm.then_inc(env.proj_ready, 1)


def project_tokens(env, pe, lds, lhs, g, kd=KD, elsewhere=0):
    nc = env.nc
    m, n = env.loads[lds[0]][1:3]
    banks = -(-n // 512)
    width = n // banks

    def out(i, b):
        return env.ps[:, 2 * i + b, :] if banks == 2 else env.ps[:, 4 + i, 0:n]

    def highs(index, i):
        hi = env.parts(lds[index])[0]
        for k in range(m):
            for part in range(2):
                for b in range(banks):
                    nc.tensor.matmul(out(i, b), lhs[part][:, index * m + k, i * P:(i + 1) * P],
                                     hi[:, k, b * width:(b + 1) * width],
                                     start=(index + k == 0 and part == 0), stop=False)

    def lows(index, i):
        lo = env.parts(lds[index])[1]
        for k in range(m):
            for b in range(banks):
                stop = index * m + k == kd - 1
                mm = nc.tensor.matmul(out(i, b), lhs[0][:, index * m + k, i * P:(i + 1) * P],
                                      lo[:, k, b * width:(b + 1) * width], start=False, stop=stop)
                if stop:
                    mm.then_inc(env.proj_ready, 1)
        if i == NT - 1 and index < len(lds) - 1:
            mm.then_inc(env.slot_done, 1)

    if g > elsewhere:
        pe.wait_ge(env.proj_taken, g - elsewhere)
    apart = len(lds) - 2 if banks == 2 else len(lds)
    for index in range(apart):
        env.wait_hi(pe, lds[index])
        for i in range(NT):
            highs(index, i)
        env.wait_lo(pe, lds[index])
        for i in range(NT):
            lows(index, i)
    if apart < len(lds):
        a, b = apart, apart + 1
        env.wait_lo(pe, lds[a])
        for index, i in ((a, 0), (a, 1), (a, 2), (b, 0), (a, 3), (b, 1), (b, 2), (b, 3)):
            if (index, i) == (b, 0):
                env.wait_lo(pe, lds[b])
            highs(index, i)
            lows(index, i)


def load_tokens(env, w, c0, n, kd=KD):
    m = env.SLOT // n
    lds = []
    for k in range(0, kd, m):
        lds.append(env.load(w_cols(w, c0, n)[:, k:k + m, :]))
        if k + m < kd:
            env.release_slot(lds[-1])
    g = env.group(NT * -(-n // 512))
    env.release(lds[-1], env.proj_ready, env.groups)
    return lds, g


def load_features(env, w, c0, n, cols=P):
    out = []
    for c in range(c0, c0 + n, cols):
        ld = env.load(w_cols(w, c, cols))
        g = env.group()
        env.release(ld, env.proj_ready, env.groups)
        out.append((ld, g))
    return out


class Stage:
    def __init__(self, env):
        self.env = env

    def tensor(self, pe):
        pass

    def scalar(self, act, step):
        pass

    def vector(self, dve, step):
        pass

    def gpsimd(self, pool, step):
        pass


class Setup(Stage):

    def __init__(self, env):
        super().__init__(env)
        self.bias = env.take(HEADS, T, at=env.words - HEADS * T)
        at = env.area
        self.rows = env.take(6, P, at=at)
        self.tab = env.take(HEADS, at=at + 1000)
        self.tab_rest = env.take(HEADS, at=at + 1016)
        self.hot = env.hot = env.ctx.enter_context(env.nc.sbuf_tensor("one_hot", [P, NDIST], BF16))
        self.tab_hi = env.ctx.enter_context(env.nc.sbuf_tensor("table_parts", [P, 3, HEADS], BF16))
        self.table3 = env.ctx.enter_context(env.nc.sbuf_tensor("table3", [P, HEADS], BF16))
        self.x_arrived = env.sem("x_arrived")
        self.table_ready = env.sem("table_ready")
        self.rows_zeroed = env.sem("rows_zeroed")
        self.bias_ready = env.sem("bias_ready")
        self.bias_taken = env.sem("bias_taken")
        self.vec_ready = env.sem("vec_ready")
        self.rows_arrived = env.sem("rows_arrived")
        self.tab_arrived = env.sem("tab_arrived")
        self.const_arrived = env.sem("const_arrived")

    def load(self, sp):
        env, io, nc = self.env, self.env.io, self.env.nc
        sp.dma_start(env.x, io["x"].rearrange("b (t p) d -> p (b t) d", p=P)).then_inc(self.x_arrived, 16)
        sp.dma_start(env.const, io["shape_constants"]).then_inc(self.const_arrived, 16)
        sp.wait_ge(self.rows_zeroed, 1)
        for part in range(3):
            sp.dma_start(self.tab[32 * part:32 * part + 32, :], io["rel_bias_table"]).then_inc(self.tab_arrived, 16)
        sp.dma_start(self.hot[:], io["distance_one_hot"]).then_inc(self.tab_arrived, 16)
        r = self.rows
        vec = lambda a: a.rearrange("(k p) -> k p", p=P)
        put = lambda row, at, n, src: sp.dma_start(r[at:at + n, row, :], src).then_inc(self.rows_arrived, 16)
        put(0, 0, 16, io["norm_pre"].rearrange("l (k p) -> (l k) p", p=P))
        put(0, 16, 64, io["norm_g_2"].rearrange("l w (k p) -> (l w k) p", p=P))
        put(0, 80, 48, io["mu_2"].rearrange("a i (k p) -> (a i k) p", p=P))
        for n, name in enumerate(["w_decay0_2", "a0_2", "k_k_2", "k_a_2"]):
            put(1, 8 * n, 8, io[name].rearrange("a (k p) -> (a k) p", p=P))
        put(1, 32, 8, io["r_k_2"].rearrange("a (k h) n -> (a k) (h n)", h=2))
        put(1, 40, 8, vec(io["kv_g_2"]))
        put(1, 48, 8, vec(io["diff_subln"][0]))
        for l in range(2):
            w = io["conv_w_2"][l].rearrange("w (k p) -> (w k) p", p=P)
            put(2 + 2 * l, 0, 88, w[0:88])
            put(3 + 2 * l, 0, 44, w[88:132])
            put(3 + 2 * l, 44, 44, vec(io["conv_b_2"][l]))
    N_ROWS = 3 + 4 + 3 + 6

    def tensor(self, pe):
        env, nc = self.env, self.env.nc
        pe.wait_ge(self.rows_arrived, 16 * self.N_ROWS)
        pe.wait_ge(self.const_arrived, 16)
        pe.wait_ge(self.tab_arrived, 64)
        for n in range(6):
            size = [128, 56, 88, 88, 88, 88][n]
            tr = nc.tensor.transpose(env.ps[:, n // 4, (n % 4) * P:(n % 4) * P + size], self.rows[0:size, n, :],
                                     env.ident[0:size, 0:size])
        tr.then_inc(self.vec_ready, 1)

    def bias_tensor(self, pe):
        env, nc = self.env, self.env.nc
        for i in range(8):
            if i >= 4:
                pe.wait_ge(self.bias_taken, i - 3)
            for c in range(32):
                at = DIST0 + P - c - 32 * i
                mm = nc.tensor.matmul(env.ps[:, 4 + i % 4, c * HEADS:(c + 1) * HEADS], self.hot[:, at:at + P],
                                      self.table3[:], start=True, stop=True)
            mm.then_inc(self.bias_ready, 1)

    def vector(self, dve, step):
        env, nc = self.env, self.env.nc
        nc.vector.memset(env.eps, EPS)
        nc.vector.memset(self.tab[:], 0.0).then_inc(self.rows_zeroed, 1)
        dve.wait_ge(self.tab_arrived, 64)
        dve.wait_ge(self.rows_zeroed, 1)
        step(nc.vector.tensor_copy(self.tab_hi[:, 0, :], self.tab))
        step(nc.vector.tensor_tensor(self.tab_rest, self.tab, self.tab_hi[:, 0, :], ALU.subtract))
        step(nc.vector.tensor_copy(self.tab_hi[:, 1, :], self.tab_rest))
        step(nc.vector.tensor_tensor(self.tab_rest, self.tab_rest, self.tab_hi[:, 1, :], ALU.subtract))
        step(nc.vector.tensor_copy(self.tab_hi[:, 2, :], self.tab_rest))
        for part in range(3):
            q = slice(32 * part, 32 * part + 32)
            nc.vector.tensor_copy(self.table3[q, :], self.tab_hi[q, part, :])
        nc.vector.memset(self.table3[96:128, :], NEG).then_inc(self.table_ready, 1)
        dve.wait_ge(self.vec_ready, 1)
        o = 0
        for n in range(6):
            size = [128, 56, 88, 88, 88, 88][n]
            step(nc.vector.tensor_copy(env.vec[:, o:o + size], env.ps[:, n // 4, (n % 4) * P:(n % 4) * P + size]))
            o += size

    def bias_vector(self, dve, step):
        env, nc = self.env, self.env.nc
        for i in range(8):
            dve.wait_ge(self.bias_ready, i + 1)
            nc.vector.tensor_copy(
                self.bias.rearrange("p h c -> p c h")[:, 2 * P + 32 * i:2 * P + 32 * (i + 1), :],
                env.ps[:, 4 + i % 4, :].rearrange("p (c h) -> p c h", h=HEADS)).then_inc(self.bias_taken, 1)
        dve.wait_ge(self.bias_taken, 8)
        step(nc.vector.tensor_copy(self.bias[:, :, 0:2 * P],
                                   self.bias[:, :, 2 * P:2 * P + 1].to_broadcast([P, HEADS, 2 * P])))


class Renorm:

    def __init__(self, env, g_row, u):
        self.env, self.g_row, self.u = env, g_row, u
        self.rms_n = env.norms - NT * env.repeats
        self.n, self.hi_n, self.g_n = env.norms, env.uhis, env.norms // NT + 1
        env.norms += NT
        if len(u) == 2:
            env.uhis += NT
        self.un = env.big.rearrange("p (t d) -> p t d", t=NT)
        self.ssq, self.rms, self.rstd = env.stat[:, 0:4], env.stat[:, 4:8], env.stat[:, 8:12]

    def fetch(self, pool):
        env = self.env
        pool.dma_start(env.next_g, self.g_row.partition_broadcast(P)).then_inc(env.next_g_arrived, 16)

    def square(self, act, step, i):
        env, nc = self.env, self.env.nc
        step(nc.scalar.activation(self.un[:, i, :], env.x[:, i, :], ACT.Square, accum_out=self.ssq[:, i:i + 1]))
        nc.scalar.activation(self.rms[:, i:i + 1], self.ssq[:, i:i + 1], ACT.Sqrt, scale=1.0 / D,
                             bias=env.eps).then_inc(env.rms_ready, 1)

    def scale(self, dve, step, i, again=False):
        env, nc = self.env, self.env.nc
        if not again:
            dve.wait_ge(env.rms_ready, self.rms_n + i + 1)
            step(nc.vector.reciprocal(self.rstd[:, i:i + 1], self.rms[:, i:i + 1]))
        dve.wait_ge(env.next_g_arrived, 16 * self.g_n)
        nc.vector.scalar_tensor_tensor(self.un[:, i, :], env.x[:, i, :], self.rstd[:, i:i + 1], env.next_g,
                                       ALU.mult, ALU.mult).then_inc(env.un_ready, 1)

    def turn(self, pe, i):
        env, nc = self.env, self.env.nc
        pe.wait_ge(env.un_ready, self.n + i + 1)
        for k in range(KD):
            tr = nc.tensor.transpose(env.ps[:, 2 * i + k // 4, (k % 4) * P:(k % 4 + 1) * P],
                                     self.un[:, i, k * P:(k + 1) * P], env.ident)
        tr.then_inc(env.un_turned, 1)

    def turned(self, i):
        return self.env.ps[:, 2 * i:2 * i + 2, :].rearrange("p b (k t) -> p (b k) t", t=P)

    def high(self, act, i):
        env, nc = self.env, self.env.nc
        act.wait_ge(env.un_turned, self.n + i + 1)
        nc.scalar.activation(self.u[0][:, :, i * P:(i + 1) * P], self.turned(i),
                             ACT.Copy).then_inc(env.uhi_ready if len(self.u) == 2 else env.uT_ready, 1)

    def low(self, dve, i):
        env, nc = self.env, self.env.nc
        if len(self.u) == 2:
            dve.wait_ge(env.uhi_ready, self.hi_n + i + 1)
            nc.vector.tensor_tensor(self.u[1][:, :, i * P:(i + 1) * P], self.turned(i),
                                    self.u[0][:, :, i * P:(i + 1) * P].bitcast(F32),
                                    ALU.subtract).then_inc(env.uT_ready, 1)

    def wait(self, pe):
        pe.wait_ge(self.env.uT_ready, self.n + NT)


class Norm(Stage):

    def __init__(self, env, g_row, u, x_arrived):
        super().__init__(env)
        self.norm, self.x_arrived = Renorm(env, g_row, u), x_arrived

    def gpsimd(self, pool, step):
        self.norm.fetch(pool)
        self.env.split_lo(pool, 1)

    def scalar(self, act, step):
        act.wait_ge(self.x_arrived, 16)
        for i in range(NT):
            self.norm.square(act, step, i)
        self.env.split_hi(act, 1)
        for i in range(NT):
            self.norm.high(act, i)

    def vector(self, dve, step):
        for i in range(NT):
            self.norm.scale(dve, step, i)
        for i in range(NT):
            self.norm.low(dve, i)

    def tensor(self, pe):
        for i in range(NT):
            self.norm.turn(pe, i)
        self.norm.wait(pe)


class NormAgain(Stage):

    def __init__(self, env, norm):
        super().__init__(env)
        self.norm = norm

    def scalar(self, act, step):
        for i in range(NT):
            self.norm.high(act, i)

    def vector(self, dve, step):
        for i in range(NT):
            self.norm.low(dve, i)

    def tensor(self, pe):
        for i in range(NT):
            self.norm.turn(pe, i)
        self.norm.wait(pe)


class Output(Stage):

    def __init__(self, env, w_out, g_row, oT, o=None, z=None, kd=KD, following=None):
        super().__init__(env)
        self.o, self.oT, self.kd, self.g_row, self.z = o, oT, kd, g_row, z
        self.n = env.outs
        env.outs += 1
        self.ot0, self.tr0 = env.ots, env.trs
        if o is not None:
            env.ots += KD
            env.trs += KD
        self.lds, self.g0 = load_tokens(env, w_out, 0, D, kd)
        self.y = env.big.rearrange("p (t d) -> p t d", t=NT)
        self.ssq, self.rms, self.rstd = env.stat[:, 16:20], env.stat[:, 20:24], env.stat[:, 24:28]
        self.tmp = env.pair_tmp
        self.norm = Renorm(env, *following) if following else None

    def tensor(self, pe):
        env, nc = self.env, self.env.nc
        if self.o is not None:
            for k in range(KD):
                if k >= 2:
                    pe.wait_ge(env.otmp_ready, self.ot0 + k - 1)
                for t in range(NT):
                    tr = nc.tensor.transpose(env.ps[:, 6 + k % 2, t * P:(t + 1) * P],
                                             self.o[:, t, k * P:(k + 1) * P], env.ident)
                tr.then_inc(env.tr_ready, 1)
            pe.wait_ge(env.oT_ready, self.ot0 + KD)
        project_tokens(env, pe, self.lds, self.oT, self.g0, self.kd)
        if self.norm:
            for i in range(NT):
                self.norm.turn(pe, i)
            self.norm.wait(pe)

    def scalar(self, act, step):
        env, nc = self.env, self.env.nc
        env.split_hi(act, self.lds[0])
        for k in range(KD if self.o is not None else 0):
            act.wait_ge(env.otmp_ready, self.ot0 + k + 1)
            nc.scalar.activation(self.oT[0][:, k, :], self.tmp[:, k % 2, :], ACT.Copy).then_inc(env.oT_hi_ready, 1)
        env.split_hi(act, self.lds[-1])
        nc.scalar.activation(env.sqrt_junk, env.eps, ACT.Sqrt)
        for i in range(NT + 3):
            if i < NT:
                act.wait_ge(env.proj_ready, self.g0 + 2 * i + 2)
                step(nc.scalar.activation(self.y[:, i, :].rearrange("p (b n) -> p b n", b=2),
                                          env.ps[:, 2 * i:2 * i + 2, :], ACT.Square,
                                          accum_out=self.ssq[:, i:i + 1]))
                nc.scalar.activation(self.rms[:, i:i + 1], self.ssq[:, i:i + 1], ACT.Sqrt, scale=1.0 / D,
                                     bias=env.eps).then_inc(env.yrms_ready, 1)
            if self.norm and 1 <= i <= NT:
                env.wait_x(act, self.n, i - 1)
                self.norm.square(act, step, i - 1)
            if self.norm and i >= 3:
                self.norm.high(act, i - 3)
                env.split_hi(act, self.lds[-1] + min(i - 2, 2))

    def gpsimd(self, pool, step):
        env = self.env
        pool.dma_start(env.post_g, self.g_row.partition_broadcast(P)).then_inc(env.g_arrived, 16)
        if self.norm:
            env.split_lo(pool, self.lds[0])
            if self.o is not None:
                pool.wait_ge(env.oT_ready, self.ot0 + KD)
            self.norm.fetch(pool)
        env.split_lo(pool, self.lds[-1])
        for i in range(1, NT - 1):
            pool.wait_ge(env.proj_taken, self.g0 + 2 * i + 2)
            env.nc.gpsimd.tensor_tensor(env.x[:, i, :], env.x[:, i, :], self.y[:, i, :],
                                        ALU.add).then_inc(env.x_added, 1)
        env.split_lo(pool, self.lds[-1] + 2)

    def vector(self, dve, step):
        env, nc = self.env, self.env.nc
        for k in range(KD if self.o is not None else 0):
            tr, tmp = env.ps[:, 6 + k % 2, :], self.tmp[:, k % 2, :]
            dve.wait_ge(env.tr_ready, self.tr0 + k + 1)
            if k >= 2:
                dve.wait_ge(env.oT_ready, self.ot0 + k - 1)
            if self.z is not None:
                nc.vector.tensor_tensor(tmp, tr, self.z[:, k, :], ALU.mult).then_inc(env.otmp_ready, 1)
            else:
                nc.vector.tensor_copy(tmp, tr).then_inc(env.otmp_ready, 1)
            if k:
                self.low(dve, k - 1)
        if self.o is not None:
            self.low(dve, KD - 1)
        dve.wait_ge(env.g_arrived, 16 * (self.n + 1))
        for i in range(NT + 3):
            if i < NT:
                dve.wait_ge(env.yrms_ready, NT * self.n + i + 1)
                step(nc.vector.reciprocal(self.rstd[:, i:i + 1], self.rms[:, i:i + 1]))
                y = self.y[:, i, :]
                nc.vector.scalar_tensor_tensor(y, env.ps[:, 2 * i:2 * i + 2, :].rearrange("p b n -> p (b n)"),
                                               self.rstd[:, i:i + 1], env.post_g, ALU.mult,
                                               ALU.mult).then_inc(env.proj_taken, 2)
            if i in (0, NT - 1):
                dve.wait_ge(env.proj_taken, self.g0 + 2 * i + 2)
                nc.vector.tensor_tensor(env.x[:, i, :], env.x[:, i, :], y, ALU.add).then_inc(env.x_edge_added, 1)
            if self.norm and 1 <= i <= NT:
                self.norm.scale(dve, step, i - 1)
            if self.norm and i >= 3:
                self.norm.low(dve, i - 3)

    def low(self, dve, k):
        env = self.env
        dve.wait_ge(env.oT_hi_ready, self.ot0 + k + 1)
        env.nc.vector.tensor_tensor(self.oT[1][:, k, :], self.tmp[:, k % 2, :], self.oT[0][:, k, :].bitcast(F32),
                                    ALU.subtract).then_inc(env.oT_ready, 1)


class NsaProject(Stage):

    def __init__(self, env, m, setup):
        super().__init__(env)
        self.m, self.setup = m, setup
        w = env.io["nsa_w_in"][0]
        width = GROUPS * DH
        self.q = load_features(env, w, 0, D)
        self.kvc = load_features(env, w, D, 2 * width)
        self.branches = []
        for br in range(2):
            at = D + (2 + 2 * br) * width
            self.branches.append((load_features(env, w, at, width), load_tokens(env, w, at + width, width)))
        at = D + 6 * width
        self.gates = (env.load(w_cols(w, at, 3 * HEADS)), env.group(NT))
        env.release(self.gates[0], env.proj_ready, env.groups)
        self.z = load_features(env, w, at + 3 * HEADS, D)

    def tensor(self, pe):
        env, nc = self.env, self.env.nc
        u = self.m.u
        for ld, g in self.q + self.kvc:
            project_features(env, pe, ld, u, g)
        self.setup.bias_tensor(pe)
        pe.wait_ge(self.setup.bias_taken, 8)
        for keys, (lds, g) in self.branches:
            for ld, gk in keys:
                project_features(env, pe, ld, u, gk)
            project_tokens(env, pe, lds, u, g, elsewhere=len(keys))
        ld, g = self.gates
        project_tokens(env, pe, [ld], u, g)
        for ld, g in self.z:
            project_features(env, pe, ld, u, g)

    def vector(self, dve, step):
        self.setup.bias_vector(dve, step)

    def gpsimd(self, pool, step):
        m, io = self.m, self.env.io
        for to in range(2):
            pool.dma_start(m.w2[:, 64 * to:64 * to + 64], io["nsa_cmp_w2_k"][0]).then_inc(m.small_arrived, 16)
        pool.dma_start(m.w2[:, 128:192], io["nsa_cmp_w2_v"][0]).then_inc(m.small_arrived, 16)
        for kv, name in enumerate(("nsa_cmp_pe_k", "nsa_cmp_pe_v")):
            pool.dma_start(m.pe_rows[0:CMP_K, kv, :],
                           io[name][0].rearrange("(k two) d -> k (two d)", two=2)).then_inc(m.small_arrived, 16)
        self.env.split_lo(pool, self.z[-1][0])

    def scalar(self, act, step):
        env, nc, m = self.env, self.env.nc, self.m
        env.split_hi(act, self.q[0][0])
        for j, (ld, g) in enumerate(self.q):
            env.split_hi(act, ld + 1)
            act.wait_ge(env.proj_ready, g + 1)
            nc.scalar.activation(m.qT[:, j, :], env.bank(g), ACT.Copy, scale=DH ** -0.5).then_inc(env.proj_taken, 1)
        for j, (ld, g) in enumerate(self.kvc):
            env.split_hi(act, ld + 1)
            dst = (m.kcT, m.vcT)[j // 2]
            act.wait_ge(env.proj_ready, g + 1)
            for half in range(2):
                src = env.bank(g)[64 * half:64 * half + 64, :]
                grp = 2 * (j % 2) + half
                nc.scalar.activation(dst[0:64, grp, :], src, ACT.Copy)
                cp = nc.scalar.activation(dst[64:128, grp, 0:T - 1], src[:, 1:T], ACT.Copy)
            cp.then_inc(env.proj_taken, 1)
        for (keys, (lds, g)), (kT, v) in zip(self.branches, ((m.ksT, m.vs), (m.kwT, m.vw))):
            for j, (ld, gk) in enumerate(keys):
                env.split_hi(act, ld + 1)
                act.wait_ge(env.proj_ready, gk + 1)
                for half in range(2):
                    for to in range(2):
                        cp = nc.scalar.activation(kT[64 * to:64 * to + 64, 2 * j + half, :],
                                                  env.bank(gk)[64 * half:64 * half + 64, :], ACT.Copy)
                cp.then_inc(env.proj_taken, 1)
            env.split_hi(act, lds[-1] + 1)
            for i in range(NT):
                act.wait_ge(env.proj_ready, g + i + 1)
                nc.scalar.activation(v[:, i, :], env.ps[:, 4 + i, 0:256], ACT.Copy).then_inc(env.proj_taken, 1)
        ld, g = self.gates
        env.split_hi(act, ld + 1)
        for i in range(NT):
            act.wait_ge(env.proj_ready, g + i + 1)
            nc.scalar.activation(m.gate[:, i, :], env.ps[:, 4 + i, 0:3 * HEADS],
                                 ACT.Sigmoid).then_inc(env.proj_taken, 1)
        for k, (ld, g) in enumerate(self.z):
            env.split_hi(act, ld + 1)
            act.wait_ge(env.proj_ready, g + 1)
            nc.scalar.activation(m.z[:, k, :], env.bank(g), ACT.Silu).then_inc(env.proj_taken, 1)
        env.split_hi(act, self.z[-1][0] + 2)


class NsaCompress(Stage):

    def __init__(self, env, m):
        super().__init__(env)
        self.m = m
        self.w1 = []
        for name in ("nsa_cmp_w1_k", "nsa_cmp_w1_v"):
            w = env.io[name][0].rearrange("(k p) n -> p k n", p=P)
            for k in range(0, CMP_K, 8):
                self.w1.append(env.load(w[:, k:k + 8, :], split=False))
                if k == 0:
                    env.release_slot(self.w1[-1])
        self.pe_rows_turned = env.sem("pe_rows_turned")
        self.pe_cols = env.sem("pe_cols_taken")
        self.hid_bias = env.sem("hid_bias")
        self.hid_bias_taken = env.sem("hid_bias_taken")
        self.hid_ready = env.sem("hid_ready")
        self.hid_taken = env.sem("hid_taken")
        for kv in range(2):
            env.release(self.w1[2 * kv + 1], self.hid_ready, kv + 1)
        self.cmp_ready = env.sem("cmp_ready")

    def tensor(self, pe):
        env, nc, m = self.env, self.env.nc, self.m
        pe.wait_ge(m.small_arrived, 16 * 5)
        for kv in range(2):
            tr = nc.tensor.transpose(env.ps[:, 4, kv * CMP_K:(kv + 1) * CMP_K], m.pe_rows[0:CMP_K, kv, :],
                                     env.ident[0:CMP_K, 0:CMP_K])
        tr.then_inc(self.pe_rows_turned, 1)
        pe.wait_ge(self.pe_cols, 1)
        for kv, src in enumerate((m.kcT, m.vcT)):
            for k in range(CMP_K):
                ld = self.w1[2 * kv + k // 8]
                if k % 8 == 0:
                    env.wait_whole(pe, ld)
                w = env.whole(ld)[:, k % 8, :]
                edge = dict(start=(k == 0), stop=(k == CMP_K - 1))
                bias = nc.tensor.matmul(env.ps[:, 5, 2 * kv:2 * kv + 2],
                                        w, m.pe_cols[:, kv * CMP_K + k:kv * CMP_K + k + 1].to_broadcast([P, 2]), **edge)
                if k == CMP_K - 1:
                    bias.then_inc(self.hid_bias, 1)
                mm = nc.tensor.matmul(env.ps[:, 6 + kv, 0:GROUPS * NC], w,
                                      src[:, :, 2 * k:2 * k + CMP_STRIDE * (NC - 1) + 1:CMP_STRIDE], **edge)
                if k == CMP_K // 2 - 1:
                    mm.then_inc(env.slot_done, 1)
            mm.then_inc(self.hid_ready, 1)
        pe.wait_ge(self.hid_taken, 2)
        nc.tensor.matmul(env.ps[:, 4, 0:GROUPS * NC], m.w2[:, 0:128], m.hid[:, 0, 0:GROUPS * NC], start=True, stop=True)
        for g in range(GROUPS):
            mm = nc.tensor.matmul(env.ps[0:NC, 5, g * DH:(g + 1) * DH], m.hid[:, 1, g * NC:(g + 1) * NC],
                                  m.w2[:, 128:192], start=True, stop=True)
        mm.then_inc(self.cmp_ready, 1)

    def scalar(self, act, step):
        env, nc, m = self.env, self.env.nc, self.m
        act.wait_ge(self.hid_bias_taken, 1)
        for kv in range(2):
            act.wait_ge(self.hid_ready, kv + 1)
            nc.scalar.activation(m.hid[:, kv, 0:GROUPS * NC], env.ps[:, 6 + kv, 0:GROUPS * NC], ACT.Silu,
                                 bias=m.hid_bias[:, 2 * kv:2 * kv + 1]).then_inc(self.hid_taken, 1)

    def vector(self, dve, step):
        env, nc, m = self.env, self.env.nc, self.m
        nc.vector.memset(m.vbd, 0.0)
        step(nc.vector.memset(m.kcmp, 0.0))
        dve.wait_ge(self.pe_rows_turned, 1)
        nc.vector.tensor_copy(m.pe_cols, env.ps[:, 4, 0:2 * CMP_K]).then_inc(self.pe_cols, 1)
        dve.wait_ge(self.hid_bias, 2)
        nc.vector.tensor_copy(m.hid_bias, env.ps[:, 5, 0:4]).then_inc(self.hid_bias_taken, 1)
        dve.wait_ge(self.cmp_ready, 1)
        step(nc.vector.tensor_copy(m.kcmp[:, :, 0:NC], env.ps[:, 4, 0:GROUPS * NC].rearrange("p (g c) -> p g c", c=NC)))
        for j in range(HPG):
            step(nc.vector.tensor_copy(m.vbd[32 * j:32 * j + NC, :, DH * j:DH * j + DH],
                                       env.ps[0:NC, 5, 0:GROUPS * DH].rearrange("p (g d) -> p g d", d=DH)))


class NsaCompressed(Stage):

    def __init__(self, env, m):
        super().__init__(env)
        self.m = m
        self.bias_ready, self.bias_taken = env.sem("cbias_ready"), env.sem("cbias_taken")
        self.s_ready, self.s_taken = env.sem("cs_ready"), env.sem("cs_taken")
        self.shifted, self.p_ready, self.p_scaled = env.sem("c_shifted"), env.sem("cp_ready"), env.sem("cp_scaled")
        self.pT_ready, self.pT_taken = env.sem("cpT_ready"), env.sem("cpT_taken")
        self.o_ready, self.o_taken = env.sem("co_ready"), env.sem("co_taken")

    def tensor(self, pe):
        env, nc, m = self.env, self.env.nc, self.m

        def scores(i):
            if i:
                pe.wait_ge(self.bias_taken, i)
            out = env.ps[:, 6, :].rearrange("p (h c) -> p h c", c=NCP)
            for c in range(NCP):
                at = DIST0 + P * i - CMP_STRIDE * c - (CMP_BLOCK - 1)
                mm = nc.tensor.matmul(out[:, :, c], m.hot[:, at:at + P], m.table3[:], start=True, stop=True)
            mm.then_inc(self.bias_ready, 1)
            if i:
                pe.wait_ge(self.s_taken, i)
            for h in range(HEADS):
                half = 64 * (h % 2)
                mm = nc.tensor.matmul(env.ps[:, 7 - 5 * (h % 2), h // 2 * NCP:(h // 2 + 1) * NCP],
                                      m.qT[half:half + 64, h // 2, i * P:(i + 1) * P],
                                      m.kcmp[half:half + 64, h // HPG, :], start=True, stop=True)
            mm.then_inc(self.s_ready, 1)

        scores(0)
        for i in range(NT):
            if i + 1 < NT:
                scores(i + 1)
            pe.wait_ge(self.p_scaled, i + 1)
            if i:
                pe.wait_ge(self.pT_taken, i)
            for g in range(GROUPS):
                tr = nc.tensor.transpose(env.ps[:, 5, g * P:(g + 1) * P], m.pc[:, g * P:(g + 1) * P], env.ident)
            tr.then_inc(self.pT_ready, 1)
            pe.wait_ge(self.pT_taken, i + 1)
            if i:
                pe.wait_ge(self.o_taken, i)
            for g in range(GROUPS):
                mm = nc.tensor.matmul(env.ps[:, 3 + g // 2, (g % 2) * 256:(g % 2) * 256 + 256],
                                      m.pcT[:, g * P:(g + 1) * P], m.vbd[:, g, :], start=True, stop=True)
            mm.then_inc(self.o_ready, 1)

    def gpsimd(self, pool, step):
        nc, m = self.env.nc, self.m
        nc.gpsimd.memset(m.q_odd[0:64], 0.0)
        step(nc.gpsimd.tensor_copy(m.q_odd[64:128], m.qT[64:128]))
        pool.wait_ge(self.s_ready, NT)
        nc.gpsimd.memset(m.qT[64:128], 0.0)

    def scalar(self, act, step):
        env, nc, m = self.env, self.env.nc, self.m

        def exp(i):
            act.wait_ge(self.shifted, i + 1)
            if i:
                act.wait_ge(self.pT_ready, i)
            nc.scalar.activation(m.pc, m.sc[:, i % 2, :], ACT.Exp).then_inc(self.p_ready, 1)

        exp(0)
        for i in range(NT):
            if i + 1 < NT:
                exp(i + 1)
            act.wait_ge(self.o_ready, i + 1)
            nc.scalar.activation(m.o[:, i, :].rearrange("p (b n) -> p b n", b=2), env.ps[:, 3:5, :],
                                 ACT.Copy).then_inc(self.o_taken, 1)

    def vector(self, dve, step):
        env, nc, m = self.env, self.env.nc, self.m
        pc = m.pc.rearrange("p (h c) -> p h c", c=NCP)
        col = m.cstat
        wide = lambda v: v.unsqueeze(2).to_broadcast([P, HEADS, NCP])

        def take(i):
            dve.wait_ge(self.bias_ready, i + 1)
            if i >= 2:
                dve.wait_ge(self.p_ready, i - 1)
            nc.vector.tensor_copy(m.sc[:, i % 2, :], env.ps[:, 6, :]).then_inc(self.bias_taken, 1)
            dve.wait_ge(self.bias_taken, i + 1)
            dve.wait_ge(self.s_ready, i + 1)
            for odd in range(2):
                part = m.sc[:, i % 2, :].rearrange("p (h two c) -> p h two c", two=2, c=NCP)[:, :, odd, :]
                add = nc.vector.tensor_tensor(part, env.ps[:, 7 - 5 * odd, 0:256].rearrange("p (h c) -> p h c", c=NCP),
                                              part, ALU.add)
            add.then_inc(self.s_taken, 1)
            dve.wait_ge(self.s_taken, i + 1)

        take(0)
        for i in range(NT):
            sc = m.sc[:, i % 2, :].rearrange("p (h c) -> p h c", c=NCP)
            step(nc.vector.tensor_reduce(col[:, 0, :], sc, AX, ALU.max))
            step(nc.vector.tensor_scalar(col[:, 0, :], col[:, 0, :], -1e20, None, ALU.max))
            nc.vector.tensor_tensor(sc, sc, wide(col[:, 0, :]), ALU.subtract).then_inc(self.shifted, 1)
            if i + 1 < NT:
                take(i + 1)
            dve.wait_ge(self.p_ready, i + 1)
            step(nc.vector.tensor_reduce(col[:, 1, :], pc, AX, ALU.add))
            step(nc.vector.tensor_scalar(col[:, 1, :], col[:, 1, :], 1e-30, None, ALU.max))
            step(nc.vector.reciprocal(col[:, 2, :], col[:, 1, :]))
            gate = m.gate[:, i, :].rearrange("p (h b) -> p h b", b=3)[:, :, 0]
            step(nc.vector.tensor_tensor(col[:, 2, :], col[:, 2, :], gate, ALU.mult))
            nc.vector.tensor_tensor(pc, pc, wide(col[:, 2, :]), ALU.mult).then_inc(self.p_scaled, 1)
            dve.wait_ge(self.pT_ready, i + 1)
            if i:
                dve.wait_ge(self.o_ready, i)
            nc.vector.tensor_copy(m.pcT, env.ps[:, 5, :]).then_inc(self.pT_taken, 1)


class Attend(Stage):

    def __init__(self, env, prefix):
        super().__init__(env)
        s = env.sem
        self.s_ready = s(prefix + "scores_ready")
        self.s_biased = s(prefix + "scores_biased")
        self.p_ready = s(prefix + "probs_ready")
        self.pT_ready = s(prefix + "probsT_ready")
        self.pT_copied = s(prefix + "probsT_copied")
        self.pv_done = s(prefix + "pv_done")
        self.o_taken = s(prefix + "o_taken")


class NsaAttend(Attend):

    def __init__(self, env, m, ahead):
        super().__init__(env, "nsa_")
        self.m, self.ahead = m, ahead
        self.o_added = env.sem("nsa_o_added")
        self.odd_copied = env.sem("nsa_odd_probsT_copied")
        self.units = [(i, g, br, j) for i in reversed(range(NT)) for g in range(GROUPS) for br in range(2) for j in range(HPG)]

    def tensor(self, pe):
        env, nc, m = self.env, self.env.nc, self.m
        n_units = len(self.units)

        def scores(u):
            i, g, br, j = self.units[u]
            h = HPG * g + j
            if u >= 3:
                pe.wait_ge(self.s_biased, u - 2)
            nc.tensor.matmul(env.ps[:, u % 3, 0:P * (i + 1)], (m.qT, m.q_odd)[h % 2][:, h // 2, i * P:(i + 1) * P],
                             (m.ksT, m.kwT)[br][:, g, 0:P * (i + 1)],
                             start=True, stop=True).then_inc(self.s_ready, 1)

        def turn(u):
            i = self.units[u][0]
            pe.wait_ge(self.p_ready, u + 1)
            if u >= 3:
                self.copied(pe, u - 3)
            for kt in range(i + 1):
                tr = nc.tensor.transpose(env.ps[:, 3 + u % 3, kt * P:(kt + 1) * P], m.p[:, u % 4, kt * P:(kt + 1) * P],
                                         env.ident)
            tr.then_inc(self.pT_ready, 1)

        def values(u):
            i, g, br, j = self.units[u]
            b = u // 8
            self.copied(pe, u)
            if u % 8 == 0 and b >= 2:
                pe.wait_ge(self.o_taken, b - 1)
            v = (m.vs, m.vw)[br]
            for kt in range(i + 1):
                mm = nc.tensor.matmul(env.ps[:, 6 + b % 2, (u % 8) * DH:(u % 8 + 1) * DH],
                                      m.pT[:, u % 3, kt * P:(kt + 1) * P], v[:, kt, g * DH:(g + 1) * DH],
                                      start=(kt == 0), stop=(kt == i))
            mm.then_inc(self.pv_done, 1)

        env.warm_up()
        for u in range(n_units + 3):
            if u < n_units:
                scores(u)
            if 2 <= u <= n_units + 1:
                turn(u - 2)
            if u >= 3:
                values(u - 3)

    def copied(self, eng, u):
        if u % 2:
            eng.wait_ge(self.odd_copied, u // 2 + 1)
        else:
            eng.wait_ge(self.pT_copied, u // 2 + 1)

    def scalar(self, act, step):
        env, nc, m = self.env, self.env.nc, self.m
        n_units = len(self.units)

        def exp(u):
            n, b = P * (self.units[u][0] + 1), u // 8
            act.wait_ge(self.s_biased, u + 1)
            if u % 8 == 0 and b >= 2:
                act.wait_ge(self.o_taken, b - 1)
            nc.scalar.activation(m.p[:, u % 4, 0:n], m.p[:, u % 4, 0:n], ACT.Exp, scale=-1.0,
                                 bias=m.nmax[:, u % 16:u % 16 + 1],
                                 accum_out=m.psum[:, u % 16:u % 16 + 1]).then_inc(self.p_ready, 1)

        def copy(u):
            n = P * (self.units[u][0] + 1)
            act.wait_ge(self.pT_ready, u + 1)
            if u >= 3:
                act.wait_ge(self.pv_done, u - 2)
            nc.scalar.activation(m.pT[:, u % 3, 0:n], env.ps[:, 3 + u % 3, 0:n], ACT.Copy).then_inc(self.odd_copied, 1)

        env.split_hi(act, self.ahead)
        for u in range(n_units + 2):
            if u >= 2 and u % 2:
                copy(u - 2)
            if u < n_units:
                exp(u)

    def gpsimd(self, pool, step):
        self.env.split_lo(pool, self.ahead)
        nc, m = self.env.nc, self.m
        for b in range(len(self.units) // 8):
            i, g = self.units[8 * b][0:2]
            o = m.o[:, i, 256 * g:256 * g + 256]
            pool.wait_ge(self.o_taken, b + 1)
            step(nc.gpsimd.tensor_tensor(o, o, m.otmp[:, 0:256], ALU.add))
            nc.gpsimd.tensor_tensor(o, o, m.otmp[:, 256:512], ALU.add).then_inc(self.o_added, 1)

    def vector(self, dve, step):
        env, nc, m = self.env, self.env.nc, self.m
        n_units = len(self.units)

        def bias(u):
            i, g, br, j = self.units[u]
            n = P * (i + 1)
            dve.wait_ge(self.s_ready, u + 1)
            if u >= 4:
                dve.wait_ge(self.pT_ready, u - 3)
            nc.vector.tensor_tensor_reduce(m.p[:, u % 4, 0:n], env.ps[:, u % 3, 0:n], m.bias[:, HPG * g + j, T - n:T],
                                           -1.0, 1e38, ALU.add, ALU.min,
                                           m.nmax[:, u % 16:u % 16 + 1]).then_inc(self.s_biased, 1)

        def copy(u):
            n = P * (self.units[u][0] + 1)
            dve.wait_ge(self.pT_ready, u + 1)
            if u >= 3:
                dve.wait_ge(self.pv_done, u - 2)
            nc.vector.tensor_copy(m.pT[:, u % 3, 0:n], env.ps[:, 3 + u % 3, 0:n]).then_inc(self.pT_copied, 1)

        def combine(b):
            i, g = self.units[8 * b][0:2]
            dve.wait_ge(self.pv_done, 8 * b + 8)
            at = 8 * (b % 2)
            step(nc.vector.reciprocal(m.scale[:, 0:8], m.psum[:, at:at + 8]))
            gate = m.gate[:, i, 12 * g:12 * g + 12].rearrange("p (j b) -> p b j", b=3)[:, 1:3, :]
            sc = m.scale[:, 0:8].rearrange("p (b j) -> p b j", b=2)
            step(nc.vector.tensor_tensor(sc, sc, gate, ALU.mult))
            if b:
                dve.wait_ge(self.o_added, b)
            nc.vector.tensor_tensor(m.otmp.rearrange("p (u d) -> p u d", d=DH),
                                    env.ps[:, 6 + b % 2, :].rearrange("p (u d) -> p u d", d=DH),
                                    m.scale[:, 0:8].unsqueeze(2).to_broadcast([P, 8, DH]),
                                    ALU.mult).then_inc(self.o_taken, 1)

        for u in range(n_units + 5):
            if u < n_units:
                bias(u)
            if 2 <= u <= n_units + 1 and u % 2 == 0:
                copy(u - 2)
            if u >= 12 and (u - 4) % 8 == 0:
                combine((u - 4) // 8 - 1)


class NsaMemory:
    def __init__(self, env, bias, setup):
        at = env.area

        def take(*shape):
            nonlocal at
            v = env.take(*shape, at=at)
            at += int(np.prod(shape))
            return v
        self.bias = bias
        self.hot, self.table3 = setup.hot, setup.table3
        self.qT = take(KD, T)
        self.ksT, self.kwT = take(GROUPS, T), take(GROUPS, T)
        self.z = take(KD, T)
        lo_at = at
        at += KD * T
        self.vs, self.vw = take(NT, 256), take(NT, 256)
        assert at <= env.words - HEADS * T
        at = lo_at
        self.u = [env.take_r("nsa_u_hi", KD, T, at=env.uT_at), env.take_r("nsa_u_lo", KD, T, at=lo_at)]
        self.sc, self.pc = take(2, 512), take(512)
        self.pcT = take(512)
        self.vbd = take(GROUPS, 256)
        self.kcmp = take(GROUPS, NCP)
        self.hid = take(2, P)
        assert at <= lo_at + KD * T
        at = lo_at
        self.p, self.pT, self.otmp = take(4, 512), take(3, 512), take(512)
        assert at <= lo_at + KD * T
        self.q_odd = env.take(KD, T, at=env.uT_at)
        small = Area(env, env.post_g_at)
        self.w2 = small(192)
        self.pe_rows = small(2, P)
        self.pe_cols = small(2 * CMP_K)
        self.hid_bias = small(4)
        assert small.at <= env.post_g_at + D
        self.small_arrived = env.sem("small_arrived")
        small = Area(env, env.small_at)
        self.gate = small(NT, 3 * HEADS)
        self.cstat = small(3, HEADS)
        self.nmax, self.psum, self.scale = small(16), small(16), small(16)
        self.kcT = env.big[:, 0:2048].rearrange("p (g t) -> p g t", g=GROUPS)
        self.vcT = env.big[:, 2048:4096].rearrange("p (g t) -> p g t", g=GROUPS)
        self.o = env.big.rearrange("p (t d) -> p t d", t=NT)


class Area:

    def __init__(self, env, at=None):
        self.env, self.at = env, env.area if at is None else at

    def __call__(self, *shape):
        v = self.env.take(*shape, at=self.at)
        n = int(np.prod(shape))
        self.at += n + -n % 8
        return v


class DiffMemory:
    def __init__(self, env, bias):
        take = Area(env)
        self.bias = bias
        self.qT, self.kT, self.v = take(KD, T), take(KD, T), take(NT, D)
        self.u = [env.take_r("diff_u_hi", KD, T, at=env.uT_at), env.take_r("diff_u_lo", KD, T, at=take.at)]
        self.oT = [env.take_r("diff_o_hi", KD, T, at=env.area), env.take_r("diff_o_lo", KD, T, at=env.area + KD * T)]
        self.z = env.big.rearrange("p (k t) -> p k t", k=KD)
        self.p, self.pT = take(6, 512), take(2, 512)
        self.sq = take(D)
        assert take.at <= env.words - HEADS * T, take.at
        self.o = env.uT.rearrange("p k t -> p (k t)").rearrange("p (t d) -> p t d", t=NT)
        small = Area(env, env.small_at)
        self.dots, self.exps, self.lam = small(2), small(2), small(1)
        self.nmax, self.psum, self.scale, self.inv = small(6), small(6), small(6), small(8)
        self.nstat, self.nrstd = small(NT * DIFF_HEADS), small(NT * DIFF_HEADS)
        self.lq, self.lprod = env.lambda_work[:, 0:4 * DH].rearrange("p (a b) -> p a b", a=4), env.lambda_work[:, 4 * DH:5 * DH]


class DiffProject(Stage):

    def __init__(self, env, m):
        super().__init__(env)
        self.m = m
        w = env.io["diff_w_in"][0]
        self.qk = load_features(env, w, 0, 2 * D)
        self.v = load_tokens(env, w, 2 * D, D)
        self.z = load_features(env, w, 3 * D, D)
        self.lq_arrived = env.sem("lq_arrived")
        self.dots_ready, self.exps_ready = env.sem("lambda_dots"), env.sem("lambda_exps")

    def gpsimd(self, pool, step):
        for n, name in enumerate(("q1", "k1", "q2", "k2")):
            pool.dma_start(self.m.lq[:, n, :],
                           self.env.io["diff_lambda_" + name][0].partition_broadcast(P)).then_inc(self.lq_arrived, 16)
        self.env.split_lo(pool, self.z[-1][0] + 2)

    def tensor(self, pe):
        env, u = self.env, self.m.u
        for ld, g in self.qk:
            project_features(env, pe, ld, u, g)
        lds, g = self.v
        project_tokens(env, pe, lds, u, g)
        for ld, g in self.z:
            project_features(env, pe, ld, u, g)

    def scalar(self, act, step):
        env, nc, m = self.env, self.env.nc, self.m
        env.split_hi(act, self.qk[0][0])
        for j, (ld, g) in enumerate(self.qk):
            env.split_hi(act, ld + 1)
            act.wait_ge(env.proj_ready, g + 1)
            nc.scalar.activation((m.qT, m.kT)[j // KD][:, j % KD, :], env.bank(g), ACT.Copy,
                                 scale=DH ** -0.5 if j < KD else 1.0).then_inc(env.proj_taken, 1)
        lds, g = self.v
        env.split_hi(act, lds[-1] + 1)
        for n in range(2 * NT):
            act.wait_ge(env.proj_ready, g + n + 1)
            nc.scalar.activation(m.v[:, n // 2, 512 * (n % 2):512 * (n % 2) + 512], env.ps[:, n, :],
                                 ACT.Copy).then_inc(env.proj_taken, 1)
        for k, (ld, g) in enumerate(self.z):
            env.split_hi(act, ld + 1)
            act.wait_ge(env.proj_ready, g + 1)
            nc.scalar.activation(m.z[:, k, :], env.bank(g), ACT.Silu).then_inc(env.proj_taken, 1)
        env.split_hi(act, self.z[-1][0] + 2)
        act.wait_ge(self.dots_ready, 1)
        nc.scalar.activation(m.exps, m.dots, ACT.Exp).then_inc(self.exps_ready, 1)

    def vector(self, dve, step):
        nc, m = self.env.nc, self.m
        dve.wait_ge(self.lq_arrived, 64)
        step(nc.vector.tensor_tensor_reduce(m.lprod, m.lq[:, 0, :], m.lq[:, 1, :], 1.0, 0.0, ALU.mult, ALU.add,
                                            m.dots[:, 0:1]))
        nc.vector.tensor_tensor_reduce(m.lprod, m.lq[:, 2, :], m.lq[:, 3, :], 1.0, 0.0, ALU.mult, ALU.add,
                                       m.dots[:, 1:2]).then_inc(self.dots_ready, 1)
        dve.wait_ge(self.exps_ready, 1)
        step(nc.vector.tensor_tensor(m.lam, m.exps[:, 1:2], m.exps[:, 0:1], ALU.subtract))
        step(nc.vector.tensor_scalar(m.lam, m.lam, -LAMBDA_INIT, None, ALU.add))
        _, g = self.z[0]
        for k in range(KD):
            dve.wait_ge(self.env.proj_taken, g + k + 1)
            nc.vector.tensor_scalar(m.z[:, k, :], m.z[:, k, :], self.env.vec[:, V_SUBLN + k:V_SUBLN + k + 1], None,
                                    ALU.mult)


class DiffAttend(Attend):

    def __init__(self, env, m):
        super().__init__(env, "diff_")
        self.m = m
        self.a_ready = env.sem("diff_combined")
        self.squared, self.summed = env.sem("diff_squared"), env.sem("diff_summed")
        self.units = [(i, h) for i in reversed(range(NT)) for h in range(DIFF_HEADS)]

    def tensor(self, pe):
        env, nc, m = self.env, self.env.nc, self.m
        n_units = len(self.units)

        def scores(u):
            i, h = self.units[u]
            if u >= 2:
                pe.wait_ge(self.s_biased, 2 * (u - 1))
            for mp in range(2):
                q = slice(64 * mp, 64 * mp + 64)
                nc.tensor.matmul(env.ps[:, 2 * (u % 2) + mp, 0:P * (i + 1)], m.qT[q, h, i * P:(i + 1) * P],
                                 m.kT[q, h, 0:P * (i + 1)], start=True, stop=True).then_inc(self.s_ready, 1)

        def turn(u):
            i = self.units[u][0]
            pe.wait_ge(self.a_ready, u + 1)
            if u >= 2:
                pe.wait_ge(self.pT_copied, u - 1)
            for kt in range(i + 1):
                tr = nc.tensor.transpose(env.ps[:, 4 + u % 2, kt * P:(kt + 1) * P],
                                         m.p[:, 2 * (u % 3), kt * P:(kt + 1) * P], env.ident)
            tr.then_inc(self.pT_ready, 1)

        def values(u):
            i, h = self.units[u]
            b = u // 4
            pe.wait_ge(self.pT_copied, u + 1)
            if u % 4 == 0 and b >= 2:
                pe.wait_ge(self.o_taken, b - 1)
            for kt in range(i + 1):
                mm = nc.tensor.matmul(env.ps[:, 6 + b % 2, (u % 4) * P:(u % 4 + 1) * P],
                                      m.pT[:, u % 2, kt * P:(kt + 1) * P], m.v[:, kt, h * P:(h + 1) * P],
                                      start=(kt == 0), stop=(kt == i))
            mm.then_inc(self.pv_done, 1)

        for u in range(n_units + 3):
            if u < n_units:
                scores(u)
            if 2 <= u <= n_units + 1:
                turn(u - 2)
            if u >= 3:
                values(u - 3)

    def scalar(self, act, step):
        env, nc, m = self.env, self.env.nc, self.m
        n_units = len(self.units)

        def exps(u):
            n = P * (self.units[u][0] + 1)
            for mp in range(2):
                act.wait_ge(self.s_biased, 2 * u + mp + 1)
                at = 2 * (u % 3) + mp
                nc.scalar.activation(m.p[:, at, 0:n], m.p[:, at, 0:n], ACT.Exp, scale=-1.0, bias=m.nmax[:, at:at + 1],
                                     accum_out=m.psum[:, at:at + 1]).then_inc(self.p_ready, 1)

        def copy(u):
            n = P * (self.units[u][0] + 1)
            act.wait_ge(self.pT_ready, u + 1)
            if u >= 2:
                act.wait_ge(self.pv_done, u - 1)
            nc.scalar.activation(m.pT[:, u % 2, 0:n], env.ps[:, 4 + u % 2, 0:n], ACT.Copy).then_inc(self.pT_copied, 1)

        for u in range(n_units + 2):
            if u < n_units:
                exps(u)
            if u >= 2:
                copy(u - 2)

    def vector(self, dve, step):
        env, nc, m = self.env, self.env.nc, self.m
        n_units = len(self.units)

        def bias(u):
            i, h = self.units[u]
            n = P * (i + 1)
            if u >= 3:
                dve.wait_ge(self.pT_ready, u - 2)
            for mp in range(2):
                bank, at = 2 * (u % 2) + mp, 2 * (u % 3) + mp
                dve.wait_ge(self.s_ready, 2 * u + mp + 1)
                nc.vector.tensor_tensor_reduce(m.p[:, at, 0:n], env.ps[:, bank, 0:n], m.bias[:, 2 * h + mp, T - n:T],
                                               -1.0, 1e38, ALU.add, ALU.min,
                                               m.nmax[:, at:at + 1]).then_inc(self.s_biased, 1)

        def combine(u):
            n, at = P * (self.units[u][0] + 1), 2 * (u % 3)
            dve.wait_ge(self.p_ready, 2 * u + 2)
            sums, r = m.psum[:, at:at + 2], m.scale[:, at:at + 2]
            step(nc.vector.reciprocal(r, sums))
            nc.vector.tensor_copy(m.inv[:, u % 8:u % 8 + 1], r[:, 0:1])
            step(nc.vector.scalar_tensor_tensor(r[:, 1:2], r[:, 1:2], m.lam, sums[:, 0:1], ALU.mult, ALU.mult))
            nc.vector.scalar_tensor_tensor(m.p[:, at, 0:n], m.p[:, at + 1, 0:n], r[:, 1:2], m.p[:, at, 0:n],
                                           ALU.mult, ALU.add).then_inc(self.a_ready, 1)

        def take(b):
            dve.wait_ge(self.pv_done, 4 * b + 4)
            nc.vector.tensor_tensor(
                m.o[:, self.units[4 * b][0], 512 * (b % 2):512 * (b % 2) + 512].rearrange("p (u d) -> p u d", d=P),
                env.ps[:, 6 + b % 2, :].rearrange("p (u d) -> p u d", d=P),
                m.inv[:, 4 * (b % 2):4 * (b % 2) + 4].unsqueeze(2).to_broadcast([P, 4, P]),
                ALU.mult).then_inc(self.o_taken, 1)

        def squares(t):
            dve.wait_ge(self.squared, t + 1)
            nc.vector.tensor_reduce(m.nstat[:, 8 * self.units[8 * t][0]:8 * self.units[8 * t][0] + 8],
                                    m.sq.rearrange("p (h d) -> p h d", d=P), AX, ALU.add).then_inc(self.summed, 1)

        for u in range(n_units + 4):
            if u < n_units:
                bias(u)
            if u >= 7 and (u - 3) % 4 == 0:
                take((u - 3) // 4 - 1)
            if u >= 13 and (u - 13) % 8 == 0:
                squares((u - 13) // 8)
            if 1 <= u <= n_units:
                combine(u - 1)

    def gpsimd(self, pool, step):
        m = self.m
        for t in range(NT - 1):
            pool.wait_ge(self.o_taken, 2 * t + 2)
            if t:
                pool.wait_ge(self.summed, t)
            o = m.o[:, self.units[8 * t][0], :]
            self.env.nc.gpsimd.tensor_tensor(m.sq, o, o, ALU.mult).then_inc(self.squared, 1)


class DiffNorm(Stage):

    def __init__(self, env, m):
        super().__init__(env)
        self.m = m
        self.ms_ready, self.rstd_ready = env.sem("subln_ms"), env.sem("subln_rstd")

    def scalar(self, act, step):
        nc, m = self.env.nc, self.m
        act.wait_ge(self.ms_ready, 1)
        nc.scalar.activation(m.nrstd, m.nstat, ACT.Sqrt).then_inc(self.rstd_ready, 1)

    def vector(self, dve, step):
        env, nc, m = self.env, self.env.nc, self.m
        c2 = (1.0 - LAMBDA_INIT) ** 2
        step(nc.vector.tensor_tensor(m.sq, m.o[:, 0, :], m.o[:, 0, :], ALU.mult))
        step(nc.vector.tensor_reduce(m.nstat[:, 0:8], m.sq.rearrange("p (h d) -> p h d", d=P), AX, ALU.add))
        step(nc.vector.tensor_scalar(m.nstat, m.nstat, 1.0 / (P * c2), EPS / c2, ALU.mult, ALU.add))
        nc.vector.reciprocal(m.nstat, m.nstat).then_inc(self.ms_ready, 1)
        dve.wait_ge(self.rstd_ready, 1)
        for i in range(NT):
            o = m.o[:, i, :].rearrange("p (h d) -> p h d", d=P)
            nc.vector.tensor_tensor(o, o, m.nrstd[:, 8 * i:8 * i + 8].unsqueeze(2).to_broadcast([P, DIFF_HEADS, P]),
                                    ALU.mult)


class FfnUp(Stage):

    def __init__(self, env, layer, m):
        super().__init__(env)
        self.layer, self.m = layer, m
        w = env.io["w_up_2"][layer]
        self.lds = []
        self.g0 = env.groups
        for j in range(FT):
            for half in range(2):
                self.lds += [ld for ld, _ in load_features(env, w, half * D_FF + j * P, P)]
        n = str(layer)
        self.scaled = env.sem("up_scaled" + n)
        self.gelu_done, self.product_ready = env.sem("gelu_done" + n), env.sem("product_ready" + n)
        self.act_hi_ready, self.act_done = env.sem("act_hi_ready" + n), env.sem("act_done" + n)

    def tensor(self, pe):
        env, nc = self.env, self.env.nc
        for n, ld in enumerate(self.lds):
            project_features(env, pe, ld, self.m.u, self.g0 + n)

    def col(self, which, half, j):
        at = V_CONV + 176 * self.layer + 44 * which + FT * half + j
        return self.env.vec[:, at:at + 1]

    def gpsimd(self, pool, step):
        self.env.split_lo(pool, self.lds[-1] + 2)

    def scalar(self, act, step):
        env, nc, m = self.env, self.env.nc, self.m

        def gelu(j):
            act.wait_ge(env.proj_taken, self.g0 + 2 * j + 2)
            if j >= 2:
                act.wait_ge(self.act_done, j - 1)
            nc.scalar.activation(m.gelu[:, j % 2, :], m.conv[:, 2 * (j % 2), :], ACT.Gelu_apprx_tanh).then_inc(self.gelu_done, 1)

        def act_hi(j):
            act.wait_ge(self.product_ready, j + 1)
            nc.scalar.activation(m.act[0][:, j, :], m.gelu[:, j % 2, :], ACT.Copy).then_inc(self.act_hi_ready, 1)

        env.split_hi(act, self.lds[0])
        for j in range(FT):
            for half in range(2):
                n = 2 * j + half
                env.split_hi(act, self.lds[n] + 1)
                g = self.g0 + n
                act.wait_ge(env.proj_ready, g + 1)
                if j >= 2:
                    act.wait_ge(self.product_ready, j - 1)
                nc.scalar.activation(m.conv[:, 2 * (j % 2) + half, :], env.bank(g), ACT.Identity,
                                     scale=self.col(2, half, j), bias=self.col(3, half, j)).then_inc(self.scaled, 1)
            if j:
                gelu(j - 1)
            if j >= 2:
                act_hi(j - 2)
        gelu(FT - 1)
        act_hi(FT - 2)
        env.split_hi(act, self.lds[-1] + 2)
        act_hi(FT - 1)

    def vector(self, dve, step):
        env, nc, m = self.env, self.env.nc, self.m

        def multiply(j):
            dve.wait_ge(self.gelu_done, j + 1)
            dve.wait_ge(env.proj_taken, self.g0 + 2 * j + 2)
            nc.vector.tensor_tensor(m.gelu[:, j % 2, :], m.gelu[:, j % 2, :], m.conv[:, 2 * (j % 2) + 1, :],
                                    ALU.mult).then_inc(self.product_ready, 1)

        def act_lo(j):
            dve.wait_ge(self.act_hi_ready, j + 1)
            nc.vector.tensor_tensor(m.act[1][:, j, :], m.gelu[:, j % 2, :], m.act[0][:, j, :].bitcast(F32),
                                    ALU.subtract).then_inc(self.act_done, 1)

        for j in range(FT):
            for half in range(2):
                g = self.g0 + 2 * j + half
                c = m.conv[:, 2 * (j % 2) + half, :]
                dve.wait_ge(self.scaled, 2 * j + half + 1)
                step(nc.vector.scalar_tensor_tensor(c[:, 1:T], env.bank(g)[:, 0:T - 1], self.col(1, half, j), c[:, 1:T],
                                                    ALU.mult, ALU.add))
                nc.vector.scalar_tensor_tensor(c[:, 2:T], env.bank(g)[:, 0:T - 2], self.col(0, half, j), c[:, 2:T],
                                               ALU.mult, ALU.add).then_inc(env.proj_taken, 1)
            if j:
                multiply(j - 1)
            if j >= 2:
                act_lo(j - 2)
        multiply(FT - 1)
        act_lo(FT - 2)
        act_lo(FT - 1)


class FfnMemory:

    def __init__(self, env):
        at = env.area
        self.act = [env.take_r("act_hi", FT, T, at=at), env.take_r("act_lo", FT, T, at=at + FT * T)]
        self.u = [env.take_r("u_hi", KD, T, at=env.uT_at), env.take_r("u_lo", KD, T, at=at + 2 * FT * T)]
        assert at + 2 * FT * T + KD * T <= env.words
        take = Area(env, env.big_at)
        self.conv, self.gelu = take(4, 512), take(2, 512)


class SwaMemory:
    def __init__(self, env):
        take = Area(env)
        lo_at = env.area + 2 * FT * T
        self.u = [env.take_r("swa_u_hi", KD, T, at=env.uT_at), env.take_r("swa_u_lo", KD, T, at=lo_at)]
        self.kT, self.v = take(GROUPS, T), take(NT, 256)
        self.q = [take(KD, T), take(KD, T)]
        self.s, self.p, self.pT = take(3, 256), take(3, 256), take(3, 256)
        self.sinks, self.nsinks = take(HEADS), take(HEADS)
        self.nmax, self.psum, self.esink, self.scale = take(16), take(16), take(16), take(16)
        self.o = env.big.rearrange("p (t d) -> p t d", t=NT)


class KvProject(Stage):

    def __init__(self, env, m, g_row):
        super().__init__(env)
        self.again = Renorm(env, g_row, m.u)
        env.repeats += 1
        self.m = m
        width = GROUPS * DH
        self.keys = load_features(env, env.io["w_kv_2"], 0, width)
        self.values = load_tokens(env, env.io["w_kv_2"], width, width)

    def tensor(self, pe):
        env = self.env
        for ld, g in self.keys:
            project_features(env, pe, ld, self.m.u, g)
        project_tokens(env, pe, self.values[0], self.m.u, self.values[1], elsewhere=len(self.keys))

    def gpsimd(self, pool, step):
        self.again.fetch(pool)
        self.env.split_lo(pool, self.values[0][-1] + 2)

    def vector(self, dve, step):
        for i in range(NT):
            self.again.scale(dve, step, i, again=True)

    def scalar(self, act, step):
        env, nc, m = self.env, self.env.nc, self.m
        env.split_hi(act, self.keys[0][0])
        for j, (ld, g) in enumerate(self.keys):
            env.split_hi(act, ld + 1)
            act.wait_ge(env.proj_ready, g + 1)
            for half in range(2):
                for to in range(2):
                    cp = nc.scalar.activation(m.kT[64 * to:64 * to + 64, 2 * j + half, :],
                                              env.bank(g)[64 * half:64 * half + 64, :], ACT.Copy)
            cp.then_inc(env.proj_taken, 1)
        lds, g = self.values
        env.split_hi(act, lds[-1] + 1)
        for i in range(NT):
            act.wait_ge(env.proj_ready, g + i + 1)
            nc.scalar.activation(m.v[:, i, :], env.ps[:, 4 + i, 0:256], ACT.Copy).then_inc(env.proj_taken, 1)
        env.split_hi(act, lds[-1] + 2)


class SwaProject(Stage):
    def __init__(self, env, m):
        super().__init__(env)
        self.m = m
        self.q = load_features(env, env.io["w_q_2"][0], 0, D)
        self.sinks_arrived = env.sem("sinks_arrived")

    def gpsimd(self, pool, step):
        pool.dma_start(self.m.sinks, self.env.io["sinks_2"][0].partition_broadcast(P)).then_inc(self.sinks_arrived, 16)
        self.env.split_lo(pool, self.q[-1][0] + 2)

    def tensor(self, pe):
        for ld, g in self.q:
            project_features(self.env, pe, ld, self.m.u, g)

    def scalar(self, act, step):
        env, nc = self.env, self.env.nc
        env.split_hi(act, self.q[0][0])
        for j, (ld, g) in enumerate(self.q):
            env.split_hi(act, ld + 1)
            act.wait_ge(env.proj_ready, g + 1)
            for odd in range(2):
                rows = slice(64 * odd, 64 * odd + 64)
                cp = nc.scalar.activation(self.m.q[odd][rows, j, :], env.bank(g)[rows], ACT.Copy, scale=DH ** -0.5)
            cp.then_inc(env.proj_taken, 1)
        env.split_hi(act, self.q[-1][0] + 2)

    def vector(self, dve, step):
        self.env.nc.vector.memset(self.m.q[0][64:128], 0.0)
        self.env.nc.vector.memset(self.m.q[1][0:64], 0.0)
        dve.wait_ge(self.sinks_arrived, 16)
        step(self.env.nc.vector.tensor_scalar(self.m.nsinks, self.m.sinks, -1.0, None, ALU.mult))


class SwaAttend(Attend):

    def __init__(self, env, m):
        super().__init__(env, "swa_")
        self.m = m
        self.esum_ready, self.esink_ready = env.sem("sink_shifted"), env.sem("sink_exp")
        self.units = [(i, h) for i in reversed(range(NT)) for h in range(HEADS)]

    def tensor(self, pe):
        env, nc, m = self.env, self.env.nc, self.m
        n_units = len(self.units)

        def scores(u):
            i, h = self.units[u]
            lo = max(i - 1, 0)
            if u >= 3:
                pe.wait_ge(self.s_biased, u - 2)
            nc.tensor.matmul(env.ps[:, u % 3, 0:P * (i + 1 - lo)], m.q[h % 2][:, h // 2, i * P:(i + 1) * P],
                             m.kT[:, h // HPG, P * lo:P * (i + 1)],
                             start=True, stop=True).then_inc(self.s_ready, 1)

        def turn(u):
            i = self.units[u][0]
            pe.wait_ge(self.p_ready, u + 1)
            if u >= 3:
                pe.wait_ge(self.pT_copied, u - 2)
            for kt in range(1 + (i > 0)):
                tr = nc.tensor.transpose(env.ps[:, 3 + u % 3, kt * P:(kt + 1) * P], m.p[:, u % 3, kt * P:(kt + 1) * P],
                                         env.ident)
            tr.then_inc(self.pT_ready, 1)

        def values(u):
            i, h = self.units[u]
            b, g, lo = u // 8, h // HPG, max(i - 1, 0)
            pe.wait_ge(self.pT_copied, u + 1)
            if u % 8 == 0 and b >= 2:
                pe.wait_ge(self.o_taken, b - 1)
            for kt in range(lo, i + 1):
                mm = nc.tensor.matmul(env.ps[:, 6 + b % 2, (u % 8) * DH:(u % 8 + 1) * DH],
                                      m.pT[:, u % 3, (kt - lo) * P:(kt - lo + 1) * P], m.v[:, kt, g * DH:(g + 1) * DH],
                                      start=(kt == lo), stop=(kt == i))
            mm.then_inc(self.pv_done, 1)

        for u in range(n_units + 3):
            if u < n_units:
                scores(u)
            if 2 <= u <= n_units + 1:
                turn(u - 2)
            if u >= 3:
                values(u - 3)

    def scalar(self, act, step):
        env, nc, m = self.env, self.env.nc, self.m
        n_units = len(self.units)

        def exp(u):
            n, b = P * (1 + (self.units[u][0] > 0)), u // 8
            act.wait_ge(self.s_biased, u + 1)
            if u >= 3:
                act.wait_ge(self.pT_ready, u - 2)
            if u % 8 == 0 and b >= 2:
                act.wait_ge(self.o_taken, b - 1)
            nc.scalar.activation(m.p[:, u % 3, 0:n], m.s[:, u % 3, 0:n], ACT.Exp, scale=-1.0,
                                 bias=m.nmax[:, u % 16:u % 16 + 1],
                                 accum_out=m.psum[:, u % 16:u % 16 + 1]).then_inc(self.p_ready, 1)

        for u in range(n_units + 5):
            if u < n_units:
                exp(u)
            if u >= 12 and (u - 4) % 8 == 0:
                b = (u - 4) // 8 - 1
                at = 8 * (b % 2)
                act.wait_ge(self.esum_ready, b + 1)
                nc.scalar.activation(m.esink[:, at:at + 8], m.esink[:, at:at + 8], ACT.Exp).then_inc(self.esink_ready, 1)

    def vector(self, dve, step):
        env, nc, m = self.env, self.env.nc, self.m
        n_units = len(self.units)
        band = env.const[:, C_BAND:C_BAND + 2 * P]

        def bias(u):
            i, h = self.units[u]
            n = P * (1 + (i > 0))
            dve.wait_ge(self.s_ready, u + 1)
            if u >= 3:
                dve.wait_ge(self.p_ready, u - 2)
            nc.vector.tensor_tensor_reduce(m.s[:, u % 3, 0:n], env.ps[:, u % 3, 0:n], band[:, 2 * P - n:2 * P],
                                           -1.0, m.nsinks[:, h:h + 1], ALU.add, ALU.min,
                                           m.nmax[:, u % 16:u % 16 + 1]).then_inc(self.s_biased, 1)

        def copy(u):
            n = P * (1 + (self.units[u][0] > 0))
            dve.wait_ge(self.pT_ready, u + 1)
            if u >= 3:
                dve.wait_ge(self.pv_done, u - 2)
            nc.vector.tensor_copy(m.pT[:, u % 3, 0:n], env.ps[:, 3 + u % 3, 0:n]).then_inc(self.pT_copied, 1)

        def combine(b):
            at, h0 = 8 * (b % 2), 8 * (b % 2)
            dve.wait_ge(self.s_biased, 8 * b + 8)
            nc.vector.tensor_tensor(m.esink[:, at:at + 8], m.nmax[:, at:at + 8], m.sinks[:, h0:h0 + 8],
                                    ALU.add).then_inc(self.esum_ready, 1)
            dve.wait_ge(self.esink_ready, b + 1)
            step(nc.vector.tensor_tensor(m.scale[:, at:at + 8], m.psum[:, at:at + 8], m.esink[:, at:at + 8], ALU.add))
            step(nc.vector.reciprocal(m.scale[:, at:at + 8], m.scale[:, at:at + 8]))
            dve.wait_ge(self.pv_done, 8 * b + 8)
            nc.vector.tensor_tensor(m.o[:, self.units[8 * b][0], 512 * (b % 2):512 * (b % 2) + 512].rearrange("p (u d) -> p u d", d=DH),
                                    env.ps[:, 6 + b % 2, :].rearrange("p (u d) -> p u d", d=DH),
                                    m.scale[:, at:at + 8].unsqueeze(2).to_broadcast([P, 8, DH]),
                                    ALU.mult).then_inc(self.o_taken, 1)

        for u in range(n_units + 5):
            if u < n_units:
                bias(u)
            if 2 <= u <= n_units + 1:
                copy(u - 2)
            if u >= 12 and (u - 4) % 8 == 0:
                combine((u - 4) // 8 - 1)


class RwkvMemory:

    def __init__(self, env):
        take = Area(env)
        self.r, self.k, self.a, self.kk = take(KD, T), take(KD, T), take(KD, T), take(KD, T)
        self.v = take(NT, D)
        l_at = take.at
        self.decay = take(KD, T)
        self.xx = self.decay
        hid = Area(env, l_at + KD * T)
        self.tanh_w, self.hid_a = hid(T), hid(T)
        a_at = env.area + 2 * KD * T
        self.mixes = [[env.take_r("mix0_hi", KD, T, at=env.big_at), env.take_r("mix0_lo", KD, T, at=a_at + 2 * KD * T)],
                      [env.take_r("mix1_hi", KD, T, at=a_at), env.take_r("mix1_lo", KD, T, at=a_at + KD * T)]]
        self.oT = [env.take_r("rwkv_o_hi", KD, T, at=env.uT_at), env.take_r("rwkv_o_lo", KD, T, at=a_at)]
        core1 = Area(env, l_at)
        u_at = 4096
        core0 = Area(env, u_at)
        self.streams = []
        for take in (core0, core1):
            st = {}
            for name in ("abT", "X", "XT", "Y", "akT", "rbT", "rkT"):
                st[name] = take(4, P)
            st["MT"] = [take(4, P), take(4, P)]
            st["Z"], st["SA"] = take(4, DH), take(4, DH)
            self.streams.append(st)
        self.tok = core0(3, 4, P)
        self.WT = core0(4, P)
        self.S = core0(KD, DH)
        assert core0.at <= u_at + 8192, core0.at
        take = Area(env, core1.at)
        self.sg = take(2, T)
        take = Area(env, env.stat_at + 64)
        self.coef = take(KD, NT)
        self.bonus = take(NT, RH)
        self.mid, self.epos = take(KD, NT), take(KD, NT)
        self.keep = take(KD)
        w = Area(env, u_at)
        self.w = [[w(T) for _ in range(7)] for _ in range(2)]
        self.gn = self.r.rearrange("p k t -> p (k t)")[:, 0:2 * D].rearrange("p (a d) -> p a d", a=2)
        self.added = self.k.rearrange("p k t -> p (k t)").rearrange("p (t d) -> p t d", t=NT)
        self.squares = self.a.rearrange("p k t -> p (k t)")[:, 0:2 * D].rearrange("p (a d) -> p a d", a=2)
        self.gate = self.decay
        self.head_rows = env.next_g
        small = Area(env, env.small_at)
        self.mean, self.var, self.grstd = small(2, RH), small(2, RH), small(2, RH)
        self.o = env.big.rearrange("p (t d) -> p t d", t=NT)


class RwkvProject(Stage):

    MIXES = [1, 2, 4, 0, 5, 3]

    def __init__(self, env, m):
        super().__init__(env)
        self.m = m
        io = env.io
        w = io["w_rkv_2"][0]
        self.w1 = load_features(env, io["w_decay1_2"][0], 0, 64, 64)[0]
        self.k = load_features(env, w[1], 0, D)
        self.a1 = load_features(env, io["a1_2"][0], 0, 64, 64)[0]
        self.r = load_features(env, w[0], 0, D)
        self.g1 = load_features(env, io["g1_2"][0], 0, P) + load_features(env, io["g1_2"][0], P, 32, 32)
        self.v = load_tokens(env, w[2], 0, D)
        self.second = []
        for name in ("w_decay2_2", "a2_2"):
            ld, g = env.load(io[name][0].unsqueeze(1), split=False), env.group(KD)
            env.release(ld, env.proj_ready, env.groups)
            self.second.append((ld, g))
        self.last = [self.w1[1], self.k[-1][1], self.a1[1], self.r[-1][1]]
        self.mixed, self.mix_hi_ready, self.mix_ready = env.sem("mixed"), env.sem("mix_hi_ready"), env.sem("mix_ready")

    def vector(self, dve, step):
        env, nc, m = self.env, self.env.nc, self.m
        step(nc.vector.tensor_scalar(m.xx[:, :, 0:1], env.uT[:, :, 0:1], -1.0, None, ALU.mult))

        def low(n, k):
            dve.wait_ge(self.mix_hi_ready, KD * n + k + 1)
            nc.vector.tensor_tensor(m.mixes[n % 2][1][:, k, :], env.pair_tmp[:, k % 2, :],
                                    m.mixes[n % 2][0][:, k, :].bitcast(F32), ALU.subtract).then_inc(self.mix_ready, 1)

        for n, i in enumerate(self.MIXES):
            for k in range(KD):
                at = V_MU + 8 * i + k
                if n == 0:
                    step(nc.vector.tensor_tensor(m.xx[:, k, 1:T], env.uT[:, k, 0:T - 1], env.uT[:, k, 1:T],
                                                 ALU.subtract))
                if KD * n + k >= 2:
                    dve.wait_ge(self.mix_ready, KD * n + k - 1)
                nc.vector.scalar_tensor_tensor(env.pair_tmp[:, k % 2, :], m.xx[:, k, :], env.vec[:, at:at + 1],
                                               env.uT[:, k, :], ALU.mult, ALU.add).then_inc(self.mixed, 1)
                if k:
                    low(n, k - 1)
            low(n, KD - 1)

    def gpsimd(self, pool, step):
        self.env.split_lo(pool, self.v[0][-1] + 4)

    def tensor(self, pe):
        env, nc, m = self.env, self.env.nc, self.m
        for n, lds in enumerate(([self.w1], self.k, [self.a1], self.r, self.g1)):
            for ld, g in lds:
                project_features(env, pe, ld, m.mixes[n % 2], g, env.loads[ld][2],
                                 (lambda k: pe.wait_ge(self.mix_ready, KD * n + k + 1)) if ld == lds[0][0] else None)
        pe.wait_ge(self.mix_ready, KD * 6)
        project_tokens(env, pe, self.v[0], m.mixes[1], self.v[1])
        pe.wait_ge(env.proj_taken, self.a1[1] + 1)
        for (ld, g), hid in zip(self.second, (m.tanh_w, m.hid_a)):
            env.wait_whole(pe, ld)
            for k in range(KD):
                env.wait_bank(pe, g + k)
                nc.tensor.matmul(env.bank(g + k), env.whole(ld)[0:64, 0, k * P:(k + 1) * P], hid[0:64, :],
                                 start=True, stop=True).then_inc(env.proj_ready, 1)

    def scalar(self, act, step):
        env, nc, m = self.env, self.env.nc, self.m

        def high(n, k):
            if n >= 2 and k == 0:
                act.wait_ge(env.proj_ready, self.last[n - 2] + 1)
            act.wait_ge(self.mixed, KD * n + k + 1)
            nc.scalar.activation(m.mixes[n % 2][0][:, k, :], env.pair_tmp[:, k % 2, :],
                                 ACT.Copy).then_inc(self.mix_hi_ready, 1)

        def take(entry, dst, func, rows=P):
            ld, g = entry
            env.split_hi(act, ld + 1)
            act.wait_ge(env.proj_ready, g + 1)
            nc.scalar.activation(dst, env.bank(g)[0:rows, :], func).then_inc(env.proj_taken, 1)

        env.split_hi(act, self.w1[0])
        for k in range(KD):
            high(0, k)
        env.split_hi(act, self.k[0][0])
        for k in range(KD):
            high(1, k)
        take(self.w1, m.tanh_w[0:64, :], ACT.Tanh, 64)
        for j, entry in enumerate(self.k):
            high(2, j)
            take(entry, m.k[:, j, :], ACT.Copy)
        for k in range(KD):
            high(3, k)
        take(self.a1, m.hid_a[0:64, :], ACT.Copy, 64)
        for j, entry in enumerate(self.r):
            high(4, j)
            take(entry, m.r[:, j, :], ACT.Copy)
        env.split_hi(act, self.g1[1][0])
        for k in range(KD):
            high(5, k)
        take(self.g1[0], m.sg[:, 0, :], ACT.Sigmoid)
        take(self.g1[1], m.sg[0:32, 1, :], ACT.Sigmoid, 32)
        lds, g = self.v
        env.split_hi(act, lds[-1])
        for n in range(2 * NT):
            act.wait_ge(env.proj_ready, g + n + 1)
            nc.scalar.activation(m.v[:, n // 2, 512 * (n % 2):512 * (n % 2) + 512], env.ps[:, n, :],
                                 ACT.Copy).then_inc(env.proj_taken, 1)
        act.wait_ge(self.mix_ready, KD * 6)
        for (ld, g), dst, col in zip(self.second, (m.decay, m.a), (V_B, V_B + 8)):
            for k in range(KD):
                act.wait_ge(env.proj_ready, g + k + 1)
                nc.scalar.activation(dst[:, k, :], env.bank(g + k), ACT.Sigmoid,
                                     bias=env.vec[:, col + k:col + k + 1]).then_inc(env.proj_taken, 1)


class RwkvPrepare(Stage):

    def __init__(self, env, m):
        super().__init__(env)
        self.m = m
        s = env.sem
        self.sq_ready, self.ss_ready, self.inv_ready = s("kk_sq_ready"), s("kk_ss_ready"), s("kk_inv_ready")
        self.norm_ready, self.mid_ready = s("kk_norm_ready"), s("mid_ready")
        self.rk_ready, self.tile_done = s("rk_ready"), s("prep_tile_done")
        self.bonus_ready = s("bonus_ready")
        self.rows_arrived, self.spread = s("head_rows_arrived"), s("norm_spread")
        self.mix_ready, self.kk_ready, self.scanned = s("k_mix_ready"), s("kk_ready"), s("scanned")

    def tensor(self, pe):
        env, nc, m = self.env, self.env.nc, self.m
        for k in range(KD):
            w = m.w[k % 2]
            pe.wait_ge(self.sq_ready, k + 1)
            at = C_HEADROW + 2 * (KD - 1) - 2 * k
            nc.tensor.matmul(env.ps[0:RH, 0, :], env.const[:, at:at + RH], w[0],
                             start=(k == 0), stop=(k == KD - 1)).then_inc(self.ss_ready, 1)
            pe.wait_ge(self.rk_ready, k + 1)
            for i in range(NT):
                mm = nc.tensor.matmul(env.ps[:, 7, i * RH + 2 * k:i * RH + 2 * k + 2], w[1][:, i * P:(i + 1) * P],
                                      env.const[:, C_HEADSEL:C_HEADSEL + 2], start=True, stop=True)
            mm.then_inc(self.bonus_ready, 1)
        pe.wait_ge(self.rows_arrived, 16)
        pe.wait_ge(self.norm_ready, 1)
        for k in range(KD):
            if k >= 4:
                pe.wait_ge(self.kk_ready, k - 3)
            nc.tensor.matmul(env.ps[:, 1 + k % 4, :], m.head_rows[0:RH, k * P:(k + 1) * P], m.w[0][2][0:RH],
                             start=True, stop=True).then_inc(self.spread, 1)

    def scalar(self, act, step):
        env, nc, m = self.env, self.env.nc, self.m
        step(nc.scalar.activation(m.keep, env.vec[:, V_B + 24:V_B + 32], ACT.Copy, scale=-1.0, bias=1.0))

        def first(k):
            w = m.w[k % 2]
            col = lambda n: env.vec[:, V_B + 8 * n + k:V_B + 8 * n + k + 1]
            if k >= 2:
                act.wait_ge(self.rk_ready, k - 1)
                act.wait_ge(self.ss_ready, k - 1)
            nc.scalar.activation(m.kk[:, k, :], m.k[:, k, :], ACT.Copy, scale=col(2))
            nc.scalar.activation(w[0], m.k[:, k, :], ACT.Square, scale=col(2)).then_inc(self.sq_ready, 1)
            nc.scalar.activation(w[5], m.a[:, k, :], ACT.Identity, scale=col(3),
                                 bias=m.keep[:, k:k + 1]).then_inc(self.mix_ready, 1)

        for k in range(KD):
            first(k)
        act.wait_ge(self.inv_ready, 1)
        nc.scalar.activation(m.w[0][2][0:RH], m.w[0][3][0:RH], ACT.Sqrt).then_inc(self.norm_ready, 1)

    def vector(self, dve, step):
        env, nc, m = self.env, self.env.nc, self.m
        v = nc.vector
        ones = env.const[:, C_ONES:C_ONES + P]

        for k in range(KD):
            w = m.w[k % 2]
            kp, r = m.k[:, k, :], m.r[:, k, :]
            dve.wait_ge(self.mix_ready, k + 1)
            step(v.tensor_tensor(kp, w[5], kp, ALU.mult))
            if k >= 2:
                dve.wait_ge(self.bonus_ready, k - 1)
            v.scalar_tensor_tensor(w[1], r, env.vec[:, V_B + 32 + k:V_B + 33 + k], kp, ALU.mult,
                                   ALU.mult).then_inc(self.rk_ready, 1)
            if k >= 2:
                dve.wait_ge(self.tile_done, k - 1)
            for c in range(NT):
                v.tensor_tensor_scan(w[6][:, c * P:(c + 1) * P], ones, m.decay[:, k, c * P:(c + 1) * P], 0.0,
                                     ALU.mult, ALU.add).then_inc(self.scanned, 1)
            dve.wait_ge(self.scanned, NT * (k + 1))
            v.tensor_copy(m.mid[:, k, :], w[6][:, P // 2 - 1:T:P]).then_inc(self.mid_ready, 1)
        dve.wait_ge(self.ss_ready, KD)
        step(v.tensor_scalar(m.w[0][3][0:RH], env.ps[0:RH, 0, :], 1e-24, None, ALU.max))
        v.reciprocal(m.w[0][3][0:RH], m.w[0][3][0:RH]).then_inc(self.inv_ready, 1)
        dve.wait_ge(self.bonus_ready, KD)
        step(v.tensor_copy(m.bonus.rearrange("p a b -> p (a b)"), env.ps[:, 7, 0:NT * RH]))
        for k in range(KD):
            dve.wait_ge(self.spread, k + 1)
            v.tensor_tensor(m.kk[:, k, :], m.kk[:, k, :], env.ps[:, 1 + k % 4, :], ALU.mult).then_inc(self.kk_ready, 1)

    def gpsimd(self, pool, step):
        env, nc, m = self.env, self.env.nc, self.m
        chunks = lambda x: x.rearrange("p (c t) -> p c t", c=NT)

        def product(k):
            pool.wait_ge(self.kk_ready, k + 1)
            nc.gpsimd.tensor_tensor(m.a[:, k, :], m.a[:, k, :], m.kk[:, k, :], ALU.mult)

        pool.dma_start(m.head_rows[0:RH], env.io["head_rows"]).then_inc(self.rows_arrived, 16)
        for k in range(KD):
            pool.wait_ge(self.mid_ready, k + 1)
            nc.gpsimd.tensor_tensor(chunks(m.decay[:, k, :]), chunks(m.w[k % 2][6]),
                                    m.mid[:, k, :].unsqueeze(2).to_broadcast([P, NT, P]),
                                    ALU.subtract).then_inc(self.tile_done, 1)
        for k in range(KD):
            product(k)


class RwkvDecay(Stage):

    def __init__(self, env, m):
        super().__init__(env)
        self.m = m
        self.exps_ready, self.taken = env.sem("decay_exps_ready"), env.sem("decay_exps_taken")
        self.cols_ready, self.k_scaled = env.sem("decay_cols_ready"), env.sem("k_scaled")

    def tensor(self, pe):
        pe.wait_ge(self.taken, KD - 3)
        self.env.warm_up()

    def gpsimd(self, pool, step):
        m, g = self.m, self.env.nc.gpsimd
        for k in range(KD):
            pool.wait_ge(self.exps_ready, k + 1)
            if k % 2:
                g.tensor_tensor(m.a[:, k, :], m.a[:, k, :], m.w[k % 2][1], ALU.mult)
            g.tensor_tensor(m.k[:, k, :], m.k[:, k, :], m.w[k % 2][1], ALU.mult).then_inc(self.k_scaled, 1)

    def scalar(self, act, step):
        env, nc, m = self.env, self.env.nc, self.m
        c = DECAY_SCALE
        step(nc.scalar.activation(m.coef, m.mid, ACT.Exp, scale=-c))
        nc.scalar.activation(m.epos, m.mid, ACT.Exp, scale=c).then_inc(self.cols_ready, 1)
        for k in range(KD):
            w = m.w[k % 2]
            if k >= 2:
                act.wait_ge(self.taken, k - 1)
                act.wait_ge(self.k_scaled, k - 1)
            nc.scalar.activation(w[0], m.decay[:, k, :], ACT.Exp, scale=-c)
            nc.scalar.activation(w[1], m.decay[:, k, :], ACT.Exp, scale=c).then_inc(self.exps_ready, 1)

    def vector(self, dve, step):
        env, nc, m = self.env, self.env.nc, self.m
        v = nc.vector
        chunks = lambda x: x.rearrange("p (c t) -> p c t", c=NT)
        dve.wait_ge(self.cols_ready, 1)
        for k in range(KD):
            w = m.w[k % 2]
            kk = chunks(m.kk[:, k, :])
            e = chunks(w[0])
            dve.wait_ge(self.exps_ready, k + 1)
            v.tensor_tensor(m.r[:, k, :], m.r[:, k, :], w[0], ALU.mult)
            if k % 2 == 0:
                v.tensor_tensor(m.a[:, k, :], m.a[:, k, :], w[1], ALU.mult)
            v.scalar_tensor_tensor(kk[:, :, 1:P], kk[:, :, 1:P], -1.0, e[:, :, 0:P - 1], ALU.mult, ALU.mult)
            v.scalar_tensor_tensor(kk[:, :, 0], kk[:, :, 0], -1.0, m.epos[:, k, :], ALU.mult, ALU.mult)
            v.tensor_tensor(m.coef[:, k, 1:NT], m.coef[:, k, 1:NT], e[:, 0:NT - 1, P - 1],
                            ALU.mult).then_inc(self.taken, 1)


class RwkvCore(Stage):

    STEPS = [(c, q) for c in range(NT) for q in range(2)]

    def __init__(self, env, m):
        super().__init__(env)
        self.m = m
        s = env.sem
        self.ready = {"A": s("core_act_ready"), "D": s("core_dve_ready")}
        self.taken = {"A": s("core_act_taken"), "D": s("core_dve_taken")}
        self.part_ready = s("level_part_ready")
        self.start_ready = s("start_ready")
        self.start_T_ready = s("start_T_ready")
        self.order = [(0, name, st) for st in range(2) for name in ("abT", "ab", "akT")] + self.late(0)
        last = len(self.STEPS) - 1
        for w in range(last + 1):
            for lv in range(1, LEVELS):
                self.order += [(w, "Y", lv, st) for st in range(2)]
                for st in range(2):
                    self.order += [(w, name, lv, st) for name in (("X", "XT") if lv < LEVELS - 1 else ("XT",))]
            fill = [] if w == last else [[(w + 1, "abT", 0), (w + 1, "ab", 0)], [(w + 1, "akT", 0), (w + 1, "abT", 1)],
                                         [(w + 1, "ab", 1), (w + 1, "akT", 1)], self.late(w + 1)]
            for name in ("WT", "SA", "y", "S"):
                self.order += [(w, name, st) for st in range(2)]
                if fill:
                    self.order += fill.pop(0)
        self.num, count = {}, {"A": 0, "D": 0}
        for key in self.order:
            engine = "A" if key[1] in ("tok", "Z", "Y", "WT", "SA", "y") else "D"
            self.num[key] = (engine, count[engine])
            count[engine] += 1

    @staticmethod
    def late(w):
        return ([(w, "tok", arr) for arr in range(3)] + [(w, name, st) for st in range(2) for name in ("rbT", "rkT")]
                + [(w, "Z", st) for st in range(2)])

    def bank(self, key):
        engine, n = self.num[key]
        return self.env.ps[:, n % 4 + (4 if engine == "D" else 0), :]

    def wait_ready(self, eng, *key):
        engine, n = self.num[key]
        eng.wait_ge(self.ready[engine], n + 1)

    def wait_taken(self, eng, *key):
        engine, n = self.num[key]
        eng.wait_ge(self.taken[engine], n + 1)

    def tensor(self, pe):
        env, nc, m = self.env, self.env.nc, self.m
        mmul = nc.tensor.matmul
        operands = {"abT": (m.a, m.kk), "ab": (m.kk, m.a), "akT": (m.k, m.kk), "rbT": (m.a, m.r), "rkT": (m.k, m.r)}
        for key in self.order:
            w, name, st = key[0], key[1], key[-1]
            c, q = self.STEPS[w]
            tok, half = slice(c * P, (c + 1) * P), slice(64 * st, 64 * st + 64)
            s = m.streams[st] if name != "tok" else None
            lv = key[2]
            if name == "Z":
                self.wait_taken(pe, w, "akT", st)
            elif name == "Y":
                pe.wait_ge(self.part_ready, 12 * w + 2 * (lv - 1) + st + 1)
                if lv == 1:
                    pe.wait_ge(self.start_ready, 2 * w + st + 1)
                else:
                    self.wait_taken(pe, w, "X", lv - 1, st)
            elif name == "X" or (name == "XT" and lv == LEVELS - 1):
                self.wait_taken(pe, w, "Y", lv, st)
                if lv == 1:
                    pe.wait_ge(self.start_T_ready, 2 * w + st + 1)
                else:
                    self.wait_taken(pe, w, "XT", lv - 1, st)
            elif name == "WT":
                self.wait_taken(pe, w, "XT", LEVELS - 1, st)
                self.wait_taken(pe, w, "tok", 0)
            elif name == "SA":
                self.wait_taken(pe, w, "Z", st)
                self.wait_taken(pe, w, "WT", st)
                if w >= 2:
                    self.wait_taken(pe, w - 2, "S", st)
            elif name == "y":
                self.wait_taken(pe, w, "SA", st)
                self.wait_taken(pe, w, "rkT", st)
            elif name == "S":
                self.wait_taken(pe, w, "tok", 2)
            engine, n = self.num[key]
            if n >= 4:
                pe.wait_ge(self.taken[engine], n - 3)
            for e in range(4):
                k, h = 4 * q + e, 2 * (4 * q + e) + st
                wide, thin = self.bank(key)[:, e * P:(e + 1) * P], self.bank(key)[:, e * DH:(e + 1) * DH]
                v = m.v[:, c, h * DH:(h + 1) * DH] if name != "tok" else None
                if name == "tok":
                    mm = nc.tensor.transpose(wide, (m.kk, m.a, m.k)[st][:, k, tok], env.ident)
                elif name in operands:
                    lhs, rhs = operands[name]
                    mm = mmul(wide, lhs[half, k, tok], rhs[half, k, tok], start=True, stop=True)
                elif name == "Z":
                    mm = mmul(thin, s["akT"][:, e, :], v, start=True, stop=True)
                elif name == "Y":
                    mm = mmul(wide, s["MT"][lv % 2][:, e, :], s["X"][:, e, :], start=True, stop=True)
                elif name == "X":
                    mm = mmul(wide, s["XT"][:, e, :], s["Y"][:, e, :], start=True, stop=True)
                elif name == "XT":
                    mm = mmul(wide, s["Y"][:, e, :], s["XT"][:, e, :], start=True, stop=True)
                elif name == "WT":
                    mm = mmul(wide[half], m.tok[:, 0, e, half], s["XT"][:, e, :], start=True, stop=True)
                elif name == "SA":
                    mm = mmul(thin, s["XT"][:, e, :], s["Z"][:, e, :], start=True, stop=(c == 0))
                    if c:
                        mm = mmul(thin, m.WT[half, e, :], m.S[half, k, :], start=False, stop=True)
                elif name == "y":
                    mmul(thin, s["rbT"][:, e, :], s["SA"][:, e, :], start=True, stop=False)
                    mm = mmul(thin, s["rkT"][:, e, :], v, start=False, stop=(c == 0))
                    if c:
                        mm = mmul(thin, m.r[half, k, tok], m.S[half, k, :], start=False, stop=True)
                else:
                    mmul(thin[half], m.tok[:, 1, e, half], s["SA"][:, e, :], start=True, stop=False)
                    mm = mmul(thin[half], m.tok[:, 2, e, half], v, start=False, stop=True)
            mm.then_inc(self.ready[engine], 1)

    def four(self, key, n=P):
        return self.bank(key)[:, 0:4 * n].rearrange("p (e n) -> p e n", e=4)

    def scalar(self, act, step):
        env, nc, m = self.env, self.env.nc, self.m
        for key in self.order:
            w, name, st = key[0], key[1], key[-1]
            if self.num[key][0] != "A":
                continue
            c, q = self.STEPS[w]
            half = slice(64 * st, 64 * st + 64)
            if name == "tok":
                dst, src = m.tok[:, st], self.four(key)
            elif name == "Y":
                if key[2] > 1:
                    self.wait_ready(act, w, "XT", key[2] - 1, st)
                dst, src = m.streams[st]["Y"], self.four(key)
            elif name == "WT":
                dst, src = m.WT[half], self.four(key)[half]
            elif name == "y":
                dst = m.kk[:, 4 * q:4 * q + 4, c * P + 64 * st:c * P + 64 * st + 64]
                src = self.four(key, DH)
            else:
                dst, src = m.streams[st][name], self.four(key, DH)
            self.wait_ready(act, *key)
            nc.scalar.activation(dst, src, ACT.Copy).then_inc(self.taken["A"], 1)

    def vector(self, dve, step):
        env, nc, m = self.env, self.env.nc, self.m
        v = nc.vector
        mask = lambda at: env.const[:, at:at + P].unsqueeze(1).to_broadcast([P, 4, P])
        masked = {"abT": (C_STRICT_T, "abT"), "ab": (C_PAIR, "X"), "akT": (C_STRICT_T, "akT"),
                  "rbT": (C_INCL_T, "rbT"), "rkT": (C_INCL_T, "rkT")}
        for key in self.order:
            w, name, st = key[0], key[1], key[-1]
            if self.num[key][0] != "D":
                continue
            c, q = self.STEPS[w]
            s = m.streams[st]
            if name in masked:
                at, dst = masked[name]
                if w:
                    if name == "abT":
                        dve.wait_ge(self.part_ready, 12 * w)
                    else:
                        self.wait_ready(dve, w - 1, *{"ab": ("Y", LEVELS - 1), "akT": ("Z",), "rbT": ("y",),
                                                      "rkT": ("y",)}[name], st)
                self.wait_ready(dve, *key)
                v.tensor_tensor(s[dst], self.four(key), mask(at), ALU.mult).then_inc(self.taken["D"], 1)
            elif name in ("X", "XT"):
                self.wait_ready(dve, *key)
                v.tensor_tensor(s[name], self.four(key), s[name], ALU.add).then_inc(self.taken["D"], 1)
            else:
                half = slice(64 * st, 64 * st + 64)
                self.wait_ready(dve, *key)
                S = m.S[half, 4 * q:4 * q + 4, :]
                new = self.four(key, DH)[half]
                coef = m.coef[half, 4 * q:4 * q + 4, c + 1:c + 2].to_broadcast([64, 4, DH]) if c < NT - 1 else None
                if c == 0:
                    v.tensor_tensor(S, new, coef, ALU.mult).then_inc(self.taken["D"], 1)
                elif c < NT - 1:
                    step(v.tensor_tensor(S, S, new, ALU.add))
                    v.tensor_tensor(S, S, coef, ALU.mult).then_inc(self.taken["D"], 1)
                else:
                    v.tensor_tensor(S, S, new, ALU.add).then_inc(self.taken["D"], 1)

    def gpsimd(self, pool, step):
        env, nc, m = self.env, self.env.nc, self.m
        g = nc.gpsimd
        mask = lambda at: env.const[:, at:at + P].unsqueeze(1).to_broadcast([P, 4, P])
        for w in range(len(self.STEPS)):
            for st in range(2):
                s = m.streams[st]
                self.wait_taken(pool, w, "ab", st)
                g.tensor_tensor(s["X"], s["X"], mask(C_IDENT), ALU.add).then_inc(self.start_ready, 1)
                g.tensor_tensor(s["MT"][1], s["abT"], mask(C_LEVEL_T), ALU.mult).then_inc(self.part_ready, 1)
            for st in range(2):
                s = m.streams[st]
                if w:
                    self.wait_ready(pool, w - 1, "SA", st)
                step(g.tensor_tensor(s["XT"], s["abT"], mask(C_PAIR_T), ALU.mult))
                g.tensor_tensor(s["XT"], s["XT"], mask(C_IDENT), ALU.add).then_inc(self.start_T_ready, 1)
            for lv in range(2, LEVELS):
                for st in range(2):
                    s = m.streams[st]
                    if lv > 2:
                        self.wait_ready(pool, w, "Y", lv - 2, st)
                    g.tensor_tensor(s["MT"][lv % 2], s["abT"], mask(C_LEVEL_T + (lv - 1) * P),
                                    ALU.mult).then_inc(self.part_ready, 1)


class RwkvGate(Stage):

    def __init__(self, env, m):
        super().__init__(env)
        self.m = m
        g2 = env.io["g2_2"][0]
        self.lds = [env.load(g2[0:P].unsqueeze(1), split=False), env.load(g2[P:160].unsqueeze(1), split=False)]
        self.g0 = env.group(KD)
        for ld in self.lds:
            env.release(ld, env.proj_ready, env.groups)
        s = env.sem
        self.rows = s("gn_rows")
        self.y_copied, self.centred, self.squared = s("y_copied"), s("y_centred"), s("y_squared")
        self.var_ready, self.std_ready, self.added_ready = s("gn_var_ready"), s("gn_std_ready"), s("gn_added_ready")

    def tensor(self, pe):
        env, nc, m = self.env, self.env.nc, self.m
        for ld in self.lds:
            env.wait_whole(pe, ld)
        w = [env.whole(ld)[:, 0, :] for ld in self.lds]
        for k in range(KD):
            g, cols = self.g0 + k, slice(k * P, (k + 1) * P)
            env.wait_bank(pe, g)
            nc.tensor.matmul(env.bank(g), w[0][:, cols], m.sg[:, 0, :], start=True, stop=False)
            nc.tensor.matmul(env.bank(g), w[1][0:32, cols], m.sg[0:32, 1, :],
                             start=False, stop=True).then_inc(env.proj_ready, 1)

    def scalar(self, act, step):
        env, nc, m = self.env, self.env.nc, self.m
        for i in range(NT):
            nc.scalar.activation(m.o[:, i, :].rearrange("p (k d) -> p k d", d=P), m.kk[:, :, i * P:(i + 1) * P],
                                 ACT.Copy).then_inc(self.y_copied, 1)
        for i in range(NT):
            act.wait_ge(self.centred, i + 1)
            nc.scalar.activation(m.squares[:, i % 2, :], m.o[:, i, :], ACT.Square).then_inc(self.squared, 1)
            for k in (2 * i, 2 * i + 1):
                act.wait_ge(env.proj_ready, self.g0 + k + 1)
                nc.scalar.activation(m.gate[:, k, :], env.bank(self.g0 + k), ACT.Copy).then_inc(env.proj_taken, 1)
            act.wait_ge(self.var_ready, i + 1)
            nc.scalar.activation(m.grstd[:, i % 2, :], m.var[:, i % 2, :], ACT.Sqrt).then_inc(self.std_ready, 1)

    def gpsimd(self, pool, step):
        env, nc, m = self.env, self.env.nc, self.m
        pool.dma_start(m.gn[:, 0, :], env.io["gn_g_2"][0].partition_broadcast(P)).then_inc(self.rows, 16)
        pool.dma_start(m.gn[:, 1, :], env.io["gn_b_2"][0].partition_broadcast(P)).then_inc(self.rows, 16)
        for i in range(NT):
            added = m.added[:, i, :]
            step(nc.gpsimd.tensor_tensor(added.rearrange("p (h d) -> p h d", d=DH),
                                         m.v[:, i, :].rearrange("p (h d) -> p h d", d=DH),
                                         m.bonus[:, i, :].unsqueeze(2).to_broadcast([P, RH, DH]), ALU.mult))
            if i == 0:
                pool.wait_ge(self.rows, 32)
            nc.gpsimd.tensor_tensor(added, added, m.gn[:, 1, :], ALU.add).then_inc(self.added_ready, 1)

    def vector(self, dve, step):
        env, nc, m = self.env, self.env.nc, self.m
        v = nc.vector
        wide = lambda c: c.unsqueeze(2).to_broadcast([P, RH, DH])
        heads = lambda x: x.rearrange("p (h d) -> p h d", d=DH)

        def centre(i):
            o, mean = heads(m.o[:, i, :]), m.mean[:, i % 2, :]
            dve.wait_ge(self.y_copied, i + 1)
            step(v.tensor_reduce(mean, o, AX, ALU.add))
            step(v.tensor_scalar(mean, mean, 1.0 / DH, None, ALU.mult))
            v.tensor_tensor(o, o, wide(mean), ALU.subtract).then_inc(self.centred, 1)

        centre(0)
        dve.wait_ge(self.rows, 32)
        for i in range(NT):
            if i + 1 < NT:
                centre(i + 1)
            flat, var = m.o[:, i, :], m.var[:, i % 2, :]
            dve.wait_ge(self.squared, i + 1)
            step(v.tensor_reduce(var, heads(m.squares[:, i % 2, :]), AX, ALU.add))
            step(v.tensor_scalar(var, var, 1.0 / DH, GN_EPS, ALU.mult, ALU.add))
            v.reciprocal(var, var).then_inc(self.var_ready, 1)
            step(v.tensor_tensor(flat, flat, m.gn[:, 0, :], ALU.mult))
            dve.wait_ge(self.std_ready, i + 1)
            step(v.tensor_tensor(heads(flat), heads(flat), wide(m.grstd[:, i % 2, :]), ALU.mult))
            dve.wait_ge(self.added_ready, i + 1)
            v.tensor_tensor(flat, flat, m.added[:, i, :], ALU.add)


def end_stage(env, eng, s):
    eng.drain().then_inc(env.stage_done, 1)
    eng.wait_ge(env.stage_done, 4 * (s + 1))


def build(nc, io, out):
    with ExitStack() as ctx:
        env = Env(nc, ctx, io)
        setup = Setup(env)
        m = NsaMemory(env, setup.bias, setup)
        dm = DiffMemory(env, setup.bias)
        rm = RwkvMemory(env)
        fm = FfnMemory(env)
        sm = SwaMemory(env)
        pre, post, g = io["norm_pre"], io["norm_post"], io["norm_g_2"]
        stages = [
            setup,
            Norm(env, pre[0], m.u, setup.x_arrived),
            NsaProject(env, m, setup),
            NsaCompress(env, m),
            NsaCompressed(env, m),
            NsaAttend(env, m, len(env.loads) + 1),
            Output(env, io["nsa_w_out"][0], post[0], m.u, m.o, m.z, following=(pre[1], dm.u)),
            DiffProject(env, dm),
            DiffAttend(env, dm),
            DiffNorm(env, dm),
            Output(env, io["diff_w_out"][0], post[1], dm.oT, dm.o, dm.z, following=(g[0, 0], [env.uT])),
            RwkvProject(env, rm),
            RwkvPrepare(env, rm),
            RwkvDecay(env, rm),
            RwkvCore(env, rm),
            RwkvGate(env, rm),
            Output(env, io["w_o_rwkv_2"][0], g[0, 1], rm.oT, rm.o, rm.gate, following=(g[0, 2], fm.u)),
            FfnUp(env, 0, fm),
            Output(env, io["w_down_2"][0], g[0, 3], fm.act, kd=FT, following=(io["kv_g_2"], sm.u)),
        ]
        kv = KvProject(env, sm, g[1, 0])
        stages += [
            kv,
            NormAgain(env, kv.again),
            SwaProject(env, sm),
            SwaAttend(env, sm),
            Output(env, io["w_o_attn_2"][0], g[1, 1], sm.u, sm.o, following=(g[1, 2], fm.u)),
            FfnUp(env, 1, fm),
            Output(env, io["w_down_2"][1], g[1, 3], fm.act, kd=FT),
        ]
        block = ctx.enter_context(nc.Block())

        @block.sync
        def _(sp):
            setup.load(sp)
            for ld in range(len(env.loads)):
                env.fetch(sp, ld)
            for i in range(NT):
                env.wait_x(sp, env.outs - 1, i)
                sp.dma_start(out[0, i * P:(i + 1) * P, :], env.x[:, i, :]).then_inc(env.stored, 16)
            sp.wait_ge(env.stored, 16 * NT)
            sp.wait_ge(env.stage_done, 4 * len(stages))

        @block.tensor
        def _(pe):
            for s, stage in enumerate(stages):
                stage.tensor(pe)
                end_stage(env, pe, s)

        @block.scalar
        def _(act):
            step = Steps(act, env.act_step)
            for s, stage in enumerate(stages):
                stage.scalar(act, step)
                end_stage(env, act, s)

        @block.vector
        def _(dve):
            step = Steps(dve, env.dve_step)
            for s, stage in enumerate(stages):
                stage.vector(dve, step)
                end_stage(env, dve, s)

        @block.gpsimd
        def _(pool):
            step = Steps(pool, env.pool_step)
            for s, stage in enumerate(stages):
                stage.gpsimd(pool, step)
                end_stage(env, pool, s)


def declare(nc, inputs):
    arrays, io = {}, {}
    given = dict(inputs)
    given["shape_constants"] = shape_constants()
    given["head_rows"] = np.kron(np.eye(RH), np.ones((1, DH))).astype(np.float32)
    given["distance_one_hot"] = distance_one_hot().astype("bfloat16")
    for name, a in given.items():
        a = np.ascontiguousarray(a)
        arrays["in_" + name] = a
        io[name] = nc.dram_tensor("in_" + name, a.shape, mybir.dt.from_np(a.dtype), kind="ExternalInput").ap()
    out = nc.dram_tensor("out", (1, T, D), F32, kind="ExternalOutput").ap()
    build(nc, io, out)
    return arrays


def kernel(**inputs):
    import concourse.bacc as _bacc
    from concourse.bass_utils import run_bass_kernel_spmd as _run

    nc = _bacc.Bacc("TRN2", target_bir_lowering=False, num_devices=1)
    arrays = declare(nc, inputs)
    r = _run(nc, [arrays], core_ids=[0])
    return r.results[0]["out"]
```
